# Optimizing a Trainium2 kernel written in Bass

```python
import math
import jax, jax.numpy as jnp
from jax import lax
import numpy as np
import jax
import jax.numpy as jnp

D_MODEL = 1024
BATCH = 1
SEQ = 512
DEPTH = 1

NSA_HEADS = 8
NSA_KV_GROUPS = 2
NSA_HPG = NSA_HEADS // NSA_KV_GROUPS
NSA_HEAD_DIM = 64
CMP_BLOCK = 32
CMP_STRIDE = 16
CMP_HIDDEN = 256
SLC_BLOCK = 64
SLC_COUNT = 16
WINDOW = 512
Q_BLOCK = 128
ROPE_THETA = 500000.0
ROPE_DIM = NSA_HEAD_DIM // 4
RET_HEADS = 4
RET_HEAD_DIM = 128
RET_CHUNK = 128
RET_ROT_BASE = 10000.0
MLP_HIDDEN = 4 * D_MODEL
NORM_EPS = 1e-6
NEG = -1e30
BIG = 1e30

NSA_Q_W = NSA_HEADS * NSA_HEAD_DIM
NSA_KV_W = NSA_KV_GROUPS * NSA_HEAD_DIM
RET_W = RET_HEADS * RET_HEAD_DIM
IN_SIZES = (NSA_Q_W, NSA_KV_W, NSA_KV_W, NSA_KV_W, NSA_KV_W, NSA_KV_W, NSA_KV_W, 3 * NSA_HEADS,
            RET_W, RET_W, RET_W, RET_W, D_MODEL, D_MODEL)
IN_WIDTH = sum(IN_SIZES)


def rmsnorm(x, g):
    xf = x.astype(jnp.float32)
    y = xf * lax.rsqrt(jnp.mean(xf * xf, axis=-1, keepdims=True) + NORM_EPS) * g.astype(jnp.float32)
    return y.astype(x.dtype)

def rotary(x, pos, rot_dim, base):
    half = rot_dim // 2
    inv = jnp.exp(-math.log(base) * jnp.arange(half, dtype=jnp.float32) * 2.0 / rot_dim)
    ang = pos.astype(jnp.float32)[..., None] * inv
    cos, sin = jnp.cos(ang)[:, :, None, :], jnp.sin(ang)[:, :, None, :]
    xf = x.astype(jnp.float32)
    x1, x2 = xf[..., :half], xf[..., half:rot_dim]
    out = jnp.concatenate([x1 * cos - x2 * sin, x1 * sin + x2 * cos, xf[..., rot_dim:]], axis=-1)
    return out.astype(x.dtype)

def nsa_mixer(q, kc, vc, ks, vs, kw, vw, gates, pe_k, pe_v, ck_w1, ck_w2, cv_w1, cv_w2):
    S = q.shape[0]
    dt = q.dtype
    G, HPG, dh = NSA_KV_GROUPS, NSA_HPG, NSA_HEAD_DIM
    n_cmp = (S - CMP_BLOCK) // CMP_STRIDE + 1
    n_slc = S // SLC_BLOCK
    n_sel = min(SLC_COUNT, n_slc)
    n_qb = S // Q_BLOCK
    scale = dh ** -0.5

    cmp_idx = jnp.arange(n_cmp)[:, None] * CMP_STRIDE + jnp.arange(CMP_BLOCK)[None, :]

    def compress(k, pe, w1, w2):
        blk = k[cmp_idx] + pe[None, :, None, :]
        blk = blk.transpose(0, 2, 1, 3).reshape(n_cmp, G, CMP_BLOCK * dh)
        return jax.nn.silu(blk @ w1) @ w2

    k_cmp = compress(kc, pe_k, ck_w1, ck_w2)
    v_cmp = compress(vc, pe_v, cv_w1, cv_w2)
    cmp_start = cmp_idx[:, 0]
    cmp_end = cmp_idx[:, -1]
    slc_start = jnp.arange(n_slc) * SLC_BLOCK
    overlap = jnp.clip(jnp.minimum(cmp_start[:, None] + CMP_BLOCK, slc_start[None, :] + SLC_BLOCK)
                       - jnp.maximum(cmp_start[:, None], slc_start[None, :]), 0, None)
    overlap = overlap.astype(jnp.float32) / CMP_BLOCK

    ks_b = ks.reshape(n_slc, SLC_BLOCK, G, dh).transpose(2, 0, 1, 3)
    vs_b = vs.reshape(n_slc, SLC_BLOCK, G, dh).transpose(2, 0, 1, 3)
    kw_pad = jnp.pad(kw, ((WINDOW, 0), (0, 0), (0, 0)))
    vw_pad = jnp.pad(vw, ((WINDOW, 0), (0, 0), (0, 0)))

    qg = q.reshape(S, G, HPG, dh)
    gg = jax.nn.sigmoid(gates.astype(jnp.float32)).reshape(S, G, HPG, 3)
    g_idx = jnp.arange(G)[:, None, None]
    blk_j = jnp.arange(n_slc)

    def block(b):
        s0 = b * Q_BLOCK
        qi = lax.dynamic_slice_in_dim(qg, s0, Q_BLOCK, 0)
        gi = lax.dynamic_slice_in_dim(gg, s0, Q_BLOCK, 0)
        t = s0 + jnp.arange(Q_BLOCK)

        sc = jnp.einsum('qghd,cgd->gqhc', qi, k_cmp).astype(jnp.float32) * scale
        valid = cmp_end[None, :] <= t[:, None]
        p_c = jax.nn.softmax(jnp.where(valid[None, :, None, :], sc, NEG), axis=-1)
        p_c = p_c * jnp.any(valid, axis=-1)[None, :, None, None].astype(jnp.float32)
        o_c = jnp.einsum('gqhc,cgd->qghd', p_c.astype(dt), v_cmp)

        imp = jnp.einsum('gqhc,cj->gqj', p_c, overlap)
        cur = t // SLC_BLOCK
        forced = (blk_j[None] == 0) | (blk_j[None] == cur[:, None]) | (blk_j[None] == cur[:, None] - 1)
        future = blk_j[None] > cur[:, None]
        imp = jnp.where(forced[None], BIG, jnp.where(future[None], NEG, imp))
        _, sel = lax.top_k(imp, n_sel)

        k_sel = ks_b[g_idx, sel].reshape(G, Q_BLOCK, n_sel * SLC_BLOCK, dh)
        v_sel = vs_b[g_idx, sel].reshape(G, Q_BLOCK, n_sel * SLC_BLOCK, dh)
        k_pos = (sel[..., None] * SLC_BLOCK + jnp.arange(SLC_BLOCK)).reshape(G, Q_BLOCK, n_sel * SLC_BLOCK)
        ss = jnp.einsum('qghd,gqkd->gqhk', qi, k_sel).astype(jnp.float32) * scale
        smask = (k_pos <= t[None, :, None])[:, :, None, :]
        p_s = jax.nn.softmax(jnp.where(smask, ss, NEG), axis=-1)
        o_s = jnp.einsum('gqhk,gqkd->qghd', p_s.astype(dt), v_sel)

        k_win = lax.dynamic_slice_in_dim(kw_pad, s0, WINDOW + Q_BLOCK, 0)
        v_win = lax.dynamic_slice_in_dim(vw_pad, s0, WINDOW + Q_BLOCK, 0)
        w_pos = s0 - WINDOW + jnp.arange(WINDOW + Q_BLOCK)
        wmask = (w_pos[None] <= t[:, None]) & (w_pos[None] > t[:, None] - WINDOW) & (w_pos[None] >= 0)
        sw = jnp.einsum('qghd,kgd->gqhk', qi, k_win).astype(jnp.float32) * scale
        p_w = jax.nn.softmax(jnp.where(wmask[None, :, None, :], sw, NEG), axis=-1)
        o_w = jnp.einsum('gqhk,kgd->qghd', p_w.astype(dt), v_win)

        o = gi[..., 0:1] * o_c + gi[..., 1:2] * o_s + gi[..., 2:3] * o_w
        return o.reshape(Q_BLOCK, NSA_HEADS * dh).astype(dt)

    out = lax.map(block, jnp.arange(n_qb))
    return out.reshape(S, NSA_HEADS * dh)

def retention(q, k, v, pos):
    B, S = q.shape[0], q.shape[1]
    H, d, C = RET_HEADS, RET_HEAD_DIM, RET_CHUNK
    q = rotary(q, pos, d, RET_ROT_BASE).astype(jnp.float32)
    k = rotary(k, pos, d, RET_ROT_BASE).astype(jnp.float32) * (d ** -0.5)
    v = v.astype(jnp.float32)
    n_c = S // C

    def chunks(a):
        return a.reshape(B, n_c, C, H, d).transpose(1, 0, 3, 2, 4)

    log_g = jnp.log(1.0 - jnp.exp2(-5.0 - jnp.arange(H, dtype=jnp.float32)))
    n = jnp.arange(C, dtype=jnp.float32)
    rel = n[:, None] - n[None, :]
    dmat = jnp.where(rel >= 0, jnp.exp(log_g[:, None, None] * jnp.maximum(rel, 0.0)), 0.0)
    xi = jnp.exp(log_g[:, None] * (n + 1.0))
    zeta = jnp.exp(log_g[:, None] * (C - 1.0 - n))
    chunk_decay = jnp.exp(log_g * C)

    def step(state, inp):
        qc, kc, vc = inp
        inner = jnp.einsum('bhnm,bhme->bhne', jnp.einsum('bhnd,bhmd->bhnm', qc, kc) * dmat, vc)
        cross = jnp.einsum('bhnd,bhde->bhne', qc, state) * xi[None, :, :, None]
        state = chunk_decay[None, :, None, None] * state + jnp.einsum(
            'bhmd,bhme->bhde', kc * zeta[None, :, :, None], vc)
        return state, inner + cross

    state0 = jnp.zeros((B, H, d, d), jnp.float32)
    _, o = lax.scan(step, state0, (chunks(q), chunks(k), chunks(v)))
    o = o.transpose(1, 0, 3, 2, 4).reshape(B, S, H, d)
    return o * lax.rsqrt(jnp.mean(o * o, axis=-1, keepdims=True) + NORM_EPS)

def first_inputs(seed: int = 0) -> dict:
    key = jax.random.key(seed)
    ks = jax.random.split(key, 20)
    f32 = jnp.float32
    nrm = lambda k, shape, s: jax.random.normal(k, shape, f32) * s
    L = DEPTH
    x = jax.random.normal(ks[0], (BATCH, SEQ, D_MODEL), f32)
    offset = jax.random.randint(ks[1], (BATCH, 1), 0, 4096, dtype=jnp.int32)
    positions = (offset + jnp.arange(SEQ, dtype=jnp.int32)[None, :]).astype(jnp.int32)
    return {
        "x": x,
        "positions": positions,
        "norm_mix": 1.0 + nrm(ks[2], (L, D_MODEL), 0.02),
        "w_in": nrm(ks[3], (L, D_MODEL, IN_WIDTH), D_MODEL ** -0.5),
        "cmp_pos_k": nrm(ks[4], (L, CMP_BLOCK, NSA_HEAD_DIM), 0.1),
        "cmp_pos_v": nrm(ks[5], (L, CMP_BLOCK, NSA_HEAD_DIM), 0.1),
        "cmp_k_w1": nrm(ks[6], (L, CMP_BLOCK * NSA_HEAD_DIM, CMP_HIDDEN), (CMP_BLOCK * NSA_HEAD_DIM) ** -0.5),
        "cmp_k_w2": nrm(ks[7], (L, CMP_HIDDEN, NSA_HEAD_DIM), CMP_HIDDEN ** -0.5),
        "cmp_v_w1": nrm(ks[8], (L, CMP_BLOCK * NSA_HEAD_DIM, CMP_HIDDEN), (CMP_BLOCK * NSA_HEAD_DIM) ** -0.5),
        "cmp_v_w2": nrm(ks[9], (L, CMP_HIDDEN, NSA_HEAD_DIM), CMP_HIDDEN ** -0.5),
        "w_proj_a": nrm(ks[10], (L, NSA_Q_W, D_MODEL), NSA_Q_W ** -0.5),
        "w_proj_b": nrm(ks[11], (L, RET_W, D_MODEL), RET_W ** -0.5),
        "w_out": nrm(ks[12], (L, D_MODEL, D_MODEL), D_MODEL ** -0.5),
        "norm_mlp": 1.0 + nrm(ks[13], (L, D_MODEL), 0.02),
        "w_up": nrm(ks[14], (L, D_MODEL, MLP_HIDDEN), D_MODEL ** -0.5),
        "w_down": nrm(ks[15], (L, MLP_HIDDEN, D_MODEL), MLP_HIDDEN ** -0.5),
        "norm_final": 1.0 + nrm(ks[16], (D_MODEL,), 0.02),
    }

def first_block(x, positions, norm_mix, w_in, cmp_pos_k, cmp_pos_v, cmp_k_w1, cmp_k_w2, cmp_v_w1, cmp_v_w2,
              w_proj_a, w_proj_b, w_out, norm_mlp, w_up, w_down, norm_final):
    B, S, _ = x.shape
    offsets = np.cumsum(IN_SIZES)[:-1].tolist()
    nsa_batched = jax.vmap(nsa_mixer, in_axes=(0,) * 8 + (None,) * 6)
    for layer in range(DEPTH):
        h = rmsnorm(x, norm_mix[layer])
        (q, kc, vc, ks, vs, kw, vw, nsa_g, rq, rk, rv, rg, gate_a, gate_b) = jnp.split(
            h @ w_in[layer], offsets, axis=-1)
        heads = lambda a, n_h, d: a.reshape(B, S, n_h, d)
        q = rotary(heads(q, NSA_HEADS, NSA_HEAD_DIM), positions, ROPE_DIM, ROPE_THETA)
        kc = rotary(heads(kc, NSA_KV_GROUPS, NSA_HEAD_DIM), positions, ROPE_DIM, ROPE_THETA)
        ks = rotary(heads(ks, NSA_KV_GROUPS, NSA_HEAD_DIM), positions, ROPE_DIM, ROPE_THETA)
        kw = rotary(heads(kw, NSA_KV_GROUPS, NSA_HEAD_DIM), positions, ROPE_DIM, ROPE_THETA)
        vc = heads(vc, NSA_KV_GROUPS, NSA_HEAD_DIM)
        vs = heads(vs, NSA_KV_GROUPS, NSA_HEAD_DIM)
        vw = heads(vw, NSA_KV_GROUPS, NSA_HEAD_DIM)
        nsa_out = nsa_batched(q, kc, vc, ks, vs, kw, vw, nsa_g.reshape(B, S, NSA_HEADS, 3),
                              cmp_pos_k[layer], cmp_pos_v[layer], cmp_k_w1[layer], cmp_k_w2[layer],
                              cmp_v_w1[layer], cmp_v_w2[layer])
        ret = retention(heads(rq, RET_HEADS, RET_HEAD_DIM), heads(rk, RET_HEADS, RET_HEAD_DIM),
                        heads(rv, RET_HEADS, RET_HEAD_DIM), positions)
        ret_out = (jax.nn.silu(rg.astype(jnp.float32)) * ret.reshape(B, S, RET_W)).astype(x.dtype)
        mix = (jax.nn.sigmoid(gate_a) * (nsa_out @ w_proj_a[layer])
               + jax.nn.sigmoid(gate_b) * (ret_out @ w_proj_b[layer]))
        x = x + mix @ w_out[layer]
        h = rmsnorm(x, norm_mlp[layer])
        x = x + jnp.square(jax.nn.relu(h @ w_up[layer])) @ w_down[layer]
    return rmsnorm(x, norm_final)


CHUNK = 64
HEAD_DIM = 64
FOX_HEADS = 8
DSA_HEADS = 8
IDX_HEADS = 8
IDX_DIM = 32
TOPK_MAX = 256
ROPE_FRACTION = 4
D_FF = 2816
N_SUBLAYERS = 3
FOX_WIDTH = FOX_HEADS * HEAD_DIM
DSA_WIDTH = DSA_HEADS * HEAD_DIM
IN_SIZES_2 = (FOX_WIDTH, FOX_WIDTH, FOX_WIDTH, FOX_HEADS, DSA_WIDTH, HEAD_DIM, HEAD_DIM, IDX_HEADS * IDX_DIM, IDX_DIM, IDX_HEADS, D_MODEL, D_MODEL)
D_IN = sum(IN_SIZES_2)


def rms_norm(x, g):
    xf = x.astype(jnp.float32)
    y = xf * lax.rsqrt(jnp.mean(xf * xf, axis=-1, keepdims=True) + NORM_EPS)
    return (y * g.astype(jnp.float32)).astype(x.dtype)

def modulate(x, g, shift, scale):
    return rms_norm(x, g) * (1 + scale[:, None, :]) + shift[:, None, :]

def swiglu(h, w1, w3, w2):
    return (jax.nn.silu(h @ w1) * (h @ w3)) @ w2

def rope_tables(positions, rot_dim):
    inv_freq = ROPE_THETA ** (-jnp.arange(0, rot_dim, 2, dtype=jnp.float32) / rot_dim)
    ang = positions.astype(jnp.float32)[..., None] * inv_freq
    return jnp.cos(ang), jnp.sin(ang)

def partial_rope(x, cos, sin):
    half = cos.shape[-1]
    x1 = x[..., :half].astype(jnp.float32)
    x2 = x[..., half:2 * half].astype(jnp.float32)
    r1 = (x1 * cos - x2 * sin).astype(x.dtype)
    r2 = (x2 * cos + x1 * sin).astype(x.dtype)
    return jnp.concatenate([r1, r2, x[..., 2 * half:]], axis=-1)

def fox_attention(q, k, v, log_f):
    B, S, H, dh = q.shape
    F = jnp.cumsum(log_f.astype(jnp.float32), axis=1).transpose(0, 2, 1)
    kpos = jnp.arange(S)
    scale = dh ** -0.5

    def block(i):
        qs = i * Q_BLOCK
        qb = lax.dynamic_slice_in_dim(q, qs, Q_BLOCK, axis=1)
        Fq = lax.dynamic_slice_in_dim(F, qs, Q_BLOCK, axis=2)
        s = jnp.einsum('bqhd,bkhd->bhqk', qb, k, preferred_element_type=jnp.float32) * scale
        s = s + Fq[..., None] - F[:, :, None, :]
        qpos = qs + jnp.arange(Q_BLOCK)
        mask = kpos[None, :] <= qpos[:, None]
        s = jnp.where(mask[None, None], s, -jnp.inf)
        p = jax.nn.softmax(s, axis=-1)
        return jnp.einsum('bhqk,bkhd->bqhd', p.astype(v.dtype), v)

    out = lax.map(block, jnp.arange(S // Q_BLOCK))
    return out.transpose(1, 0, 2, 3, 4).reshape(B, S, H, dh)

def dsa_attention(q, k, v, iq, ik, iw, top_k):
    B, S, H, dh = q.shape
    kchunk = jnp.arange(S) // CHUNK
    scale = dh ** -0.5
    idx_scale = IDX_DIM ** -0.5

    def block(i):
        qs = i * Q_BLOCK
        qb = lax.dynamic_slice_in_dim(q, qs, Q_BLOCK, axis=1)
        iqb = lax.dynamic_slice_in_dim(iq, qs, Q_BLOCK, axis=1)
        iwb = lax.dynamic_slice_in_dim(iw, qs, Q_BLOCK, axis=1)
        qchunk = (qs + jnp.arange(Q_BLOCK)) // CHUNK
        admissible = kchunk[None, :] <= qchunk[:, None]
        dots = jnp.einsum('bqhd,bkd->bqhk', iqb, ik, preferred_element_type=jnp.float32) * idx_scale
        score = jnp.einsum('bqh,bqhk->bqk', iwb.astype(jnp.float32), jax.nn.relu(dots))
        score = jnp.where(admissible[None], score, -jnp.inf)
        _, sel = lax.top_k(score, top_k)
        kg = jax.vmap(lambda kb, ib: kb[ib])(k, sel)
        vg = jax.vmap(lambda vb, ib: vb[ib])(v, sel)
        valid = (sel // CHUNK) <= qchunk[None, :, None]
        s = jnp.einsum('bqhd,bqkd->bhqk', qb, kg, preferred_element_type=jnp.float32) * scale
        s = jnp.where(valid[:, None], s, -jnp.inf)
        p = jax.nn.softmax(s, axis=-1)
        return jnp.einsum('bhqk,bqkd->bqhd', p.astype(vg.dtype), vg)

    out = lax.map(block, jnp.arange(S // Q_BLOCK))
    return out.transpose(1, 0, 2, 3, 4).reshape(B, S, H, dh)

def hybrid_mixer(h, w_in, fox_f_bias, fox_qk_g, dsa_qk_g, w_br_fox, w_br_dsa, w_out, rope_a, rope_i, top_k):
    B, S, _ = h.shape
    cos_a, sin_a = rope_a
    cos_i, sin_i = rope_i
    z = h @ w_in
    split_points = [int(p) for p in np.cumsum(IN_SIZES_2)[:-1]]
    (fq, fk, fv, ff, dq, dk, dv, iq, ik, iw, ga, gb) = jnp.split(z, split_points, axis=-1)
    fq = rms_norm(fq.reshape(B, S, FOX_HEADS, HEAD_DIM), fox_qk_g[0])
    fk = rms_norm(fk.reshape(B, S, FOX_HEADS, HEAD_DIM), fox_qk_g[1])
    fv = fv.reshape(B, S, FOX_HEADS, HEAD_DIM)
    log_f = jax.nn.log_sigmoid(ff.astype(jnp.float32) + fox_f_bias.astype(jnp.float32))
    ya = fox_attention(fq, fk, fv, log_f).reshape(B, S, FOX_WIDTH)
    dq = partial_rope(rms_norm(dq.reshape(B, S, DSA_HEADS, HEAD_DIM), dsa_qk_g[0]), cos_a[:, :, None, :], sin_a[:, :, None, :])
    dk = partial_rope(rms_norm(dk, dsa_qk_g[1]), cos_a, sin_a)
    iq = partial_rope(iq.reshape(B, S, IDX_HEADS, IDX_DIM), cos_i[:, :, None, :], sin_i[:, :, None, :])
    ik = partial_rope(ik, cos_i, sin_i)
    iw = iw * (IDX_HEADS ** -0.5)
    yb = dsa_attention(dq, dk, dv, iq, ik, iw, top_k).reshape(B, S, DSA_WIDTH)
    merged = jax.nn.sigmoid(ga) * (ya @ w_br_fox) + jax.nn.sigmoid(gb) * (yb @ w_br_dsa)
    return merged @ w_out

def second_inputs(seed: int = 0) -> dict:
    key = jax.random.key(seed)
    ks = jax.random.split(key, 24)
    L = DEPTH

    def nrm(k, shape, fan_in, gain=1.0):
        return jax.random.normal(k, shape, jnp.float32) * (gain * fan_in ** -0.5)

    x = jax.random.normal(ks[0], (BATCH, SEQ, D_MODEL), jnp.float32)
    c = jax.random.normal(ks[1], (BATCH, D_MODEL), jnp.float32)
    offsets = jax.random.randint(ks[2], (BATCH, 1), 0, 1024) * CHUNK
    positions = (offsets + jnp.arange(SEQ, dtype=jnp.int32)[None, :]).astype(jnp.int32)
    ada_w = nrm(ks[3], (L, D_MODEL, 3 * N_SUBLAYERS * D_MODEL), D_MODEL, 0.5)
    ada_b = 0.02 * jax.random.normal(ks[4], (L, 3 * N_SUBLAYERS * D_MODEL), jnp.float32)
    norm_g = 1.0 + 0.05 * jax.random.normal(ks[5], (L, N_SUBLAYERS, D_MODEL), jnp.float32)
    ffn1_w1 = nrm(ks[6], (L, D_MODEL, D_FF), D_MODEL)
    ffn1_w3 = nrm(ks[7], (L, D_MODEL, D_FF), D_MODEL)
    ffn1_w2 = nrm(ks[8], (L, D_FF, D_MODEL), D_FF)
    w_in = nrm(ks[9], (L, D_MODEL, D_IN), D_MODEL)
    fox_f_bias = 2.0 + 0.1 * jax.random.normal(ks[10], (L, FOX_HEADS), jnp.float32)
    fox_qk_g = 1.0 + 0.05 * jax.random.normal(ks[11], (L, 2, HEAD_DIM), jnp.float32)
    dsa_qk_g = 1.0 + 0.05 * jax.random.normal(ks[12], (L, 2, HEAD_DIM), jnp.float32)
    w_br_fox = nrm(ks[13], (L, FOX_WIDTH, D_MODEL), FOX_WIDTH)
    w_br_dsa = nrm(ks[14], (L, DSA_WIDTH, D_MODEL), DSA_WIDTH)
    w_out = nrm(ks[15], (L, D_MODEL, D_MODEL), D_MODEL)
    ffn2_w1 = nrm(ks[16], (L, D_MODEL, D_FF), D_MODEL)
    ffn2_w3 = nrm(ks[17], (L, D_MODEL, D_FF), D_MODEL)
    ffn2_w2 = nrm(ks[18], (L, D_FF, D_MODEL), D_FF)
    return {'x': x, 'c': c, 'positions': positions, 'ada_w': ada_w, 'ada_b': ada_b,
            'norm_g': norm_g, 'ffn1_w1': ffn1_w1, 'ffn1_w3': ffn1_w3, 'ffn1_w2': ffn1_w2,
            'w_in': w_in, 'fox_f_bias': fox_f_bias, 'fox_qk_g': fox_qk_g, 'dsa_qk_g': dsa_qk_g,
            'w_br_fox': w_br_fox, 'w_br_dsa': w_br_dsa, 'w_out': w_out,
            'ffn2_w1': ffn2_w1, 'ffn2_w3': ffn2_w3, 'ffn2_w2': ffn2_w2}

def second_block(x, c, positions, ada_w, ada_b, norm_g, ffn1_w1, ffn1_w3, ffn1_w2, w_in, fox_f_bias, fox_qk_g, dsa_qk_g, w_br_fox, w_br_dsa, w_out, ffn2_w1, ffn2_w3, ffn2_w2):
    B, S, _ = x.shape
    top_k = min(TOPK_MAX, S // 4)
    rope_a = rope_tables(positions, HEAD_DIM // ROPE_FRACTION)
    rope_i = rope_tables(positions, IDX_DIM // ROPE_FRACTION)
    cond = jax.nn.silu(c)
    for l in range(DEPTH):
        mod = (cond @ ada_w[l] + ada_b[l]).reshape(B, N_SUBLAYERS, 3, D_MODEL)
        h = modulate(x, norm_g[l, 0], mod[:, 0, 0], mod[:, 0, 1])
        x = x + 0.5 * mod[:, 0, 2][:, None, :] * swiglu(h, ffn1_w1[l], ffn1_w3[l], ffn1_w2[l])
        h = modulate(x, norm_g[l, 1], mod[:, 1, 0], mod[:, 1, 1])
        y = hybrid_mixer(h, w_in[l], fox_f_bias[l], fox_qk_g[l], dsa_qk_g[l], w_br_fox[l], w_br_dsa[l], w_out[l], rope_a, rope_i, top_k)
        x = x + mod[:, 1, 2][:, None, :] * y
        h = modulate(x, norm_g[l, 2], mod[:, 2, 0], mod[:, 2, 1])
        x = x + 0.5 * mod[:, 2, 2][:, None, :] * swiglu(h, ffn2_w1[l], ffn2_w3[l], ffn2_w2[l])
    return x


def setup_inputs(seed=0):
    out = dict(first_inputs(seed))
    for name, value in second_inputs(seed + 1).items():
        if name != "x":
            out[name + "_2"] = value
    return out


def reference(
    x, positions, norm_mix, w_in, cmp_pos_k, cmp_pos_v, cmp_k_w1, cmp_k_w2, cmp_v_w1, cmp_v_w2,
    w_proj_a, w_proj_b, w_out, norm_mlp, w_up, w_down, norm_final, c_2, positions_2, ada_w_2,
    ada_b_2, norm_g_2, ffn1_w1_2, ffn1_w3_2, ffn1_w2_2, w_in_2, fox_f_bias_2, fox_qk_g_2,
    dsa_qk_g_2, w_br_fox_2, w_br_dsa_2, w_out_2, ffn2_w1_2, ffn2_w3_2, ffn2_w2_2,
):
    x = first_block(
        x, positions, norm_mix, w_in, cmp_pos_k, cmp_pos_v, cmp_k_w1, cmp_k_w2, cmp_v_w1,
        cmp_v_w2, w_proj_a, w_proj_b, w_out, norm_mlp, w_up, w_down, norm_final,
    )
    return second_block(
        x, c_2, positions_2, ada_w_2, ada_b_2, norm_g_2, ffn1_w1_2, ffn1_w3_2, ffn1_w2_2,
        w_in_2, fox_f_bias_2, fox_qk_g_2, dsa_qk_g_2, w_br_fox_2, w_br_dsa_2, w_out_2,
        ffn2_w1_2, ffn2_w3_2, ffn2_w2_2,
    )


_drawn_inputs = setup_inputs


def setup_inputs(seed=0):
    import zlib

    import numpy as np

    out = dict(_drawn_inputs(seed))
    spreads = {}
    factors = {'norm_mix': 3.777,
     'cmp_pos_k': 8.0,
     'cmp_pos_v': 3.876,
     'norm_mlp': 3.072,
     'norm_final': 2.802,
     'ada_b_2': 3.493,
     'norm_g_2': 4.241,
     'fox_f_bias_2': 64.0,
     'fox_qk_g_2': 8.0,
     'dsa_qk_g_2': 8.0}
    for name, (base, spread) in spreads.items():
        noise = np.random.default_rng([zlib.crc32(name.encode()), seed]).standard_normal(out[name].shape)
        drawn = base * np.exp(spread * noise) if base else spread * noise
        out[name] = jnp.asarray(drawn.astype(out[name].dtype))
    for name, factor in factors.items():
        out[name] = (out[name] * factor).astype(out[name].dtype)
    return out
```

```python
import math
from contextlib import ExitStack

import numpy as np
import concourse.bass as bass
from concourse import mybir

F32 = mybir.dt.float32
F32R = mybir.dt.float32r
I32 = mybir.dt.int32
ALU = mybir.AluOpType
ACT = mybir.ActivationFunctionType
AX = mybir.AxisListType.X

P = 128
S = 512
NT = S // P
D = 1024
KD = D // P
SLAB = 1024
SLOTS = 4
EPS = 1e-6
NEG = -1e30
TAKEN = -2e30
MAGIC = 12582912.0
TOPK = min(256, S // 4)

W1 = dict(q=0, kc=512, vc=640, ks=768, vs=896, kw=1024, vw=1152, gates=1280, rq=1304, rk=1816, rv=2328, rg=2840,
          ga=3352, gb=4376)
W2 = dict(fq=0, fk=512, fv=1024, ff=1536, dq=1544, dk=2056, dv=2120, iq=2184, ik=2440, iw=2472, ga=2480, gb=3504)
MLP_H = 4096
FFN_H = 2816
N_CMP = (S - 32) // 16 + 1
CMP_S = 16

C_ID, C_MEAN, C_HD128, C_HD64, C_PN, C_PR, C_PI, C_CAUSAL, C_ADM, C_CMP, C_MISC = [i * P for i in range(11)]
C_AV = C_MISC
C_INV = C_MISC + NT
C_EPS = C_INV + 4
C_END = C_EPS + 1

V_MIX, V_MLP, V_FINAL, V_G2, V_C, V_ADAB = 0, 8, 16, 24, 48, 56
V2_PEK, V2_PEV, V2_FQ, V2_FK, V2_DQ, V2_DK, V2_N = 0, 16, 32, 33, 34, 35, 36


def weight_stream():
    at, n = {}, 0
    for name, count in (("ret", 16), ("nsa", 10), ("cmpk", 4), ("cmpv", 4), ("mix1", 24), ("out1", 8),
                        ("up0", 16), ("down0", 16), ("up1", 16), ("down1", 16),
                        ("f1up0", 24), ("f1down0", 12), ("f1up1", 20), ("f1down1", 10),
                        ("fox", 12), ("dsa", 7), ("mix2", 24), ("out2", 8),
                        ("f2up0", 24), ("f2down0", 12), ("f2up1", 20), ("f2down1", 10)):
        at[name] = n
        n += count
    return at, n


AT, N_SLABS = weight_stream()


def proj_blocks():
    rope = lambda t, i, trig, perm, scale=1.0: ("rope", t, i, trig, perm, scale)
    first = [("B", W1["rq"] + 256 * b, 128, False, [rope("rqT", 2 * b + c, 1, C_PR) for c in range(2)]) for b in range(2)]
    first += [("B", W1["rk"] + 256 * b, 128, False,
               [rope("rkT", 2 * b + c, 1, C_PR, 128 ** -0.5) for c in range(2)]) for b in range(2)]
    first += [("A", W1["rv"] + 256 * b, 128, ("rv", 256 * b)) for b in range(2)]
    first += [("B", W1["rg"] + 256 * b, 128, False, [("silu", "srg", 2 * b + c) for c in range(2)]) for b in range(2)]
    nsa = [("B", W1["q"] + 128 * b, 256, True, [rope("qT", 2 * b + c, 0, C_PN, 0.125) for c in range(2)]) for b in range(2)]
    nsa += [("B", W1["kc"], 128, False, [rope("kvT", 0, 0, C_PN), ("copy", "kvT", 1)]),
            ("B", W1["ks"], 256, False, [rope("kvT", 2, 0, C_PN), rope("kvT", 3, 0, C_PN)]),
            ("A", W1["vs"], 256, ("vrow", 0)), ("G", 24, "gates", 1)]
    fox = [("B", W2["fq"] + 256 * b, 128, False, [("norm", "fqT", 2 * b + c, 0) for c in range(2)]) for b in range(2)]
    fox += [("B", W2["fk"] + 256 * b, 128, False, [("norm", "fkT", 2 * b + c, 1) for c in range(2)]) for b in range(2)]
    fox += [("A", W2["fv"] + 256 * b, 128, ("fv", 256 * b)) for b in range(2)] + [("G", 48, "rowS", 2)]
    dsa = [("B", W2["dq"] + 256 * b, 128, False, [("normrope", "dqT", 2 * b + c, 2, 0, C_PN) for c in range(2)])
           for b in range(2)]
    dsa += [("B", W2["iq"], 128, False, [rope("iqT", c, 1, C_PI) for c in range(2)])]
    dsa += [("K", W2["dk"], 0, False, [("normrope", "dkT", 0, 3, 0, C_PN), rope("ikT", 0, 1, C_PI)])]
    return first, nsa, fox, dsa


def plan_projection(blocks):
    chunks, per_block = [], []
    for n, b in enumerate(blocks):
        mine = []
        if b[0] in "BK":
            for c in b[4]:
                if c[0] in ("rope", "norm", "normrope"):
                    mine.append(len(chunks))
                    chunks.append(c)
        per_block.append(mine)
    turns = []
    for n in range(len(blocks) + 2):
        now = []
        if 0 <= n - 2 < len(blocks):
            now += [("perm", v) for v in per_block[n - 2] if chunks[v][0] == "normrope"]
        if 0 <= n - 1 < len(blocks):
            now += [("perm" if chunks[v][0] == "rope" else "ms", v) for v in per_block[n - 1]]
        turns.append(now)
    return chunks, turns


def mix_kernel(nc, T, out):
    with ExitStack() as ctx:
        def sem(name):
            return ctx.enter_context(nc.semaphore(name))

        base = 16512
        used = [base]

        def sb(name, shape, dt=F32, at=None):
            size = int(np.prod(shape[1:])) * 4
            if at is None:
                at = used[0]
                used[0] += (size + 31) // 32 * 32
                assert used[0] <= 229344, used[0]
            return nc.alloc_sbuf_tensor_at(name, list(shape), dt, offset=at)

        KB = 1024
        xT = sb("xT", [P, KD, S])
        hhi = sb("hhi", [P, KD, S], F32R)
        hlo = sb("hlo", [P, KD, S], F32R)
        raw = sb("raw", [P, SLOTS, SLAB])
        whi = sb("whi", [P, SLOTS, SLAB], F32R)
        wlo = sb("wlo", [P, SLOTS, SLAB], F32R)
        R = used[0]
        used[0] += 64 * KB
        hidhi = sb("hidhi", [P, 16, S], F32R, R)
        hidlo = sb("hidlo", [P, 16, S], F32R, R + 32 * KB)
        mixhi = sb("mixhi", [P, KD, S], F32R, R + 32 * KB)
        mixlo = sb("mixlo", [P, KD, S], F32R, R + 48 * KB)
        xrow = sb("xrow", [P, NT, D], F32, R + 32 * KB)
        adaw = sb("adaw", [P, 8, SLAB], F32, R)
        t4 = lambda name, at, n=4, dt=F32: sb(name, [P, n, S], dt, R + at * KB)
        rqT, rkT, qT, srg, kvT, rv = (t4(n, a) for n, a in (("rqT", 0), ("rkT", 8), ("qT", 16), ("srg", 24),
                                                         ("kvT", 32), ("rv", 44)))
        vrow = sb("vrow", [P, NT, 256], F32, R + 40 * KB)
        dmat = t4("dmat", 52)
        gates = sb("gates", [P, NT, 24], F32, R + 60 * KB)
        kcmpT = sb("kcmpT", [P, 32], F32, R + 61 * KB)
        vcmp = sb("vcmp", [32, P], F32, R + 61 * KB + 128)
        cmpw2 = sb("cmpw2", [P, 2, 2, 64], F32, R + 62 * KB)
        hidc = sb("hidc", [P, 2, 64], F32, R + 63 * KB)
        sigc = sb("sigc", [P, 2, 64], F32, R + 63 * KB + 512)
        kshift = sb("kshift", [P, 2, S], F32, R + 44 * KB)
        blkf = sb("blkf", [P, CMP_S, 62], F32, R + 48 * KB)
        blkhi = sb("blkhi", [P, CMP_S, 62], F32R, R + 52 * KB)
        blklo = sb("blklo", [P, CMP_S, 62], F32R, R + 56 * KB)
        O1 = {"a": (t4("nsahi", 16, 4, F32R), t4("nsalo", 24, 4, F32R)),
              "b": (t4("rethi", 0, 4, F32R), t4("retlo", 8, 4, F32R))}
        fqT, fkT, dqT, fv = (t4(n, a) for n, a in (("fqT", 0), ("fkT", 8), ("dqT", 16), ("fv", 32)))
        fkb = t4("fkb", 24, 2)
        dkT = t4("dkT", 40, 1)
        dvrow = sb("dvrow", [P, NT, 64], F32, R + 42 * KB)
        iqT = t4("iqT", 46, 2)
        ikT = t4("ikT", 50, 1)
        sel = t4("sel", 52)
        score = t4("score", 60, 2)
        rowS = sb("rowS", [P, NT, 48], F32, R + 43 * KB)
        FT = sb("FT", [8, S], F32, R + 44 * KB)
        O2 = {"a": (t4("foxhi", 0, 4, F32R), t4("foxlo", 8, 4, F32R)),
              "b": (t4("dsahi", 16, 4, F32R), t4("dsalo", 24, 4, F32R))}
        trig = sb("trig", [P, 2, 2, S])
        cst = sb("cst", [P, C_END])
        vec = sb("vec", [P, P])
        vec2 = sb("vec2", [P, V2_N])
        mod = sb("mod", [P, 72])
        geff = sb("geff", [P, 24])
        foxb = sb("foxb", [8, 1])
        st = sb("st", [P, 4, S])
        tmp = sb("tmp", [P, 4, S])
        rstd = sb("rstd", [P, S])
        Pb = sb("Pb", [P, 2, S])
        posi = sb("posi", [P, S], I32, used[0])
        PT = sb("PT", [P, 2, S])
        SQ = [Pb[:, 0, :], Pb[:, 1, :], PT[:, 0, :], PT[:, 1, :]]
        stat = sb("stat", [P, 4, 4])
        Fq = sb("Fq", [P, NT, 8])
        posf = tmp[:, 3, :]
        wsm = sb("wsm", [P, KD, 48], F32, None)
        wsmhi = sb("wsmhi", [P, KD, 48], F32R)
        wsmlo = sb("wsmlo", [P, KD, 48], F32R)
        rows = Pb[:, :, :].rearrange("p a n -> p (a n)")
        Sp = tmp[:, 0:2, :]
        dkrow = tmp[:, 2, :].rearrange("p (t n) -> p t n", t=NT)
        ikrow = tmp[:, 3, :].rearrange("p (t n) -> p t n", t=NT)
        top8 = sb("top8", [P, 8])
        BUF = dict(rqT=rqT, rkT=rkT, qT=qT, srg=srg, kvT=kvT, rv=rv, vrow=vrow, fqT=fqT, fkT=fkT, dqT=dqT, fv=fv,
                   iqT=iqT, ikT=ikT, dkT=dkT)
        ps = ctx.enter_context(nc.psum_tensor("ps", [P, 8, S], F32))
        col = lambda c, n=1: cst[:, c:c + n]
        ident = cst[:, C_ID:C_ID + P]

        w_landed = [sem(f"w_landed{i}") for i in range(SLOTS)]
        w_go = sem("w_go")
        w_hi = sem("w_hi")
        w_split = sem("w_split")
        w_used = sem("w_used")
        ld_cst, ld_x, ld_rows, ld_pos, ld_dmat, ld_w2 = (sem(n) for n in ("ld_cst", "ld_x", "ld_rows", "ld_pos",
                                                                          "ld_dmat", "ld_w2"))
        ld_wsm = sem("ld_wsm")
        wsm_hi, wsm_ready = sem("wsm_hi"), sem("wsm_ready")
        x_turned, x_ready = sem("x_turned"), sem("x_ready")
        vec_turned, vec_ready, vec_scaled = sem("vec_turned"), sem("vec_ready"), sem("vec_scaled")
        cond_sig, cond_ready = sem("cond_sig"), sem("cond_ready")
        ada_landed = [sem(f"ada_landed{i}") for i in range(8)]
        ada_used, mod_ready = sem("ada_used"), sem("mod_ready")
        trig_arg, trig_ready = sem("trig_arg"), sem("trig_ready")
        n_sq, n_sum, n_root, n_t, n_hi, h_ready = (sem(n) for n in ("n_sq", "n_sum", "n_root", "n_t", "n_hi", "h_ready"))
        dve = sem("dve_chain")
        act = sem("act_chain")
        pj_mm, pj_ev, pj_post, pj_root, pj_dve, pj_silu = (sem(n) for n in ("pj_mm", "pj_ev", "pj_post", "pj_root",
                                                                             "pj_dve", "pj_silu"))
        rt_qk, rt_sd, rt_pv, rt_ev, rt_sum, rt_root, rt_o, rt_hi, rt_done = (
            sem(n) for n in ("rt_qk", "rt_sd", "rt_pv", "rt_ev", "rt_sum", "rt_root", "rt_o", "rt_hi", "rt_done"))
        cm_shift, cm_blk, cm_mm, cm_sig, cm_hid, cm_out, cm_done = (
            sem(n) for n in ("cm_shift", "cm_blk", "cm_mm", "cm_sig", "cm_hid", "cm_out", "cm_done"))
        f_turn, f_z, f_e, f_l, f_scan, f_back, f_ready = (sem(n) for n in ("f_turn", "f_z", "f_e", "f_l", "f_scan",
                                                                            "f_back", "f_ready"))
        fk_mm, fk_ready = sem("fk_mm"), sem("fk_ready")
        ix_mm, ix_relu, ix_acc, ix_done = sem("ix_mm"), sem("ix_relu"), sem("ix_acc"), sem("ix_done")
        mx_g, mx_p, mx_sig, mx_m, mx_t, mx_hi, mx_ready = (sem(n) for n in ("mx_g", "mx_p", "mx_sig", "mx_m", "mx_t",
                                                                            "mx_hi", "mx_ready"))
        dn_done = sem("dn_done")
        up_mm, up_relu, up_t, up_hi, up_ready = (sem(n) for n in ("up_mm", "up_relu", "up_t", "up_hi", "up_ready"))
        ff_g, ff_u, ff_sig, ff_m1, ff_m2, ff_hi, ff_ready = (sem(n) for n in ("ff_g", "ff_u", "ff_sig", "ff_m1", "ff_m2",
                                                                              "ff_hi", "ff_ready"))
        y_turned, y_ready, y_stored = sem("y_turned"), sem("y_ready"), sem("y_stored")

        BL = dict(zip(("ret", "nsa", "fox", "dsa"), proj_blocks()))
        PLAN = {name: plan_projection(b) for name, b in BL.items()}
        G0, P0, R0, SL0 = {}, {}, {}, {}
        g = p = r = sl = 0
        n_out = {"A": 4, "G": 4, "B": 2, "K": 6}
        for name, blocks in BL.items():
            G0[name], P0[name], R0[name], SL0[name] = g, p, r, sl
            g += sum(n_out[b[0]] for b in blocks)
            p += sum(len(t) for t in PLAN[name][1])
            r += sum(k == "ms" for t in PLAN[name][1] for k, _ in t)
            sl += sum(c[0] == "silu" for b in blocks if b[0] == "B" for c in b[4])
        PEND = dict(zip(BL, [P0["nsa"], P0["fox"], P0["dsa"], p]))
        GEND = dict(zip(BL, [G0["nsa"], G0["fox"], G0["dsa"], g]))
        post_event, last_event = {}, {}
        for name in BL:
            p = P0[name]
            for turn in PLAN[name][1]:
                for kind, v in turn:
                    post_event[name, kind, v] = p
                    last_event[name, v] = p
                    p += 1
        MS_EVENT = {}
        n_ms = {}
        for name in BL:
            for turn in PLAN[name][1]:
                for kind, v in turn:
                    if kind == "ms":
                        n_ms[name, v] = len(MS_EVENT)
                        MS_EVENT[len(MS_EVENT)] = post_event[name, kind, v]
        post_ms = lambda name, v: n_ms[name, v]
        N_ROW_DMAS = 13
        OUT_DONE = {}
        mm = 0
        for name, blocks in BL.items():
            g, s = G0[name], AT[name]
            for b in blocks:
                s += {"A": 2, "B": 2, "K": 1, "G": 0}[b[0]]
                for x in range(n_out[b[0]]):
                    if b[0] != "G" and x == {"A": 3, "B": 1, "K": 3}[b[0]]:
                        OUT_DONE[g] = (w_used, s)
                    else:
                        mm += 1
                        OUT_DONE[g] = (pj_mm, mm)
                    g += 1
        DOWN_DONE = {}
        X_BEFORE_NORM = [0, 8, 24, 32, 48, 56]
        X_BEFORE_DOWN = dict(out1=8, down0=16, down1=24, f1down0=40, f1down1=48, out2=56, f2down0=64, f2down1=72)
        H_NORM = {0: 0, 1: 1, 3: 2, 4: 3, 5: 4}
        GAIN = {0: vec[:, V_MIX:V_MIX + 8], 1: vec[:, V_MLP:V_MLP + 8], 2: vec[:, V_FINAL:V_FINAL + 8],
                3: geff[:, 0:8], 4: geff[:, 8:16], 5: geff[:, 16:24]}
        SHIFT = {3: mod[:, 0:8], 4: mod[:, 24:32], 5: mod[:, 48:56]}
        QKG = {0: V2_FQ, 1: V2_FK, 2: V2_DQ, 3: V2_DK}
        DOWN_K = dict(down0=16, down1=16, f1down0=12, f1down1=10, f2down0=12, f2down1=10, out1=8, out2=8)
        for d, name in enumerate(X_BEFORE_DOWN):
            for m in range(KD):
                DOWN_DONE[name, m] = (dn_done, 7 * d + m + 1) if m < KD - 1 else (w_used, AT[name] + DOWN_K[name])

        def gate_done(b, n, br, c):
            return (mx_g, 8 * b + 2 * n + br + 1) if c == 0 else (w_used, AT[("mix1", "mix2")[b]] + 6 * n + 3 * br + 2)

        def branch_done(b, n, br, c):
            return (mx_p, 8 * b + 2 * n + br + 1) if c == 0 else (w_used, AT[("mix1", "mix2")[b]] + 6 * n + 3 * br + 3)

        def nsa_steps():
            out_ = []
            for c in range(4):
                for g in range(2):
                    for i in range(NT):
                        rows_ = slice(64 * g, 64 * g + 64)
                        head = 4 * g + c
                        q = qT[rows_, c, i * P:(i + 1) * P]
                        for b, (k, v) in enumerate((
                                (kcmpT[rows_, 0:N_CMP], [vcmp[0:N_CMP, 64 * g:64 * g + 64]]),
                                (kvT[rows_, 2, 0:(i + 1) * P], [vrow[:, j, 64 * g:64 * g + 64] for j in range(i + 1)]),
                                (kvT[rows_, 3, 0:(i + 1) * P],
                                 [vrow[:, j, 128 + 64 * g:192 + 64 * g] for j in range(i + 1)]))):
                            out_.append(dict(q=q, k=k, v=v, n=k.shape[-1], i=i, c=c, half=g, mask="cmp" if b == 0 else "causal",
                                             gate=gates[:, i, 3 * head + b:3 * head + b + 1], first=b == 0, last=b == 2,
                                             av=col(C_AV + i) if b == 0 else None))
            return out_

        def fox_steps():
            return [dict(q=fqT[64 * g:64 * g + 64, c, i * P:(i + 1) * P], k=fkT[64 * g:64 * g + 64, c, 0:(i + 1) * P],
                         v=[fv[:, j, 64 * (2 * c + g):64 * (2 * c + g) + 64] for j in range(i + 1)], n=(i + 1) * P, i=i, c=c,
                         half=g, mask="fox", head=2 * c + g, gate=None, av=None, first=True, last=True)
                    for c in range(4) for g in range(2) for i in range(NT)]

        def dsa_steps():
            return [dict(q=dqT[64 * g:64 * g + 64, c, i * P:(i + 1) * P], k=dkT[64 * g:64 * g + 64, 0, 0:(i + 1) * P],
                         v=[dvrow[:, j, :] for j in range(i + 1)], n=(i + 1) * P, i=i, c=c, half=g, mask="dsa",
                         gate=None, av=None, first=True, last=True)
                    for c in range(4) for g in range(2) for i in range(NT)]

        STEPS = {"nsa": nsa_steps(), "fox": fox_steps(), "dsa": dsa_steps()}
        at_qk, at_max, at_exp, at_nrm, at_tr, at_pt, at_pv, at_hi, at_done = (
            {ph: sem(f"{ph}_{w}") for ph in STEPS} for w in ("qk", "max", "exp", "nrm", "tr", "pt", "pv", "hi", "done"))
        OUT = {"nsa": O1["a"], "fox": O2["a"], "dsa": O2["b"]}
        CHUNK_END = {ph: [max(s for s, t in enumerate(steps) if t["c"] == c) for c in range(4)]
                     for ph, steps in STEPS.items()}
        AFTER = 3

        block = ctx.enter_context(nc.Block())

        @block.sync
        def _(sp):
            def load(s, src, after=None):
                slot = AT_SLOT(s)
                if after is not None:
                    sp.wait_ge(w_split, after)
                if len(src.shape) == 4:
                    for g in range(2):
                        dst = raw[:, slot, :].rearrange("p (k g n) -> p k g n", k=src.shape[1], g=2)[:, :, g, :]
                        sp.dma_start(dst, src[:, :, g, :]).then_inc(w_landed[slot], 16)
                    return
                for a in (0, 64):
                    dst = raw[a:a + 64, slot, :]
                    if len(src.shape) == 3:
                        dst = dst.rearrange("p (k n) -> p k n", k=src.shape[1])
                    sp.dma_start(dst, src[a:a + 64]).then_inc(w_landed[slot], 16)

            def AT_SLOT(s):
                return s % SLOTS

            def load_next(s, src):
                load(s, src, s - SLOTS + 1 if s >= SLOTS else None)

            def cols(w, k0, c0, stride):
                v = w[k0 * P:(k0 + 4) * P, :].rearrange("(k p) n -> p k n", p=P)
                if stride == P:
                    return v[:, :, c0:c0 + 256]
                return v[:, :, c0:c0 + 2 * stride].rearrange("p k (g n) -> p k g n", n=stride)[:, :, :, 0:P]

            def load_projection(name, w, start=0, end=N_SLABS):
                s = AT[name]
                for b in BL[name]:
                    if b[0] in "AB":
                        for q in range(2):
                            if start <= s - AT[name] < end:
                                load_next(s, cols(w, 4 * q, b[1], b[2]))
                            s += 1
                    elif b[0] == "K":
                        load_next(s, w.rearrange("(k p) n -> p k n", p=P)[:, :, b[1]:b[1] + P])
                        s += 1

            def load_mix(name, w, ga, gb, wa, wb, heads_apart):
                s = AT[name]
                for n in range(4):
                    for gate, wp, apart in ((ga, wa, heads_apart), (gb, wb, False)):
                        for q in range(2):
                            load_next(s, cols(w, 4 * q, gate + 256 * n, P))
                            s += 1
                        if apart:
                            sp.wait_ge(w_split, s - SLOTS + 1)
                            for g in range(2):
                                sp.dma_start(
                                    raw[64 * g:64 * g + 64, s % SLOTS, :].rearrange("p (k n) -> p k n", k=4),
                                    wp[256 * g:256 * g + 256, 256 * n:256 * n + 256].rearrange("(c p) n -> p c n", p=64),
                                ).then_inc(w_landed[s % SLOTS], 16)
                        else:
                            load_next(s, cols(wp, 0, 256 * n, P))
                        s += 1

            def load_rows(name, w, k0):
                s0 = AT[name]
                K = DOWN_K[name]
                v = w.rearrange("(k p) n -> k p n", p=P)
                n4 = K // 4
                with sp.Fori(0, n4) as i:
                    for j in range(4):
                        sp.wait_ge(w_split, i * 4 + (s0 + j - SLOTS + 1))
                        for a in (0, 64):
                            sp.dma_start(raw[a:a + 64, (s0 + j) % SLOTS, :],
                                         v[bass.ds(i * 4 + (k0 + j), 1), a:a + 64, :].rearrange("k p n -> (k p) n"))\
                              .then_inc(w_landed[(s0 + j) % SLOTS], 16)
                for k in range(4 * n4, K):
                    load_next(s0 + k, v[k0 + k])

            def load_up(name, c0, ws):
                s0 = AT[name]
                per = 2 * len(ws)
                n = {"up0": 4, "up1": 4}.get(name, (6 if name.endswith("0") else 5))
                body = [(w, q, b) for b in range(2 if len(ws) == 1 else 1) for w in ws for q in range(2)]
                step = 256 * (2 if len(ws) == 1 else 1)
                assert len(body) == 4
                with sp.Fori(0, n) as i:
                    for j, (w, q, b) in enumerate(body):
                        sp.wait_ge(w_split, i * 4 + (s0 + j - SLOTS + 1))
                        v = w[4 * q * P:4 * (q + 1) * P, :].rearrange("(k p) n -> p k n", p=P)
                        for a in (0, 64):
                            sp.dma_start(raw[a:a + 64, (s0 + j) % SLOTS, :].rearrange("p (k n) -> p k n", k=4),
                                         v[a:a + 64, :, bass.ds(i * step + (c0 + 256 * b), 256)])\
                              .then_inc(w_landed[(s0 + j) % SLOTS], 16)

            w_in, w_in_2 = T["w_in"][0], T["w_in_2"][0]
            ada = T["ada_w_2"][0].rearrange("(k p) n -> p k n", p=P)

            def load_ada(j, i, src):
                sp.dma_start(adaw[:, j, :].rearrange("p (k n) -> p k n", k=KD), src).then_inc(ada_landed[j], 16)

            for j in range(8):
                load_ada(j, 0, ada[:, :, P * j:P * j + P])
            load_projection("ret", w_in, 0, SLOTS)
            with sp.Fori(1, 9) as i:
                for j in range(8):
                    sp.wait_ge(ada_used, i * 8 + (j - 7))
                    load_ada(j, i, ada[:, :, bass.ds(i * 8 * P + P * j, P)])
            load_projection("ret", w_in, SLOTS, 16)
            load_projection("nsa", w_in)
            for name, w in (("cmpk", T["cmp_k_w1"][0]), ("cmpv", T["cmp_v_w1"][0])):
                v = w.rearrange("(s p) n -> p s n", p=P)
                for q in range(4):
                    load_next(AT[name] + q, v[:, 4 * q:4 * q + 4, :])
            load_mix("mix1", w_in, W1["ga"], W1["gb"], T["w_proj_a"][0], T["w_proj_b"][0], True)
            load_rows("out1", T["w_out"][0], 0)
            for h in range(2):
                load_up(f"up{h}", 2048 * h, [T["w_up"][0]])
                load_rows(f"down{h}", T["w_down"][0], 16 * h)

            def load_ffn(f, w1, w3, w2):
                for h in range(2):
                    load_up(f"{f}up{h}", 1536 * h, [w1, w3])
                    load_rows(f"{f}down{h}", w2, 12 * h)

            load_ffn("f1", T["ffn1_w1_2"][0], T["ffn1_w3_2"][0], T["ffn1_w2_2"][0])
            load_projection("fox", w_in_2)
            load_projection("dsa", w_in_2)
            load_mix("mix2", w_in_2, W2["ga"], W2["gb"], T["w_br_fox_2"][0], T["w_br_dsa_2"][0], False)
            load_rows("out2", T["w_out_2"][0], 0)
            load_ffn("f2", T["ffn2_w1_2"][0], T["ffn2_w3_2"][0], T["ffn2_w2_2"][0])
            for t in range(NT):
                sp.wait_ge(y_ready, 2 * t + 2)
                sp.dma_start(out[0, t * P:(t + 1) * P, :], xrow[:, t, :]).then_inc(y_stored, 16)
            sp.wait_ge(y_stored, 16 * NT)

        @block.gpsimd
        def _(pool):
            def split(slot, n, landed, free, by_head=False):
                pool.wait_ge(w_landed[slot], landed)
                if free is not None:
                    pool.wait_ge(w_used, free)
                    pool.sem_inc(w_go, 1)
                if by_head:
                    src = raw[:, slot, :].rearrange("p (k g c d) -> p c k g d", k=4, g=2, c=2)
                    view = lambda t: t[:, slot, :].rearrange("p (k c g d) -> p c k g d", k=4, g=2, c=2)
                    parts = [(view(whi)[:, c], view(wlo)[:, c], src[:, c]) for c in range(2)]
                else:
                    parts = [(whi[:, slot, :], wlo[:, slot, :], raw[:, slot, :])]
                for hi, lo, src in parts:
                    last = pool.tensor_copy(hi, src)
                last.then_inc(w_hi, 1)
                pool.wait_ge(w_hi, n)
                for hi, lo, src in parts:
                    last = pool.tensor_tensor(lo, src, hi.bitcast(F32), ALU.subtract)
                last.then_inc(w_split, 1)

            def rounds(first, end):
                with pool.Fori(first, end) as i:
                    for j in range(SLOTS):
                        split(j, i * SLOTS + (j + 1), i * 32 + 32, i * SLOTS + (j + 1 - SLOTS))

            q_round = AT["nsa"] // SLOTS
            for s in range(SLOTS):
                split(s, s + 1, 32, None)
            rounds(1, q_round)
            for s in range(SLOTS * q_round, SLOTS * (q_round + 1)):
                split(s % SLOTS, s + 1, 32 * (s // SLOTS + 1), s - SLOTS + 1, by_head=True)
            rounds(q_round + 1, N_SLABS // SLOTS)
            for s in range(N_SLABS // SLOTS * SLOTS, N_SLABS):
                split(s % SLOTS, s + 1, 32 * (s // SLOTS + 1), s - SLOTS + 1)

        @block.tensor
        def _(pe):
            def three(out_, lhi, llo, rhi, rlo, first, last):
                pe.matmul(out_, lhi, rhi, start=first, stop=False)
                pe.matmul(out_, lhi, rlo, start=False, stop=False)
                return pe.matmul(out_, llo, rhi, start=False, stop=last)

            def slab(s, k=4):
                return (whi[:, s % SLOTS, :].rearrange("p (k n) -> p k n", k=k),
                        wlo[:, s % SLOTS, :].rearrange("p (k n) -> p k n", k=k))

            def norm(n):
                for m in range(KD):
                    pe.wait_ge(n_sq, 8 * n + m + 1)
                    pe.matmul(ps[:, 0, :], cst[:, C_MEAN:C_MEAN + P], st[:, m % 2, :], start=m == 0, stop=m == KD - 1)\
                      .then_inc(n_sum, 1)

            def projection(name, hn):
                chunks, turns = PLAN[name]
                s, g = AT[name], G0[name]
                p, v = P0[name], 0
                out_of = []
                blocks = BL[name]

                def bank(x):
                    if x - 4 >= G0[name]:
                        pe.wait_ge(pj_ev, x - 3)
                    return x % 4

                for n in range(len(blocks) + 2):
                    if n < len(blocks):
                        b = blocks[n]
                        if b[0] == "B":
                            banks = [bank(g + c) for c in range(2)]
                            for q in range(2):
                                pe.wait_ge(w_split, s + 1)
                                hi, lo = slab(s)
                                for c in range(2):
                                    for k in range(4):
                                        kk = 4 * q + k
                                        if n == 0 and c == 0:
                                            pe.wait_ge(h_ready, 8 * hn + kk + 1)
                                        cc = slice(P * c, P * c + P)
                                        mm = three(ps[:, banks[c], :], hi[:, k, cc], lo[:, k, cc], hhi[:, kk, :], hlo[:, kk, :],
                                                   kk == 0, kk == 7)
                                    if q == 1 and c == 0:
                                        mm.then_inc(pj_mm, 1)
                                mm.then_inc(w_used, 1)
                                s += 1
                            for c in range(2):
                                if b[4][c][0] in ("rope", "norm", "normrope"):
                                    out_of.append(g + c)
                            g += 2
                        elif b[0] == "A":
                            banks = [bank(g + t) for t in range(NT)]
                            for q in range(2):
                                pe.wait_ge(w_split, s + 1)
                                hi, lo = slab(s)
                                for t in range(NT):
                                    tt = slice(t * P, t * P + P)
                                    for k in range(4):
                                        kk = 4 * q + k
                                        mm = three(ps[:, banks[t], 0:256], hhi[:, kk, tt], hlo[:, kk, tt], hi[:, k, :],
                                                   lo[:, k, :], kk == 0, kk == 7)
                                    if q == 1 and t < NT - 1:
                                        mm.then_inc(pj_mm, 1)
                                mm.then_inc(w_used, 1)
                                s += 1
                            g += NT
                        elif b[0] == "G":
                            pe.wait_ge(wsm_ready, b[3])
                            for t in range(NT):
                                tt = slice(t * P, t * P + P)
                                bk = bank(g)
                                for k in range(KD):
                                    mm = three(ps[:, bk, 0:b[1]], hhi[:, k, tt], hlo[:, k, tt], wsmhi[:, k, 0:b[1]],
                                               wsmlo[:, k, 0:b[1]], k == 0, k == 7)
                                mm.then_inc(pj_mm, 1)
                                g += 1
                        else:
                            pe.wait_ge(w_split, s + 1)
                            hi, lo = slab(s, KD)
                            for t in range(NT):
                                tt = slice(t * P, t * P + P)
                                bk = bank(g)
                                for k in range(KD):
                                    mm = three(ps[:, bk, 0:P], hhi[:, k, tt], hlo[:, k, tt], hi[:, k, :], lo[:, k, :],
                                               k == 0, k == 7)
                                if t < NT - 1:
                                    mm.then_inc(pj_mm, 1)
                                g += 1
                            mm.then_inc(w_used, 1)
                            s += 1
                            pe.wait_ge(pj_ev, g)
                            for rowsrc in (dkrow, ikrow):
                                bk = bank(g)
                                for t in range(NT):
                                    mm = pe.transpose(ps[:, bk, t * P:t * P + P], rowsrc[:, t, :], ident)
                                mm.then_inc(pj_mm, 1)
                                out_of.append(g)
                                g += 1
                    for kind, v in turns[n]:
                        c = chunks[v]
                        if p - 4 >= P0[name]:
                            pe.wait_ge(pj_dve, p - 3)
                        if kind == "ms":
                            pe.wait_ge(pj_ev, out_of[v] + 1)
                            m = post_ms(name, v)
                            pe.matmul(ps[:, 4 + p % 4, :], cst[:, C_HD64:C_HD64 + P], SQ[m % 4], start=True, stop=True)\
                              .then_inc(pj_post, 1)
                        else:
                            if c[0] == "rope":
                                pe.wait_ge(pj_ev, out_of[v] + 1)
                            else:
                                pe.wait_ge(pj_dve, post_event[name, "ms", v] + 1)
                            perm = c[4] if c[0] == "rope" else c[5]
                            pe.matmul(ps[:, 4 + p % 4, :], cst[:, perm:perm + P], st[:, v % 4, :], start=True, stop=True)\
                              .then_inc(pj_post, 1)
                        p += 1

            def retention():
                idx = 0

                def pv(x):
                    h, j = x // NT, x % NT
                    pe.wait_ge(rt_sd, x + 1)
                    if j == 0 and h >= 2:
                        pe.wait_ge(rt_ev, h - 1)
                    pe.matmul(ps[:, 3 + h % 2, j * P:S], rv[:, j, h * P:h * P + P], Pb[:, x % 2, 0:S - j * P],
                              start=j == 0, stop=j == NT - 1).then_inc(rt_pv, 1)

                def head_sum(h):
                    pe.wait_ge(rt_ev, h + 1)
                    pe.matmul(ps[:, 5 + h % 2, :], cst[:, C_HD128:C_HD128 + P], PT[:, h % 2, :], start=True, stop=True)\
                      .then_inc(rt_sum, 1)

                pe.wait_ge(pj_dve, PEND["ret"])
                pe.wait_ge(pj_ev, GEND["ret"])
                for h in range(4):
                    for j in range(NT):
                        if idx >= 3:
                            pe.wait_ge(rt_sd, idx - 2)
                        pe.matmul(ps[:, idx % 3, 0:S - j * P], rkT[:, h, j * P:j * P + P], rqT[:, h, j * P:S],
                                  start=True, stop=True).then_inc(rt_qk, 1)
                        if idx >= 1:
                            pv(idx - 1)
                        if j == 2 and h >= 1:
                            head_sum(h - 1)
                        idx += 1
                pv(15)
                head_sum(3)

            def compress():
                for kv, name in enumerate(("cmpk", "cmpv")):
                    pe.wait_ge(cm_blk, kv + 1)
                    if kv == 0:
                        pe.wait_ge(pj_ev, GEND["nsa"])
                    else:
                        pe.wait_ge(cm_hid, 2)
                    for q in range(4):
                        s = AT[name] + q
                        pe.wait_ge(w_split, s + 1)
                        hi, lo = slab(s)
                        for hc in range(2):
                            for k in range(4):
                                kk = 4 * q + k
                                mm = three(ps[:, hc, 0:62], hi[:, k, P * hc:P * hc + P], lo[:, k, P * hc:P * hc + P],
                                           blkhi[:, kk, :], blklo[:, kk, :], kk == 0, kk == CMP_S - 1)
                            if q == 3 and hc == 0:
                                mm.then_inc(cm_mm, 1)
                        mm.then_inc(w_used, 1)
                    pe.wait_ge(cm_hid, 2 * kv + 2)
                    if kv == 0:
                        pe.wait_ge(ld_w2, 32)
                    for g in range(2):
                        gs = slice(64 * g, 64 * g + 64)
                        for hc in range(2):
                            hid = hidc[:, hc, N_CMP * g:N_CMP * (g + 1)]
                            if kv == 0:
                                mm = pe.matmul(ps[gs, 2, 0:N_CMP], cmpw2[:, 0, hc, :], hid, start=hc == 0, stop=hc == 1)
                            else:
                                mm = pe.matmul(ps[0:N_CMP, 3, gs], hid, cmpw2[:, 1, hc, :], start=hc == 0, stop=hc == 1)
                    mm.then_inc(cm_out, 1)

            def attention(ph):
                steps = STEPS[ph]

                def scores(s):
                    t = steps[s]
                    if s >= 3:
                        pe.wait_ge(at_exp[ph], s - 2)
                    if t["mask"] == "fox" and t["i"] == 0:
                        h = t["head"]
                        if h >= 1:
                            pe.wait_ge(fk_ready, h)
                        pe.matmul(ps[:, 7, :], cst[0:8, C_ID + h:C_ID + h + 1].broadcast_to([8, P]), FT[:, :],
                                  start=True, stop=True).then_inc(fk_mm, 1)
                    pe.matmul(ps[:, s % 3, 0:t["n"]], t["q"], t["k"], start=True, stop=True).then_inc(at_qk[ph], 1)

                def turn(s):
                    t = steps[s]
                    pe.wait_ge(at_nrm[ph], s + 1)
                    if s >= 2:
                        pe.wait_ge(at_pt[ph], s - 1)
                    for j in range(len(t["v"])):
                        nk = min(P, t["n"] - j * P)
                        mm = pe.transpose(ps[0:nk, 3 + s % 2, j * P:j * P + P], Pb[:, s % 2, j * P:j * P + nk], ident)
                    mm.then_inc(at_tr[ph], 1)

                def values(s):
                    t = steps[s]
                    pe.wait_ge(at_pt[ph], s + 1)
                    if t["c"] >= 2 and s == CHUNK_END[ph][t["c"] - 1] + 1:
                        pe.wait_ge(at_done[ph], t["c"] - 1)
                    nv = len(t["v"])
                    for j in range(nv):
                        nk = min(P, t["n"] - j * P)
                        mm = pe.matmul(ps[64 * t["half"]:64 * t["half"] + 64, 5 + t["c"] % 2, t["i"] * P:(t["i"] + 1) * P],
                                       t["v"][j], PT[0:nk, s % 2, j * P:j * P + P], start=t["first"] and j == 0,
                                       stop=t["last"] and j == nv - 1)
                    mm.then_inc(at_pv[ph], 1)

                n = len(steps)
                scores(0)
                scores(1)
                for s in range(n + 1):
                    if s < n:
                        turn(s)
                    if s + 2 < n:
                        scores(s + 2)
                    if s >= 1:
                        values(s - 1)

            def forget():
                pe.wait_ge(pj_ev, GEND["fox"])
                pe.wait_ge(pj_dve, PEND["fox"])
                for t in range(NT):
                    mm = pe.transpose(ps[0:8, 7, t * P:t * P + P], rowS[:, t, 0:8], ident)
                mm.then_inc(f_turn, 1)
                pe.wait_ge(f_scan, 1)
                for t in range(NT):
                    mm = pe.transpose(ps[:, 6, 8 * t:8 * t + 8], FT[:, t * P:t * P + P], cst[0:8, C_ID:C_ID + 8])
                mm.then_inc(f_back, 1)
                pe.wait_ge(f_ready, 1)

            def index_scores():
                pe.wait_ge(pj_ev, GEND["dsa"])
                pe.wait_ge(pj_dve, PEND["dsa"])
                x = 0
                for i in range(1, NT):
                    for h in range(8):
                        rs = slice(32 * (h % 4), 32 * (h % 4) + 32)
                        if x >= 4:
                            pe.wait_ge(ix_relu, x - 3)
                        pe.matmul(ps[:, x % 4, 0:(i + 1) * P], iqT[rs, h // 4, i * P:(i + 1) * P], ikT[rs, 0, 0:(i + 1) * P],
                                  start=True, stop=True).then_inc(ix_mm, 1)
                        x += 1

            def mix(b, name, outs):
                s = AT[name]
                for n in range(4):
                    for br in range(2):
                        x0 = 16 * b + 4 * n + 2 * br
                        for c in range(2):
                            if n >= 1:
                                pe.wait_ge(mx_sig, x0 + c - 4 + 1)
                        for q in range(2):
                            pe.wait_ge(w_split, s + 1)
                            hi, lo = slab(s)
                            for c in range(2):
                                for k in range(4):
                                    kk = 4 * q + k
                                    mm = three(ps[:, 4 * br + c, :], hi[:, k, P * c:P * c + P], lo[:, k, P * c:P * c + P],
                                               hhi[:, kk, :], hlo[:, kk, :], kk == 0, kk == 7)
                                if q == 1 and c == 0:
                                    mm.then_inc(mx_g, 1)
                            mm.then_inc(w_used, 1)
                            s += 1
                        pe.wait_ge(w_split, s + 1)
                        hi, lo = slab(s)
                        ohi, olo = outs["ab"[br]]
                        for c in range(2):
                            if n >= 1:
                                pe.wait_ge(mx_m, x0 + c - 4 + 1)
                            for k in range(4):
                                mm = three(ps[:, 4 * br + 2 + c, :], hi[:, k, P * c:P * c + P], lo[:, k, P * c:P * c + P],
                                           ohi[:, k, :], olo[:, k, :], k == 0, k == 3)
                            if c == 0:
                                mm.then_inc(mx_p, 1)
                        mm.then_inc(w_used, 1)
                        s += 1

            def down(name, ahi, alo, ready, ready0, banks_free):
                K, s0 = DOWN_K[name], AT[name]

                def one(k, i=None, j=0):
                    if i is None:
                        s = s0 + k
                        pe.wait_ge(w_split, s + 1)
                        pe.wait_ge(ready, ready0 + k + 1)
                        rhi, rlo = ahi[:, k, :], alo[:, k, :]
                    else:
                        s = s0 + 1 + j
                        pe.wait_ge(w_split, i * 4 + (s + 1))
                        rhi = ahi[:, bass.ds(i * 4 + (1 + j), 1), :].rearrange("p k n -> p (k n)")
                        rlo = alo[:, bass.ds(i * 4 + (1 + j), 1), :].rearrange("p k n -> p (k n)")
                    hi, lo = slab(s, KD)
                    for m in range(KD):
                        if k == 0:
                            banks_free(m)
                        mm = three(ps[:, m, :], hi[:, m, :], lo[:, m, :], rhi, rlo, k == 0, k == K - 1)
                        if k == K - 1 and m < KD - 1:
                            mm.then_inc(dn_done, 1)
                    mm.then_inc(w_used, 1)

                if K > 8:
                    one(0)
                    pe.wait_ge(ready, ready0 + K)
                    loops = (K - 2) // 4
                    with pe.Fori(0, loops) as i:
                        for j in range(4):
                            one(1, i, j)
                    for k in range(1 + 4 * loops, K):
                        one(k)
                else:
                    for k in range(K):
                        one(k)

            def up(h):
                s0, u0 = AT[f"up{h}"], 16 * h

                def blocks(i):
                    for b in range(2):
                        for q in range(2):
                            j = 2 * b + q
                            pe.wait_ge(w_split, i * 4 + (s0 + j + 1))
                            hi, lo = slab(s0 + j)
                            for c in range(2):
                                ch = 2 * b + c
                                if q == 0:
                                    if isinstance(i, int):
                                        if h == 1:
                                            pe.wait_ge(x_ready, X_BEFORE_DOWN["down0"] + ch + 1)
                                    else:
                                        pe.wait_ge(up_relu, i * 4 + (u0 + ch - 3))
                                for k in range(4):
                                    kk = 4 * q + k
                                    if isinstance(i, int) and h == 0 and b == 0 and c == 0:
                                        pe.wait_ge(h_ready, 8 + kk + 1)
                                    mm = three(ps[:, ch, :], hi[:, k, P * c:P * c + P], lo[:, k, P * c:P * c + P],
                                               hhi[:, kk, :], hlo[:, kk, :], kk == 0, kk == 7)
                                if q == 1 and c == 0:
                                    mm.then_inc(up_mm, 1)
                            mm.then_inc(w_used, 1)

                blocks(0)
                with pe.Fori(1, 4) as i:
                    blocks(i)

            def ffn_up(f, h, hn):
                s0, u0 = AT[f"f{f + 1}up{h}"], 22 * f + 12 * h
                n = 6 - h
                before = X_BEFORE_DOWN[f"f{f + 1}down0"]

                def blocks(i):
                    for w, done, free in ((0, ff_g, ff_m1), (1, ff_u, ff_m2)):
                        for q in range(2):
                            j = 2 * w + q
                            pe.wait_ge(w_split, i * 4 + (s0 + j + 1))
                            hi, lo = slab(s0 + j)
                            for c in range(2):
                                if q == 0:
                                    if isinstance(i, int):
                                        if h == 1:
                                            pe.wait_ge(x_ready, before + 2 * w + c + 1)
                                    else:
                                        pe.wait_ge(free, i * 2 + (u0 + c - 1))
                                for k in range(4):
                                    kk = 4 * q + k
                                    if isinstance(i, int) and h == 0 and w == 0 and c == 0:
                                        pe.wait_ge(h_ready, 8 * hn + kk + 1)
                                    mm = three(ps[:, 2 * w + c, :], hi[:, k, P * c:P * c + P], lo[:, k, P * c:P * c + P],
                                               hhi[:, kk, :], hlo[:, kk, :], kk == 0, kk == 7)
                                if q == 1 and c == 0:
                                    mm.then_inc(done, 1)
                            mm.then_inc(w_used, 1)

                blocks(0)
                with pe.Fori(1, n) as i:
                    blocks(i)

            def ffn(f, hn):
                for h in range(2):
                    name = f"f{f + 1}down{h}"
                    ffn_up(f, h, hn)
                    u1 = 22 * f + 12 * h + (12 if h == 0 else 10)

                    def free(m):
                        if m < 4:
                            pe.wait_ge((ff_m1, ff_m2)[m // 2], u1)
                        elif h == 1:
                            pe.wait_ge(x_ready, X_BEFORE_DOWN[f"f{f + 1}down0"] + m + 1)
                    down(name, hidhi, hidlo, ff_ready, 22 * f + 12 * h, free)

            pe.wait_ge(ld_cst, 16)
            for m in range(KD):
                if m == 0:
                    pe.wait_ge(ld_x, 16)
                for t in range(NT):
                    mm = pe.transpose(ps[:, m, t * P:t * P + P], xrow[:, t, m * P:m * P + P], ident)
                mm.then_inc(x_turned, 1)
            pe.wait_ge(ld_rows, 16 * N_ROW_DMAS)
            pe.wait_ge(x_ready, 2)
            pe.transpose(ps[:, 0, 0:P], rows[:, 0:P], ident).then_inc(vec_turned, 1)
            pe.transpose(ps[:, 1, 0:V2_N], rows[0:V2_N, P:2 * P], cst[0:V2_N, C_ID:C_ID + V2_N]).then_inc(vec_turned, 1)
            pe.wait_ge(vec_ready, 2)
            norm(0)
            pe.wait_ge(cond_ready, 1)

            def ada_units(i):
                for j in range(8):
                    pe.wait_ge(ada_landed[j], i * 16 + 16)
                    for k in range(KD):
                        o = ps[:, 7, 8 * i + j:8 * i + j + 1] if isinstance(i, int) else ps[:, 7, bass.ds(i * 8 + j, 1)]
                        mm = pe.matmul(o, adaw[:, j, k * P:k * P + P], vec[:, V_C + k:V_C + k + 1], start=k == 0,
                                       stop=k == KD - 1)
                    mm.then_inc(ada_used, 1)

            ada_units(0)
            with pe.Fori(1, 9) as i:
                ada_units(i)
            pe.wait_ge(mod_ready, 1)
            projection("ret", 0)
            retention()
            pe.wait_ge(rt_done, 4)
            projection("nsa", 0)
            compress()
            pe.wait_ge(cm_done, 2)
            pe.wait_ge(pj_dve, PEND["nsa"])
            attention("nsa")
            pe.wait_ge(at_done["nsa"], 4)
            mix(0, "mix1", O1)
            down("out1", mixhi, mixlo, mx_ready, 0,
                 lambda m: pe.wait_ge((mx_sig, mx_m)[m // 2 % 2], 12 + 2 * (m // 4) + m % 2 + 1))
            norm(1)
            up(0)
            down("down0", hidhi, hidlo, up_ready, 0, lambda m: pe.wait_ge(up_relu, 12 + m + 1) if m < 4 else None)
            up(1)
            down("down1", hidhi, hidlo, up_ready, 16,
                 lambda m: pe.wait_ge(up_relu, 28 + m + 1) if m < 4 else pe.wait_ge(x_ready, 16 + m + 1))
            norm(2)
            norm(3)
            ffn(0, 2)
            norm(4)
            projection("fox", 3)
            forget()
            attention("fox")
            pe.wait_ge(at_done["fox"], 4)
            projection("dsa", 3)
            index_scores()
            pe.wait_ge(ix_relu, 24)
            attention("dsa")
            pe.wait_ge(at_done["dsa"], 4)
            mix(1, "mix2", O2)
            down("out2", mixhi, mixlo, mx_ready, 8,
                 lambda m: pe.wait_ge((mx_sig, mx_m)[m // 2 % 2], 28 + 2 * (m // 4) + m % 2 + 1))
            norm(5)
            ffn(1, 4)
            for t in range(NT):
                for m in range(KD):
                    if t == 0:
                        pe.wait_ge(x_ready, 73 + m)
                    mm = pe.transpose(ps[:, 2 * t + m // 4, (m % 4) * P:(m % 4 + 1) * P], xT[:, m, t * P:t * P + P], ident)
                    if m % 4 == 3:
                        mm.then_inc(y_turned, 1)

        @block.scalar
        def _(sc):
            dn = [0]

            def norm(n):
                for m in range(KD):
                    sc.wait_ge(x_ready, X_BEFORE_NORM[n] + m + 1)
                    if m >= 2:
                        sc.wait_ge(n_sum, 8 * n + m - 1)
                    sc.activation(st[:, m % 2, :], xT[:, m, :], ACT.Square).then_inc(n_sq, 1)
                sc.wait_ge(n_sum, 8 * n + 8)
                sc.activation(rstd[:, :], ps[:, 0, :], ACT.Sqrt, bias=col(C_EPS)).then_inc(n_root, 1)
                if n in H_NORM:
                    h8 = 8 * H_NORM[n]
                    for m in range(KD):
                        sc.wait_ge(n_t, h8 + m + 1)
                        if n in SHIFT:
                            sc.activation(hhi[:, m, :], st[:, 2 + m % 2, :], ACT.Identity,
                                          bias=SHIFT[n][:, m:m + 1]).then_inc(n_hi, 1)
                        else:
                            sc.activation(hhi[:, m, :], st[:, 2 + m % 2, :], ACT.Copy).then_inc(n_hi, 1)

            def projection(name):
                chunks, turns = PLAN[name]
                g, v, x, root, silu, p = G0[name], 0, 0, R0[name], SL0[name], P0[name]
                msq = R0[name]
                for n in range(len(BL[name]) + 2):
                    if n < len(BL[name]):
                        b = BL[name][n]
                        if b[0] == "K":
                            sc.activation(ikrow.rearrange("p t (a d) -> p t a d", a=4),
                                          rowS[:, :, 8:40].unsqueeze(2).broadcast_to([P, NT, 4, 32]), ACT.Copy)
                            for t in range(NT):
                                sc.wait_ge(*OUT_DONE[g])
                                sc.activation(dvrow[:, t, :], ps[:, g % 4, 64:128], ACT.Copy)
                                sc.activation(dkrow[:, t, :].rearrange("p (a d) -> p a d", a=2),
                                              ps[:, g % 4, 0:64].unsqueeze(1).broadcast_to([P, 2, 64]), ACT.Copy)\
                                  .then_inc(pj_ev, 1)
                                g += 1
                        for c in (b[4] if b[0] in "BK" else ()):
                            sc.wait_ge(*OUT_DONE[g])
                            o = ps[:, g % 4, :]
                            if c[0] == "copy":
                                sc.activation(BUF[c[1]][:, c[2], :], o, ACT.Copy).then_inc(pj_ev, 1)
                            elif c[0] == "silu":
                                if silu - 2 >= SL0[name]:
                                    sc.wait_ge(pj_silu, silu - 1)
                                sc.activation(Pb[:, silu % 2, :], o, ACT.Copy)
                                sc.activation(PT[:, silu % 2, :], o, ACT.Sigmoid).then_inc(pj_ev, 1)
                                silu += 1
                            else:
                                if v >= 4:
                                    sc.wait_ge(pj_dve, last_event[name, v - 4] + 1)
                                scale = c[5] if c[0] == "rope" else 1.0
                                a = sc.activation(st[:, v % 4, :], o, ACT.Copy, scale=scale)
                                if c[0] != "rope":
                                    if msq - 4 >= R0[name]:
                                        sc.wait_ge(pj_dve, MS_EVENT[msq - 4] + 1)
                                    a = sc.activation(SQ[msq % 4], o, ACT.Square)
                                    msq += 1
                                a.then_inc(pj_ev, 1)
                                v += 1
                            g += 1
                        if b[0] in "AG":
                            for t in range(NT):
                                sc.wait_ge(*OUT_DONE[g])
                                if b[0] == "A":
                                    sc.activation(BUF[b[3][0]][:, t, b[3][1]:b[3][1] + 256], ps[:, g % 4, 0:256], ACT.Copy)\
                                      .then_inc(pj_ev, 1)
                                elif b[2] == "gates":
                                    sc.activation(gates[:, t, :], ps[:, g % 4, 0:24], ACT.Sigmoid).then_inc(pj_ev, 1)
                                else:
                                    sc.activation(rowS[:, t, :], ps[:, g % 4, 0:48], ACT.Copy).then_inc(pj_ev, 1)
                                g += 1
                    for kind, _ in turns[n]:
                        if kind == "ms":
                            sc.wait_ge(pj_post, p + 1)
                            sc.activation(SQ[root % 4], ps[:, 4 + p % 4, :], ACT.Sqrt, bias=col(C_EPS)).then_inc(pj_root, 1)
                            root += 1
                        p += 1

            def retention():
                for h in range(4):
                    sc.wait_ge(rt_pv, 4 * h + 4)
                    if h >= 2:
                        sc.wait_ge(rt_done, h - 1)
                    sc.activation(st[:, h % 2, :], ps[:, 3 + h % 2, :], ACT.Copy)
                    sc.activation(PT[:, h % 2, :], ps[:, 3 + h % 2, :], ACT.Square).then_inc(rt_ev, 1)
                    sc.wait_ge(rt_sum, h + 1)
                    sc.activation(PT[:, h % 2, :], ps[:, 5 + h % 2, :], ACT.Sqrt, bias=col(C_EPS)).then_inc(rt_root, 1)
                    sc.wait_ge(rt_o, h + 1)
                    sc.activation(O1["b"][0][:, h, :], st[:, h % 2, :], ACT.Copy).then_inc(rt_hi, 1)

            def shift_dmas(kv):
                for g in range(2):
                    src = kvT[64 * g:64 * g + 64, kv, :]
                    sc.dma_start(kshift[0:64, g, :], src).then_inc(cm_shift, 16)
                    sc.dma_start(kshift[64:128, g, 0:S - 1], src[:, 1:S]).then_inc(cm_shift, 16)

            def attention(ph):
                steps = STEPS[ph]
                ohi = OUT[ph][0]

                def outputs(c):
                    sc.wait_ge(at_pv[ph], CHUNK_END[ph][c] + 1)
                    sc.activation(ohi[:, c, :], ps[:, 5 + c % 2, :], ACT.Copy).then_inc(at_hi[ph], 1)

                def copy_turned(s):
                    sc.wait_ge(at_tr[ph], s + 1)
                    if s >= 2:
                        sc.wait_ge(at_pv[ph], s - 1)
                    t = steps[s]
                    nk, w = min(P, t["n"]), len(t["v"]) * P
                    sc.activation(PT[0:nk, s % 2, 0:w], ps[0:nk, 3 + s % 2, 0:w], ACT.Copy).then_inc(at_pt[ph], 1)

                for s, t in enumerate(steps):
                    if t["mask"] == "fox" and t["i"] == 0:
                        h = t["head"]
                        sc.wait_ge(fk_mm, h + 1)
                        if h >= 2:
                            sc.wait_ge(at_max[ph], s - NT)
                        sc.activation(fkb[:, h % 2, :], ps[:, 7, :], ACT.Copy).then_inc(fk_ready, 1)
                    sc.wait_ge(at_max[ph], s + 1)
                    if s >= 2:
                        sc.wait_ge(at_tr[ph], s - 1)
                    src = Sp[:, s % 2, 0:t["n"]] if t["mask"] in ("fox", "dsa") else ps[:, s % 3, 0:t["n"]]
                    sc.activation(Pb[:, s % 2, 0:t["n"]], src, ACT.Exp, bias=stat[:, s % 4, 0:1],
                                  accum_out=stat[:, s % 4, 1:2]).then_inc(at_exp[ph], 1)
                    if s >= 1:
                        copy_turned(s - 1)
                    for c in range(4):
                        if s == CHUNK_END[ph][c] + AFTER:
                            outputs(c)
                copy_turned(len(steps) - 1)
                outputs(3)

            def forget():
                z, e = tmp[0:8, 0, :], tmp[0:8, 1, :]
                sc.wait_ge(f_turn, 1)
                sc.activation(z, ps[0:8, 7, :], ACT.Identity, bias=foxb[:, 0:1]).then_inc(f_z, 1)
                sc.wait_ge(f_e, 1)
                sc.activation(e, e, ACT.Exp, scale=-1.0).then_inc(f_l, 1)
                sc.wait_ge(f_e, 2)
                sc.activation(e, e, ACT.Ln).then_inc(f_l, 1)
                sc.wait_ge(f_back, 1)
                sc.activation(Fq[:, :, :], ps[:, 6, 0:32].rearrange("p (t h) -> p t h", t=NT), ACT.Copy).then_inc(f_ready, 1)

            def index_scores():
                x = 0
                for i in range(1, NT):
                    for h in range(8):
                        sc.wait_ge(ix_mm, x + 1)
                        if x >= 2:
                            sc.wait_ge(ix_acc, x - 1)
                        sc.activation(st[:, x % 2, 0:(i + 1) * P], ps[:, x % 4, 0:(i + 1) * P], ACT.Relu, scale=32 ** -0.5)\
                          .then_inc(ix_relu, 1)
                        x += 1

            def mix(b):
                for n in range(4):
                    for br in range(2):
                        for c in range(2):
                            x = 16 * b + 4 * n + 2 * br + c
                            sc.wait_ge(*gate_done(b, n, br, c))
                            if n >= 1:
                                sc.wait_ge(mx_m, x - 3)
                            sc.activation(st[:, 2 * br + c, :], ps[:, 4 * br + c, :], ACT.Sigmoid).then_inc(mx_sig, 1)
                    for c in range(2):
                        x = 8 * b + 2 * n + c
                        sc.wait_ge(mx_t, x + 1)
                        sc.activation(mixhi[:, 2 * n + c, :], tmp[:, c, :], ACT.Copy).then_inc(mx_hi, 1)

            def up(h):
                u0 = 16 * h

                def chunks(i):
                    for c in range(4):
                        at = lambda k: i * 4 + (u0 + c + k)
                        if c % 2 == 0:
                            sc.wait_ge(up_mm, i * 2 + (8 * h + c // 2 + 1))
                        else:
                            sc.wait_ge(w_used, i * 4 + (AT[f"up{h}"] + c + 1))
                        sc.activation(st[:, c, :], ps[:, c, :], ACT.Relu).then_inc(up_relu, 1)
                        sc.wait_ge(up_t, at(1))
                        o = hidhi[:, c, :] if isinstance(i, int) else hidhi[:, bass.ds(i * 4 + c, 1), :].rearrange(
                            "p k n -> p (k n)")
                        sc.activation(o, tmp[:, c, :], ACT.Copy).then_inc(up_hi, 1)
                chunks(0)
                with sc.Fori(1, 4) as i:
                    chunks(i)

            def ffn_up(f, h):
                u0 = 22 * f + 12 * h

                def chunks(i):
                    at = lambda c, k: i * 2 + (u0 + c + k)
                    for c in range(2):
                        if c == 0:
                            sc.wait_ge(ff_g, i + (11 * f + 6 * h + 1))
                        else:
                            sc.wait_ge(w_used, i * 4 + (AT[f"f{f + 1}up{h}"] + 2))
                        sc.activation(st[:, c, :], ps[:, c, :], ACT.Sigmoid).then_inc(ff_sig, 1)
                    for c in range(2):
                        sc.wait_ge(ff_m2, at(c, 1))
                        o = hidhi[:, c, :] if isinstance(i, int) else hidhi[:, bass.ds(i * 2 + c, 1), :].rearrange(
                            "p k n -> p (k n)")
                        sc.activation(o, tmp[:, 2 + c, :], ACT.Copy).then_inc(ff_hi, 1)
                chunks(0)
                with sc.Fori(1, 6 - h) as i:
                    chunks(i)

            def small_weights(count, parts):
                for lo, src in parts:
                    sc.dma_start(wsm[:, :, lo:lo + src.shape[2]], src).then_inc(ld_wsm, 16)

            sc.dma_start(cst[:, :], T["consts"]).then_inc(ld_cst, 16)
            sc.dma_start(xrow[:, :, :], T["x"][0].rearrange("(t p) d -> p t d", p=P)).then_inc(ld_x, 16)
            vectors = [(V_MIX, T["norm_mix"][0]), (V_MLP, T["norm_mlp"][0]), (V_FINAL, T["norm_final"]),
                       (V_G2, T["norm_g_2"][0].rearrange("s d -> (s d)")), (V_C, T["c_2"][0]), (V_ADAB, T["ada_b_2"][0])]
            for at, v in vectors:
                n = v.shape[0] // P
                sc.dma_start(rows[at:at + n, 0:P], v.rearrange("(r p) -> r p", p=P)).then_inc(ld_rows, 16)
            for at, v in ((V2_PEK, T["cmp_pos_k"][0]), (V2_PEV, T["cmp_pos_v"][0])):
                sc.dma_start(rows[at:at + CMP_S, P:2 * P], v.rearrange("(s l) d -> s (l d)", l=2)).then_inc(ld_rows, 16)
            for at, v in ((V2_FQ, T["fox_qk_g_2"][0]), (V2_DQ, T["dsa_qk_g_2"][0])):
                for half in range(2):
                    sc.dma_start(rows[at:at + 2, P + 64 * half:P + 64 * half + 64], v).then_inc(ld_rows, 16)
            sc.dma_start(foxb[:, :], T["fox_f_bias_2"][0].rearrange("(h a) -> h a", a=1)).then_inc(ld_rows, 16)
            sc.dma_start(posi[:, :], T["positions"].broadcast_to([P, S])).then_inc(ld_pos, 16)
            sc.dma_start(dmat[:, :, :], T["decay"].rearrange("p (h n) -> p h n", h=4)).then_inc(ld_dmat, 16)
            win = T["w_in"][0].rearrange("(k p) n -> p k n", p=P)
            with nc.allow_non_contiguous_dma(reason="24 gate columns"):
                small_weights(1, [(0, win[:, :, W1["gates"]:W1["gates"] + 24])])
            for kv, n in enumerate(("cmp_k_w2", "cmp_v_w2")):
                sc.dma_start(cmpw2[:, kv, :, :], T[n][0].rearrange("(c p) n -> p c n", p=P)).then_inc(ld_w2, 16)
            sc.wait_ge(vec_turned, 1)
            sc.activation(vec[:, :], ps[:, 0, 0:P], ACT.Copy).then_inc(vec_ready, 1)
            sc.wait_ge(vec_turned, 2)
            sc.activation(vec2[:, :], ps[:, 1, 0:V2_N], ACT.Copy).then_inc(vec_ready, 1)
            norm(0)
            sc.wait_ge(vec_ready, 2)
            sc.activation(geff[:, 0:8], vec[:, V_C:V_C + 8], ACT.Sigmoid).then_inc(cond_sig, 1)

            def sines(table):
                for f in range(2):
                    sc.wait_ge(trig_arg, 4 * table[1] + 2 * table[0] + f + 1)
                    sc.activation(trig[:, table[0], f, :], trig[:, table[0], f, :], ACT.Sin).then_inc(trig_ready, 1)

            for tb in range(2):
                sines((tb, 0))
            projection("ret")
            retention()
            projection("nsa")
            sc.wait_ge(pj_dve, PEND["nsa"])
            sc.wait_ge(pj_ev, GEND["nsa"])
            shift_dmas(0)
            for kv in range(2):
                for hc in range(2):
                    sc.wait_ge(*((cm_mm, kv + 1) if hc == 0 else (w_used, AT[("cmpk", "cmpv")[kv]] + 4)))
                    if kv == 1 and hc == 0:
                        sc.wait_ge(cm_hid, 2)
                    sc.activation(sigc[:, hc, 0:62], ps[:, hc, 0:62], ACT.Sigmoid).then_inc(cm_sig, 1)
                if kv == 0:
                    sc.wait_ge(cm_blk, 1)
                    shift_dmas(1)
            attention("nsa")
            sc.dma_start(posi[:, :], T["positions_2"].broadcast_to([P, S])).then_inc(ld_pos, 16)
            sc.wait_ge(wsm_ready, 1)
            win2 = T["w_in_2"][0].rearrange("(k p) n -> p k n", p=P)
            sc.wait_ge(pj_ev, GEND["nsa"])
            with nc.allow_non_contiguous_dma(reason="48 narrow columns"):
                small_weights(2, [(0, win2[:, :, W2["ff"]:W2["ff"] + 8]), (8, win2[:, :, W2["ik"]:W2["ik"] + 40])])
            mix(0)
            norm(1)
            up(0)
            for tb in range(2):
                sines((tb, 1))
            up(1)
            norm(2)
            norm(3)
            for h in range(2):
                ffn_up(0, h)
            norm(4)
            projection("fox")
            forget()
            attention("fox")
            projection("dsa")
            index_scores()
            attention("dsa")
            mix(1)
            norm(5)
            for h in range(2):
                ffn_up(1, h)
            for t in range(NT):
                for b in range(2):
                    sc.wait_ge(y_turned, 2 * t + b + 1)
                    sc.activation(xrow[:, t, 512 * b:512 * b + 512], ps[:, 2 * t + b, :], ACT.Copy).then_inc(y_ready, 1)

        @block.vector
        def _(v_):
            ve = v_
            chain = [0]

            def link(ins):
                chain[0] += 1
                ins.then_inc(dve, 1)
                ve.wait_ge(dve, chain[0])

            def norm(n):
                ve.wait_ge(n_root, n + 1)
                link(ve.reciprocal(rstd[:, :], rstd[:, :]))
                if n not in H_NORM:
                    for m in range(KD):
                        ve.scalar_tensor_tensor(out=xT[:, m, :], in0=xT[:, m, :], scalar=GAIN[n][:, m:m + 1],
                                                in1=rstd[:, :], op0=ALU.mult, op1=ALU.mult).then_inc(x_ready, 1)
                    return
                h8 = 8 * H_NORM[n]

                def low(m):
                    ve.wait_ge(n_hi, h8 + m + 1)
                    hi_ = hhi[:, m, :].bitcast(F32)
                    if n in SHIFT:
                        i_ = ve.scalar_tensor_tensor(out=hlo[:, m, :], in0=st[:, 2 + m % 2, :], scalar=SHIFT[n][:, m:m + 1],
                                                     in1=hi_, op0=ALU.add, op1=ALU.subtract)
                    else:
                        i_ = ve.tensor_tensor(hlo[:, m, :], st[:, 2 + m % 2, :], hi_, ALU.subtract)
                    i_.then_inc(h_ready, 1)

                for m in range(KD):
                    if m >= 2:
                        ve.wait_ge(h_ready, h8 + m - 1)
                    ve.scalar_tensor_tensor(out=st[:, 2 + m % 2, :], in0=xT[:, m, :], scalar=GAIN[n][:, m:m + 1],
                                            in1=rstd[:, :], op0=ALU.mult, op1=ALU.mult).then_inc(n_t, 1)
                    if m >= 1:
                        low(m - 1)
                low(KD - 1)

            def trig_tables(b):
                ve.wait_ge(ld_pos, 16 * (b + 1))
                if b == 1:
                    ve.wait_ge(up_ready, 16)
                link(ve.tensor_copy(posf, posi[:, :]))
                c1, c2 = 6.28125, 1.934051513671875e-03
                c3 = 2 * math.pi - c1 - c2
                ang, k = tmp[:, 0, :], tmp[:, 1, :]
                for tb in range(2):
                    link(ve.tensor_scalar(ang, posf, col(C_INV + 2 * b + tb), None, ALU.mult))
                    for f in range(2):
                        r = trig[:, tb, f, :]
                        link(ve.tensor_scalar(k, ang, 1 / (2 * math.pi), 0.25 if f == 0 else 0.0, ALU.mult, ALU.add))
                        link(ve.tensor_scalar(k, k, MAGIC, MAGIC, ALU.add, ALU.subtract))
                        link(ve.scalar_tensor_tensor(out=r, in0=k, scalar=-c1, in1=ang, op0=ALU.mult, op1=ALU.add))
                        link(ve.scalar_tensor_tensor(out=r, in0=k, scalar=-c2, in1=r, op0=ALU.mult, op1=ALU.add))
                        link(ve.scalar_tensor_tensor(out=r, in0=k, scalar=-c3, in1=r, op0=ALU.mult, op1=ALU.add))
                        link(ve.tensor_scalar(r, r, math.pi / 2 if f == 0 else 0.0, 3.1415925, ALU.add, ALU.min))
                        ve.tensor_scalar(r, r, -3.1415925, None, ALU.max).then_inc(trig_arg, 1)

            def projection(name, table_base):
                chunks, turns = PLAN[name]
                p, root, silu = P0[name], R0[name], SL0[name]
                g = G0[name]
                first_perm = [True]
                for n in range(len(BL[name]) + 2):
                    if n < len(BL[name]):
                        b = BL[name][n]
                        if b[0] == "B":
                            for c in range(2):
                                if b[4][c][0] == "silu":
                                    ve.wait_ge(pj_ev, g + c + 1)
                                    ve.tensor_tensor(srg[:, b[4][c][2], :], Pb[:, silu % 2, :], PT[:, silu % 2, :],
                                                     ALU.mult).then_inc(pj_silu, 1)
                                    silu += 1
                        g += n_out[b[0]]
                    for kind, v in turns[n]:
                        c = chunks[v]
                        if kind == "ms":
                            r = SQ[root % 4]
                            ve.wait_ge(pj_root, root + 1)
                            link(ve.reciprocal(r, r))
                            dst = BUF[c[1]][:, c[2], :] if c[0] == "norm" else st[:, v % 4, :]
                            gc = QKG[c[3]]
                            ve.scalar_tensor_tensor(out=dst, in0=st[:, v % 4, :], scalar=vec2[:, gc:gc + 1], in1=r,
                                                    op0=ALU.mult, op1=ALU.mult).then_inc(pj_dve, 1)
                            root += 1
                        else:
                            if first_perm[0]:
                                ve.wait_ge(trig_ready, table_base + 4)
                                first_perm[0] = False
                            tb = c[3] if c[0] == "rope" else c[4]
                            ve.wait_ge(pj_post, p + 1)
                            if p >= 1:
                                ve.wait_ge(pj_dve, p)
                            link(ve.tensor_tensor(tmp[:, 0, :], st[:, v % 4, :], trig[:, tb, 0, :], ALU.mult))
                            link(ve.tensor_tensor(tmp[:, 1, :], ps[:, 4 + p % 4, :], trig[:, tb, 1, :], ALU.mult))
                            ve.tensor_tensor(BUF[c[1]][:, c[2], :], tmp[:, 0, :], tmp[:, 1, :], ALU.add)\
                              .then_inc(pj_dve, 1)
                        p += 1

            def retention():
                def finish(h):
                    ve.wait_ge(rt_root, h + 1)
                    r, o = PT[:, h % 2, :], st[:, h % 2, :]
                    link(ve.reciprocal(r, r))
                    link(ve.tensor_tensor(o, o, r, ALU.mult))
                    ve.tensor_tensor(o, o, srg[:, h, :], ALU.mult).then_inc(rt_o, 1)
                    ve.wait_ge(rt_hi, h + 1)
                    ve.tensor_tensor(O1["b"][1][:, h, :], o, O1["b"][0][:, h, :].bitcast(F32), ALU.subtract)\
                      .then_inc(rt_done, 1)

                ve.wait_ge(pj_silu, 4)
                ve.wait_ge(ld_dmat, 16)
                x = 0
                for h in range(4):
                    for j in range(NT):
                        n = S - j * P
                        ve.wait_ge(rt_qk, x + 1)
                        if x >= 2:
                            ve.wait_ge(rt_pv, x - 1)
                        ve.tensor_tensor(Pb[:, x % 2, 0:n], ps[:, x % 3, 0:n], dmat[:, h, 0:n], ALU.mult).then_inc(rt_sd, 1)
                        if j == 2 and h >= 1:
                            finish(h - 1)
                        x += 1
                finish(3)

            def compress():
                for kv in range(2):
                    ve.wait_ge(cm_shift, 64 * (kv + 1))
                    if kv == 1:
                        ve.wait_ge(w_used, AT["cmpk"] + 4)
                    pe_col = V2_PEK if kv == 0 else V2_PEV
                    for g in range(2):
                        v = kshift[:, g, :].rearrange("p (c t) -> p t c", t=16)
                        for a in range(2):
                            last = ve.tensor_tensor(
                                blkf[:, 8 * a:8 * a + 8, N_CMP * g:N_CMP * (g + 1)], v[:, 0:16:2, a:a + N_CMP],
                                vec2[:, pe_col + 8 * a:pe_col + 8 * a + 8].unsqueeze(2).broadcast_to([P, 8, N_CMP]), ALU.add)
                    link(last)
                    link(ve.tensor_copy(blkhi[:, :, :], blkf[:, :, :]))
                    ve.tensor_tensor(blklo[:, :, :], blkf[:, :, :], blkhi[:, :, :].bitcast(F32), ALU.subtract)\
                      .then_inc(cm_blk, 1)
                    for hc in range(2):
                        ve.wait_ge(cm_sig, 2 * kv + hc + 1)
                        if kv == 1 and hc == 0:
                            ve.wait_ge(cm_out, 1)
                        ve.tensor_tensor(hidc[:, hc, 0:62], ps[:, hc, 0:62], sigc[:, hc, 0:62], ALU.mult).then_inc(cm_hid, 1)
                    ve.wait_ge(cm_out, kv + 1)
                    if kv == 0:
                        ve.tensor_copy(kcmpT[:, 0:N_CMP], ps[:, 2, 0:N_CMP]).then_inc(cm_done, 1)
                    else:
                        ve.tensor_copy(vcmp[0:N_CMP, :], ps[0:N_CMP, 3, 0:P]).then_inc(cm_done, 1)

            def attention(ph):
                steps = STEPS[ph]
                ohi, olo = OUT[ph]

                def scores(s):
                    t = steps[s]
                    n, i = t["n"], t["i"]
                    sp_, o, dg = Sp[:, s % 2, 0:n], ps[:, s % 3, 0:n], slice(i * P, i * P + P)
                    ve.wait_ge(at_qk[ph], s + 1)
                    if t["mask"] in ("fox", "dsa") and s >= 2:
                        ve.wait_ge(at_exp[ph], s - 1)
                    if s >= 4:
                        ve.wait_ge(at_exp[ph], s - 3)
                    if t["mask"] == "causal":
                        link(ve.tensor_tensor(ps[:, s % 3, dg], ps[:, s % 3, dg], cst[:, C_CAUSAL:C_CAUSAL + P], ALU.add))
                    elif t["mask"] == "cmp":
                        link(ve.tensor_tensor(o, o, cst[:, C_CMP + 32 * i:C_CMP + 32 * i + n], ALU.add))
                    elif t["mask"] == "fox":
                        h = t["head"]
                        if i == 0:
                            ve.wait_ge(fk_ready, h + 1)
                        link(ve.scalar_tensor_tensor(out=sp_, in0=o, scalar=Fq[:, i, h:h + 1], in1=fkb[:, h % 2, 0:n],
                                                     op0=ALU.add, op1=ALU.subtract))
                        link(ve.tensor_tensor(Sp[:, s % 2, dg], Sp[:, s % 2, dg], cst[:, C_CAUSAL:C_CAUSAL + P], ALU.add))
                    else:
                        link(ve.tensor_tensor(sp_, o, sel[:, i, 0:n], ALU.add))
                    ve.tensor_reduce(stat[:, s % 4, 0:1], sp_ if t["mask"] in ("fox", "dsa") else o, AX, ALU.max,
                                     negate=True).then_inc(at_max[ph], 1)

                def normalise(s):
                    t = steps[s]
                    r = stat[:, s % 4, 2:3]
                    ve.wait_ge(at_exp[ph], s + 1)
                    link(ve.reciprocal(r, stat[:, s % 4, 1:2]))
                    if t["av"] is not None and t["i"] == 0:
                        link(ve.tensor_tensor(r, r, t["av"], ALU.mult))
                    pb = Pb[:, s % 2, 0:t["n"]]
                    if t["gate"] is not None:
                        ve.tensor_scalar(pb, pb, r, t["gate"], ALU.mult, ALU.mult).then_inc(at_nrm[ph], 1)
                    else:
                        ve.tensor_scalar(pb, pb, r, None, ALU.mult).then_inc(at_nrm[ph], 1)

                def outputs(c):
                    ve.wait_ge(at_hi[ph], c + 1)
                    ve.tensor_tensor(olo[:, c, :], ps[:, 5 + c % 2, :], ohi[:, c, :].bitcast(F32), ALU.subtract)\
                      .then_inc(at_done[ph], 1)

                for s in range(len(steps)):
                    scores(s)
                    if s >= 1:
                        normalise(s - 1)
                    for c in range(4):
                        if s == CHUNK_END[ph][c] + AFTER + 1:
                            outputs(c)
                normalise(len(steps) - 1)
                outputs(3)

            def forget():
                z, e, mn = tmp[0:8, 0, :], tmp[0:8, 1, :], tmp[0:8, 2, :]
                ve.wait_ge(f_z, 1)
                ve.scalar_tensor_tensor(out=e, in0=z, scalar=-1.0, in1=z, op0=ALU.mult, op1=ALU.max).then_inc(f_e, 1)
                ve.tensor_scalar(mn, z, 0.0, None, ALU.min)
                ve.wait_ge(f_l, 1)
                ve.tensor_scalar(e, e, 1.0, None, ALU.add).then_inc(f_e, 1)
                ve.wait_ge(f_l, 2)
                ve.tensor_tensor_scan(FT[:, :], mn, e, 0.0, ALU.add, ALU.subtract).then_inc(f_scan, 1)

            def index_scores():
                ve.tensor_copy(sel[:, 0, 0:P], cst[:, C_ADM:C_ADM + P])
                ve.wait_ge(pj_ev, GEND["dsa"])
                link(ve.tensor_scalar(rowS[:, :, 40:48], rowS[:, :, 40:48], 8 ** -0.5, None, ALU.mult))
                x = 0
                for i in range(1, NT):
                    n = (i + 1) * P
                    w = score[:, i % 2, 0:n]
                    for h in range(8):
                        r = st[:, x % 2, 0:n]
                        iw = rowS[:, i, 40 + h:41 + h]
                        ve.wait_ge(ix_relu, x + 1)
                        if h == 0:
                            a = ve.tensor_scalar(w, r, iw, None, ALU.mult)
                        else:
                            ve.wait_ge(ix_acc, x)
                            a = ve.scalar_tensor_tensor(out=w, in0=r, scalar=iw, in1=w, op0=ALU.mult, op1=ALU.add)
                        a.then_inc(ix_acc, 1)
                        x += 1
                    ve.wait_ge(ix_acc, x)
                    dg = score[:, i % 2, i * P:(i + 1) * P]
                    link(ve.tensor_tensor(dg, dg, cst[:, C_ADM:C_ADM + P], ALU.add))
                    for _ in range(TOPK // 8):
                        link(ve.max(top8[:, :], w))
                        link(ve.match_replace(w, top8[:, :], w, TAKEN))
                    link(ve.tensor_scalar(sel[:, i, 0:n], w, (NEG + TAKEN) / 2, NEG, ALU.is_gt, ALU.mult))

            def mix(b):
                for n in range(4):
                    if n >= 1:
                        ve.wait_ge(mx_ready, 8 * b + 2 * n)
                    for br in range(2):
                        for c in range(2):
                            x = 16 * b + 4 * n + 2 * br + c
                            ve.wait_ge(mx_sig, x + 1)
                            ve.wait_ge(*branch_done(b, n, br, c))
                            ve.tensor_tensor(tmp[:, 2 * br + c, :], ps[:, 4 * br + 2 + c, :], st[:, 2 * br + c, :], ALU.mult)\
                              .then_inc(mx_m, 1)
                    for c in range(2):
                        ve.wait_ge(mx_m, 16 * b + 4 * n + 2 + c + 1)
                        ve.tensor_tensor(tmp[:, c, :], tmp[:, c, :], tmp[:, 2 + c, :], ALU.add).then_inc(mx_t, 1)
                    for c in range(2):
                        ve.wait_ge(mx_hi, 8 * b + 2 * n + c + 1)
                        ve.tensor_tensor(mixlo[:, 2 * n + c, :], tmp[:, c, :], mixhi[:, 2 * n + c, :].bitcast(F32),
                                         ALU.subtract).then_inc(mx_ready, 1)

            def down(name, scale=None):
                for m in range(KD):
                    ve.wait_ge(*DOWN_DONE[name, m])
                    if scale is None:
                        ve.tensor_tensor(xT[:, m, :], xT[:, m, :], ps[:, m, :], ALU.add).then_inc(x_ready, 1)
                    else:
                        ve.scalar_tensor_tensor(out=xT[:, m, :], in0=ps[:, m, :], scalar=scale[:, m:m + 1], in1=xT[:, m, :],
                                                op0=ALU.mult, op1=ALU.add).then_inc(x_ready, 1)

            def up(h):
                def chunks(i):
                    for c in range(4):
                        at = i * 4 + (16 * h + c + 1)
                        ve.wait_ge(up_relu, at)
                        if not isinstance(i, int):
                            ve.wait_ge(up_ready, i * 4 + (16 * h + c - 3))
                        ve.tensor_tensor(tmp[:, c, :], st[:, c, :], st[:, c, :], ALU.mult).then_inc(up_t, 1)
                        ve.wait_ge(up_hi, at)
                        pick = lambda t: t[:, c, :] if isinstance(i, int) else t[:, bass.ds(i * 4 + c, 1), :].rearrange(
                            "p k n -> p (k n)")
                        ve.tensor_tensor(pick(hidlo), tmp[:, c, :], pick(hidhi).bitcast(F32), ALU.subtract)\
                          .then_inc(up_ready, 1)
                chunks(0)
                with ve.Fori(1, 4) as i:
                    chunks(i)

            def ffn_up(f, h):
                u0 = 22 * f + 12 * h

                def chunks(i):
                    at = lambda c: i * 2 + (u0 + c + 1)
                    for c in range(2):
                        ve.wait_ge(ff_sig, at(c))
                        ve.tensor_tensor(tmp[:, c, :], ps[:, c, :], st[:, c, :], ALU.mult).then_inc(ff_m1, 1)
                    for c in range(2):
                        if c == 0:
                            ve.wait_ge(ff_u, i + (11 * f + 6 * h + 1))
                        else:
                            ve.wait_ge(w_used, i * 4 + (AT[f"f{f + 1}up{h}"] + 4))
                        ve.wait_ge(ff_m1, at(c))
                        if not isinstance(i, int):
                            ve.wait_ge(ff_ready, i * 2 + (u0 + c - 1))
                        ve.tensor_tensor(tmp[:, 2 + c, :], ps[:, 2 + c, :], tmp[:, c, :], ALU.mult).then_inc(ff_m2, 1)
                    for c in range(2):
                        ve.wait_ge(ff_hi, at(c))
                        pick = lambda t: t[:, c, :] if isinstance(i, int) else t[:, bass.ds(i * 2 + c, 1), :].rearrange(
                            "p k n -> p (k n)")
                        ve.tensor_tensor(pick(hidlo), tmp[:, 2 + c, :], pick(hidhi).bitcast(F32), ALU.subtract)\
                          .then_inc(ff_ready, 1)
                chunks(0)
                with ve.Fori(1, 6 - h) as i:
                    chunks(i)

            def ffn(f, scale):
                for h in range(2):
                    ffn_up(f, h)
                    down(f"f{f + 1}down{h}", scale)

            def split_small(b):
                ve.wait_ge(ld_wsm, 16 if b == 0 else 48)
                n = 24 if b == 0 else 48
                ve.tensor_copy(wsmhi[:, :, 0:n], wsm[:, :, 0:n]).then_inc(wsm_hi, 1)
                ve.wait_ge(wsm_hi, b + 1)
                ve.tensor_tensor(wsmlo[:, :, 0:n], wsm[:, :, 0:n], wsmhi[:, :, 0:n].bitcast(F32), ALU.subtract)\
                  .then_inc(wsm_ready, 1)

            for m in range(KD):
                ve.wait_ge(x_turned, m + 1)
                ve.tensor_copy(xT[:, m, :], ps[:, m, :]).then_inc(x_ready, 1)
            ve.wait_ge(vec_ready, 2)
            for c in (V2_FQ, V2_DQ):
                link(ve.tensor_scalar(vec2[:, c:c + 1], vec2[:, c:c + 1], 0.125, None, ALU.mult))
            norm(0)
            ve.wait_ge(cond_sig, 1)
            ve.tensor_tensor(vec[:, V_C:V_C + 8], vec[:, V_C:V_C + 8], geff[:, 0:8], ALU.mult).then_inc(cond_ready, 1)
            trig_tables(0)
            split_small(0)
            ve.wait_ge(ada_used, 72)
            link(ve.tensor_tensor(mod[:, :], ps[:, 7, 0:72], vec[:, V_ADAB:V_ADAB + 72], ALU.add))
            for j in range(3):
                link(ve.scalar_tensor_tensor(out=geff[:, 8 * j:8 * j + 8], in0=mod[:, 24 * j + 8:24 * j + 16], scalar=1.0,
                                             in1=vec[:, V_G2 + 8 * j:V_G2 + 8 * j + 8], op0=ALU.add, op1=ALU.mult))
                if j != 1:
                    link(ve.tensor_scalar(mod[:, 24 * j + 16:24 * j + 24], mod[:, 24 * j + 16:24 * j + 24], 0.5, None,
                                          ALU.mult))
            ve.tensor_copy(stat[:, 0, 3:4], mod[:, 0:1]).then_inc(mod_ready, 1)
            projection("ret", 0)
            retention()
            projection("nsa", 0)
            compress()
            attention("nsa")
            mix(0)
            down("out1")
            norm(1)
            up(0)
            trig_tables(1)
            split_small(1)
            down("down0")
            up(1)
            down("down1")
            norm(2)
            norm(3)
            ffn(0, mod[:, 16:24])
            norm(4)
            projection("fox", 4)
            forget()
            attention("fox")
            projection("dsa", 4)
            index_scores()
            attention("dsa")
            mix(1)
            down("out2", mod[:, 40:48])
            norm(5)
            ffn(1, mod[:, 64:72])



def constants():
    c = np.zeros((P, C_END), np.float32)
    r = np.arange(P)
    c[:, C_ID:C_ID + P] = np.eye(P)
    c[:, C_MEAN:C_MEAN + P] = 1.0 / D
    c[:, C_HD128:C_HD128 + P] = 1.0 / 128
    c[:, C_HD64:C_HD64 + P] = (r[:, None] // 64 == r[None, :] // 64) / 64.0
    for at, width, rot in ((C_PN, 64, 16), (C_PR, 128, 128), (C_PI, 32, 8)):
        half = rot // 2
        for m in range(P):
            d = m % width
            if d < half:
                c[m + half, at + m] = -1.0
            elif d < rot:
                c[m - half, at + m] = 1.0
    c[:, C_CAUSAL:C_CAUSAL + P] = np.where(r[None, :] <= r[:, None], 0.0, NEG)
    c[:, C_ADM:C_ADM + P] = np.where(r[None, :] // 64 <= r[:, None] // 64, 0.0, NEG)
    for i in range(NT):
        t = i * P + r
        end = 16 * np.arange(N_CMP) + 31
        c[:, C_CMP + 32 * i:C_CMP + 32 * i + N_CMP] = np.where(end[None, :] <= t[:, None], 0.0, NEG)
        c[:, C_AV + i] = t >= 31
    f32 = np.float32

    def inverse(base, rot):
        return np.exp(f32(-math.log(base)) * np.arange(rot // 2, dtype=f32) * f32(2.0) / f32(rot))

    def inverse2(rot):
        return (500000.0 ** (-np.arange(0, rot, 2, dtype=f32) / f32(rot)).astype(np.float64)).astype(f32)

    for n, (inv, width) in enumerate(((inverse(500000.0, 16), 64), (inverse(10000.0, 128), 128), (inverse2(16), 64),
                                      (inverse2(8), 32))):
        half = len(inv)
        for m in range(P):
            d = m % width
            c[m, C_INV + n] = inv[d % half] if d < 2 * half else 0.0
    c[:, C_EPS] = EPS
    return c


def decay_table():
    g = 1.0 - 2.0 ** (-5.0 - np.arange(4))
    rel = np.arange(S)[None, :] - np.arange(P)[:, None]
    t = np.where(rel[:, None, :] >= 0, g[None, :, None] ** np.maximum(rel, 0)[:, None, :], 0.0)
    return np.ascontiguousarray(t.reshape(P, 4 * S).astype(np.float32))


_NAMES = ["x", "positions", "norm_mix", "w_in", "cmp_pos_k", "cmp_pos_v", "cmp_k_w1", "cmp_k_w2", "cmp_v_w1", "cmp_v_w2",
          "w_proj_a", "w_proj_b", "w_out", "norm_mlp", "w_up", "w_down", "norm_final", "c_2", "positions_2", "ada_w_2",
          "ada_b_2", "norm_g_2", "ffn1_w1_2", "ffn1_w3_2", "ffn1_w2_2", "w_in_2", "fox_f_bias_2", "fox_qk_g_2",
          "dsa_qk_g_2", "w_br_fox_2", "w_br_dsa_2", "w_out_2", "ffn2_w1_2", "ffn2_w3_2", "ffn2_w2_2"]


def kernel(**inputs):
    import concourse.bacc as bacc
    from concourse.bass_utils import run_bass_kernel_spmd

    nc = bacc.Bacc("TRN2", target_bir_lowering=False, num_devices=1)
    arrays = {name: np.ascontiguousarray(inputs[name]) for name in _NAMES}
    arrays["consts"] = constants()
    arrays["decay"] = decay_table()
    tensors = {name: nc.dram_tensor(f"in_{name}", a.shape, mybir.dt.from_np(a.dtype), kind="ExternalInput").ap()
               for name, a in arrays.items()}
    out = nc.dram_tensor("out_y", (1, S, D), F32, kind="ExternalOutput").ap()
    mix_kernel(nc, tensors, out)
    r = run_bass_kernel_spmd(nc, [{f"in_{name}": a for name, a in arrays.items()}], core_ids=[0])
    return r.results[0]["out_y"]
```

```python
import math
from contextlib import ExitStack

import numpy as np
import concourse.bass as bass
from concourse import mybir

F32 = mybir.dt.float32
F32R = mybir.dt.float32r
I32 = mybir.dt.int32
ALU = mybir.AluOpType
ACT = mybir.ActivationFunctionType
AX = mybir.AxisListType.X

P = 128
S = 512
NT = S // P
D = 1024
KD = D // P
SLAB = 1024
SLOTS = 4
ADA_SLOTS = 6
EPS = 1e-6
NEG = -1e30
TAKEN = -2e30
MAGIC = 12582912.0
TOPK = min(256, S // 4)

W1 = dict(q=0, kc=512, vc=640, ks=768, vs=896, kw=1024, vw=1152, gates=1280, rq=1304, rk=1816, rv=2328, rg=2840,
          ga=3352, gb=4376)
W2 = dict(fq=0, fk=512, fv=1024, ff=1536, dq=1544, dk=2056, dv=2120, iq=2184, ik=2440, iw=2472, ga=2480, gb=3504)
N_CMP = (S - 32) // 16 + 1
CMP_S = 16

C_ID, C_MEAN, C_HD128, C_HD64, C_PN, C_PR, C_PI, C_CAUSAL, C_ADM, C_CMP, C_MISC = [i * P for i in range(11)]
C_AV = C_MISC
C_INV = C_MISC + NT
C_EPS = C_INV + 4
C_END = C_EPS + 1

V_MIX, V_MLP, V_FINAL, V_G2, V_C, V_ADAB = 0, 8, 16, 24, 48, 56
V2_PEK, V2_PEV, V2_FQ, V2_FK, V2_DQ, V2_DK, V2_N = 0, 16, 32, 33, 34, 35, 36


def weight_stream():
    at, n = {}, 0
    for name, count in (("nsa", 10), ("rq", 4), ("cmpk", 4), ("rk", 4), ("cmpv", 4), ("rvg", 8), ("mix1", 24), ("out1", 8),
                        ("up0", 16), ("down0", 16), ("up1", 16), ("down1", 16),
                        ("f1up0", 24), ("f1down0", 12), ("f1up1", 20), ("f1down1", 10),
                        ("fox", 8), ("dsa", 11), ("mix2", 24), ("out2", 8),
                        ("f2up0", 24), ("f2down0", 12), ("f2up1", 20), ("f2down1", 10)):
        at[name] = n
        n += count
    return at, n


AT, N_SLABS = weight_stream()


def proj_blocks():
    rope = lambda t, i, trig, perm, scale=1.0: ("rope", t, i, trig, perm, scale)
    nsa = [("B", W1["q"] + 128 * b, 256, True, [rope("qT", 2 * b + c, 0, C_PN, 0.125) for c in range(2)]) for b in range(2)]
    nsa += [("B", W1["kc"], 128, False, [rope("kvT", 0, 0, C_PN), ("copy", "kvT", 1)]),
            ("B", W1["ks"], 256, False, [rope("kvT", 2, 0, C_PN), rope("kvT", 3, 0, C_PN)]),
            ("A", W1["vs"], 256, ("vrow", 0)), ("G", 24, "gates", 1)]
    rq = [("B", W1["rq"] + 256 * b, 128, False, [rope("rqT", 2 * b + c, 1, C_PR) for c in range(2)]) for b in range(2)]
    rk = [("B", W1["rk"] + 256 * b, 128, False,
           [rope("rkT", 2 * b + c, 1, C_PR, 128 ** -0.5) for c in range(2)]) for b in range(2)]
    rvg = [("A", W1["rv"] + 256 * b, 128, ("rv", 256 * b)) for b in range(2)]
    rvg += [("B", W1["rg"] + 256 * b, 128, False, [("silu", "srg", 2 * b + c) for c in range(2)]) for b in range(2)]
    fox = [("B", W2["fq"] + 256 * b, 128, False, [("norm", "fqT", 2 * b + c, 0) for c in range(2)]) for b in range(2)]
    fox += [("B", W2["fk"] + 256 * b, 128, False, [("norm", "fkT", 2 * b + c, 1) for c in range(2)]) for b in range(2)]
    fox += [("G", 48, "rowS", 2)]
    dsa = [("K", W2["dk"], 0, False, [("normrope", "dkT", 0, 3, 0, C_PN), rope("ikT", 0, 1, C_PI)])]
    dsa += [("B", W2["dq"] + 256 * b, 128, False, [("normrope", "dqT", 2 * b + c, 2, 0, C_PN) for c in range(2)])
           for b in range(2)]
    dsa += [("B", W2["iq"], 128, False, [rope("iqT", c, 1, C_PI) for c in range(2)])]
    dsa += [("A", W2["fv"] + 256 * b, 128, ("fv", 256 * b)) for b in range(2)]
    return nsa, rq, rk, rvg, fox, dsa


def plan_projection(blocks):
    chunks, per_block = [], []
    for n, b in enumerate(blocks):
        mine = []
        if b[0] in "BK":
            for c in b[4]:
                if c[0] in ("rope", "norm", "normrope"):
                    mine.append(len(chunks))
                    chunks.append(c)
        per_block.append(mine)
    turns = []
    for n in range(len(blocks) + 2):
        now = []
        if 0 <= n - 2 < len(blocks):
            now += [("perm", v) for v in per_block[n - 2] if chunks[v][0] == "normrope"]
        if 0 <= n - 1 < len(blocks):
            now += [("perm" if chunks[v][0] == "rope" else "ms", v) for v in per_block[n - 1]]
        turns.append(now)
    return chunks, turns


def mix_kernel(nc, T, out):
    with ExitStack() as ctx:
        def sem(name):
            return ctx.enter_context(nc.semaphore(name))

        base = 16512
        used = [base]

        def sb(name, shape, dt=F32, at=None):
            size = int(np.prod(shape[1:])) * 4
            if at is None:
                at = used[0]
                used[0] += (size + 31) // 32 * 32
                assert used[0] <= 229344, used[0]
            return nc.alloc_sbuf_tensor_at(name, list(shape), dt, offset=at)

        KB = 1024
        xT = sb("xT", [P, KD, S])
        hhi = sb("hhi", [P, KD, S], F32R)
        hlo = sb("hlo", [P, KD, S], F32R)
        raw = sb("raw", [P, SLOTS, SLAB])
        whi = sb("whi", [P, SLOTS, SLAB], F32R)
        wlo = sb("wlo", [P, SLOTS, SLAB], F32R)
        R = used[0]
        used[0] += 64 * KB
        hidhi = sb("hidhi", [P, 16, S], F32R, R)
        hidlo = sb("hidlo", [P, 16, S], F32R, R + 32 * KB)
        mixhi = sb("mixhi", [P, KD, S], F32R, R + 32 * KB)
        mixlo = sb("mixlo", [P, KD, S], F32R, R + 48 * KB)
        xrow = sb("xrow", [P, NT, D], F32, R + 32 * KB)
        adaw = sb("adaw", [P, 4, SLAB], F32, R + 44 * KB)
        t4 = lambda name, at, n=4, dt=F32: sb(name, [P, n, S], dt, R + at * KB)
        rqT, rkT, qT, srg, kvT, rv = (t4(n, a) for n, a in (("rqT", 0), ("rkT", 8), ("qT", 16), ("srg", 24),
                                                         ("kvT", 32), ("rv", 44)))
        vrow = sb("vrow", [P, NT, 256], F32, R + 40 * KB)
        dmat = t4("dmat", 52)
        gates = sb("gates", [P, NT, 24], F32, R + 60 * KB)
        kcmpT = sb("kcmpT", [P, 32], F32, R + 61 * KB)
        vcmp = sb("vcmp", [32, P], F32, R + 61 * KB + 128)
        cmpw2 = sb("cmpw2", [P, 2, 2, 64], F32, R + 62 * KB)
        hidc = sb("hidc", [P, 2, 2, 64], F32, R + 63 * KB)
        kshift = sb("kshift", [P, 2, S], F32, R + 24 * KB)
        blkhi = sb("blkhi", [P, CMP_S, 62], F32R, R + 52 * KB)
        blklo = sb("blklo", [P, CMP_S, 62], F32R, R + 56 * KB)
        O1 = {"a": (t4("nsahi", 16, 4, F32R), t4("nsalo", 24, 4, F32R)),
              "b": (t4("rethi", 0, 4, F32R), t4("retlo", 8, 4, F32R))}
        fqT, fkT, dqT, fv = (t4(n, a) for n, a in (("fqT", 0), ("fkT", 8), ("dqT", 16), ("fv", 32)))
        fkb = t4("fkb", 24, 2)
        dkT = t4("dkT", 40, 1)
        dvrow = sb("dvrow", [P, NT, 64], F32, R + 42 * KB)
        iqT = t4("iqT", 46, 2)
        ikT = t4("ikT", 50, 1)
        sel = t4("sel", 52)
        score = t4("score", 60, 2)
        rowS = sb("rowS", [P, NT, 48], F32, R + 43 * KB)
        FT = sb("FT", [8, S], F32, R + 44 * KB)
        O2 = {"a": (t4("foxhi", 0, 4, F32R), t4("foxlo", 8, 4, F32R)),
              "b": (t4("dsahi", 16, 4, F32R), t4("dsalo", 24, 4, F32R))}
        trig = sb("trig", [P, 2, 2, S])
        cst = sb("cst", [P, C_END])
        vec = sb("vec", [P, P])
        vec2 = sb("vec2", [P, V2_N])
        mod = sb("mod", [P, 72])
        geff = sb("geff", [P, 24])
        foxb = sb("foxb", [8, 1])
        st = sb("st", [P, 4, S])
        tmp = sb("tmp", [P, 4, S])
        shared = sb("shared", [P, S])
        rdiag = shared[:, :].rearrange("p (t n) -> p t n", t=NT)
        early, root = sb("early", [P, 8]), sb("root", [P, 6, NT])
        hidrow = shared[:, :].rearrange("p (v n) -> p v n", v=2)
        narrowT = shared
        Pb = sb("Pb", [P, 2, S])
        posi = sb("posi", [P, S], I32, used[0])
        PT = sb("PT", [P, 2, S])
        SQ = [Pb[:, 0, :], Pb[:, 1, :], PT[:, 0, :], PT[:, 1, :]]
        stat = sb("stat", [P, 8, 4])
        Fq = sb("Fq", [P, NT, 8])
        diag = sb("diag", [P, 2, P])
        posf = tmp[:, 3, :]
        SQUARES = [st[:, 0, :], st[:, 1, :], st[:, 2, :], st[:, 3, :], tmp[:, 2, :], tmp[:, 3, :], st[:, 0, :], st[:, 1, :]]
        blkf = tmp[:, 2:4, :].rearrange("p a n -> p (a n)")[:, 0:CMP_S * 62].rearrange("p (s c) -> p s c", s=CMP_S)
        wsm = sb("wsm", [P, KD, 48], F32, None)
        wsmhi = sb("wsmhi", [P, KD, 48], F32R)
        wsmlo = sb("wsmlo", [P, KD, 48], F32R)
        rows = Pb[:, :, :].rearrange("p a n -> p (a n)")
        Sp = tmp[:, 0:2, :]
        dkrow = tmp[:, 2, :].rearrange("p (t n) -> p t n", t=NT)
        ikrow = tmp[:, 3, :].rearrange("p (t n) -> p t n", t=NT)
        top8 = sb("top8", [P, 8])
        PB4 = [Pb[:, 0, :], Pb[:, 1, :], st[:, 2, :], st[:, 3, :]]
        PT4 = [PT[:, 0, :], PT[:, 1, :], st[:, 0, :], st[:, 1, :]]
        BUF = dict(rqT=rqT, rkT=rkT, qT=qT, srg=srg, kvT=kvT, rv=rv, vrow=vrow, fqT=fqT, fkT=fkT, dqT=dqT, fv=fv,
                   iqT=iqT, ikT=ikT, dkT=dkT)
        ps = ctx.enter_context(nc.psum_tensor("ps", [P, 8, S], F32))
        col = lambda c, n=1: cst[:, c:c + n]
        ident = cst[:, C_ID:C_ID + P]

        def ada_slot(u):
            n = u % ADA_SLOTS
            return adaw[:, n, :] if n < 4 else trig[:, n - 4, :, :].rearrange("p a n -> p (a n)")

        def modsum(b):
            return tmp[:, 2 * (b % 2):2 * (b % 2) + 2, :].rearrange("p a n -> p (a n)")

        w_landed = [sem(f"w_landed{i}") for i in range(SLOTS)]
        w_hi = sem("w_hi")
        w_split = sem("w_split")
        w_used = sem("w_used")
        ld_x = [sem("ld_x0"), sem("ld_x1")]
        ld_cst, ld_rows, ld_pos, ld_dmat, ld_w2 =  (sem(n) for n in ("ld_cst", "ld_rows", "ld_pos",
                                                                          "ld_dmat", "ld_w2"))
        ld_wsm = sem("ld_wsm")
        wsm_hi, wsm_ready = sem("wsm_hi"), sem("wsm_ready")
        x_turned, x_ready = sem("x_turned"), sem("x_ready")
        vec_turned, vec_ready = sem("vec_turned"), sem("vec_ready")
        cond_sig, cond_ready = sem("cond_sig"), sem("cond_ready")
        ada_landed = [sem(f"ada_landed{i}") for i in range(ADA_SLOTS)]
        mod_prod, mod_added, mod_summed, mod_ready = (sem(n) for n in ("mod_prod", "mod_added", "mod_summed", "mod_ready"))
        trig_arg, trig_ready = sem("trig_arg"), sem("trig_ready")
        n_add, n_diag, n_all = sem("n_add"), sem("n_diag"), sem("n_all")
        n_sq, n_sum, n_root, n_t, n_hi, h_ready = (sem(n) for n in ("n_sq", "n_sum", "n_root", "n_t", "n_hi", "h_ready"))
        dve = sem("dve_chain")
        pj_mm, pj_ev, pj_post, pj_root, pj_dve, pj_silu = (sem(n) for n in ("pj_mm", "pj_ev", "pj_post", "pj_root",
                                                                             "pj_dve", "pj_silu"))
        rt_qk, rt_sd, rt_pv, rt_ev, rt_sum, rt_root, rt_rcp, rt_m, rt_o, rt_hi, rt_done = (
            sem(n) for n in ("rt_qk", "rt_sd", "rt_pv", "rt_ev", "rt_sum", "rt_root", "rt_rcp", "rt_m", "rt_o", "rt_hi", "rt_done"))
        cm_shift, cm_blk, cm_sig, cm_hid, cm_turn, cm_hidT, cm_out, cm_done = (
            sem(n) for n in ("cm_shift", "cm_blk", "cm_sig", "cm_hid", "cm_turn", "cm_hidT", "cm_out", "cm_done"))
        f_z, f_e, f_l, f_scan, f_back, f_ready = (sem(n) for n in ("f_z", "f_e", "f_l", "f_scan",
                                                                            "f_back", "f_ready"))
        fk_mm, fk_ready = sem("fk_mm"), sem("fk_ready")
        ix_mm, ix_relu, ix_acc, ix_done = sem("ix_mm"), sem("ix_relu"), sem("ix_acc"), sem("ix_done")
        mx_g, mx_p, mx_sig, mx_m, mx_t, mx_hi, mx_ready = (sem(n) for n in ("mx_g", "mx_p", "mx_sig", "mx_m", "mx_t",
                                                                            "mx_hi", "mx_ready"))
        dn_done = sem("dn_done")
        up_mm, up_relu, up_t, up_hi, up_ready = (sem(n) for n in ("up_mm", "up_relu", "up_t", "up_hi", "up_ready"))
        ff_g, ff_u, ff_sig, ff_m1, ff_m2, ff_hi, ff_ready = (sem(n) for n in ("ff_g", "ff_u", "ff_sig", "ff_m1", "ff_m2",
                                                                              "ff_hi", "ff_ready"))
        y_turned, y_ready, y_stored = sem("y_turned"), sem("y_ready"), sem("y_stored")

        BL = dict(zip(("nsa", "rq", "rk", "rvg", "fox", "dsa"), proj_blocks()))
        PLAN = {name: plan_projection(b) for name, b in BL.items()}
        G0, P0, R0, SL0 = {}, {}, {}, {}
        g = p = r = sl = 0
        n_out = {"A": 4, "G": 2, "B": 2, "K": 6}
        for name, blocks in BL.items():
            G0[name], P0[name], R0[name], SL0[name] = g, p, r, sl
            g += sum(n_out[b[0]] for b in blocks)
            p += sum(len(t) for t in PLAN[name][1])
            r += sum(k == "ms" for t in PLAN[name][1] for k, _ in t)
            sl += sum(c[0] == "silu" for b in blocks if b[0] == "B" for c in b[4])
        PEND = dict(zip(BL, [*list(P0.values())[1:], p]))
        GEND = dict(zip(BL, [*list(G0.values())[1:], g]))
        post_event, last_event = {}, {}
        for name in BL:
            p = P0[name]
            for turn in PLAN[name][1]:
                for kind, v in turn:
                    post_event[name, kind, v] = p
                    last_event[name, v] = p
                    p += 1
        SLOT_FREE = {}
        slot_event = {}
        for name in BL:
            for v in range(len(PLAN[name][0])):
                SLOT_FREE[name, v] = slot_event.get(v % 4, -1) + 1
                slot_event[v % 4] = last_event[name, v]
        MS_EVENT = {}
        n_ms = {}
        for name in BL:
            for turn in PLAN[name][1]:
                for kind, v in turn:
                    if kind == "ms":
                        n_ms[name, v] = len(MS_EVENT)
                        MS_EVENT[len(MS_EVENT)] = post_event[name, kind, v]
        N_ROW_DMAS = 13
        OUT_DONE = {}
        mm = 0
        for name, blocks in BL.items():
            g, s = G0[name], AT[name]
            for b in blocks:
                s += {"A": 2, "B": 2, "K": 1, "G": 0}[b[0]]
                for x in range(n_out[b[0]]):
                    if b[0] != "G" and x == {"A": 3, "B": 1, "K": 3}[b[0]]:
                        OUT_DONE[g] = (w_used, s)
                    else:
                        mm += 1
                        OUT_DONE[g] = (pj_mm, mm)
                    g += 1
        DOWN_DONE = {}
        X_BEFORE_NORM = [0, 8, 24, 32, 48, 56]
        X_BEFORE_DOWN = dict(out1=8, down0=16, down1=24, f1down0=40, f1down1=48, out2=56, f2down0=64, f2down1=72)
        H_NORM = {0: 0, 1: 1, 3: 2, 4: 3, 5: 4}
        GAIN = {0: vec[:, V_MIX:V_MIX + 8], 1: vec[:, V_MLP:V_MLP + 8], 2: vec[:, V_FINAL:V_FINAL + 8],
                3: geff[:, 0:8], 4: geff[:, 8:16], 5: geff[:, 16:24]}
        SHIFT = {3: mod[:, 0:8], 4: mod[:, 24:32], 5: mod[:, 48:56]}
        QKG = {0: V2_FQ, 1: V2_FK, 2: V2_DQ, 3: V2_DK}
        DOWN_K = dict(down0=16, down1=16, f1down0=12, f1down1=10, f2down0=12, f2down1=10, out1=8, out2=8)
        for d, name in enumerate(X_BEFORE_DOWN):
            for m in range(KD):
                DOWN_DONE[name, m] = (dn_done, 7 * d + m + 1) if m < KD - 1 else (w_used, AT[name] + DOWN_K[name])

        def gate_done(b, n, br, c):
            return (mx_g, 8 * b + 2 * n + br + 1) if c == 0 else (w_used, AT[("mix1", "mix2")[b]] + 6 * n + 3 * br + 2)

        def branch_done(b, n, br, c):
            return (mx_p, 8 * b + 2 * n + br + 1) if c == 0 else (w_used, AT[("mix1", "mix2")[b]] + 6 * n + 3 * br + 3)

        def nsa_steps():
            out_ = []
            for c in range(4):
                for g in range(2):
                    for i in range(NT):
                        rows_ = slice(64 * g, 64 * g + 64)
                        head = 4 * g + c
                        q = qT[rows_, c, i * P:(i + 1) * P]
                        for b, (k, v) in enumerate((
                                (kcmpT[rows_, 0:N_CMP], [vcmp[0:N_CMP, 64 * g:64 * g + 64]]),
                                (kvT[rows_, 2, 0:(i + 1) * P], [vrow[:, j, 64 * g:64 * g + 64] for j in range(i + 1)]),
                                (kvT[rows_, 3, 0:(i + 1) * P],
                                 [vrow[:, j, 128 + 64 * g:192 + 64 * g] for j in range(i + 1)]))):
                            out_.append(dict(q=q, k=k, v=v, n=k.shape[-1], i=i, c=c, half=g, mask="cmp" if b == 0 else "causal",
                                             gate=gates[:, i, 3 * head + b:3 * head + b + 1], first=b == 0, last=b == 2,
                                             av=col(C_AV + i) if b == 0 else None))
            return out_

        def fox_steps():
            return [dict(q=fqT[64 * g:64 * g + 64, c, i * P:(i + 1) * P], k=fkT[64 * g:64 * g + 64, c, 0:(i + 1) * P],
                         v=[fv[:, j, 64 * (2 * c + g):64 * (2 * c + g) + 64] for j in range(i + 1)], n=(i + 1) * P, i=i, c=c,
                         half=g, mask="fox", head=2 * c + g, gate=None, av=None, first=True, last=True)
                    for c in range(4) for g in range(2) for i in range(NT)]

        def dsa_steps():
            return [dict(q=dqT[64 * g:64 * g + 64, c, i * P:(i + 1) * P], k=dkT[64 * g:64 * g + 64, 0, 0:(i + 1) * P],
                         v=[dvrow[:, j, :] for j in range(i + 1)], n=(i + 1) * P, i=i, c=c, half=g, mask="dsa",
                         gate=None, av=None, first=True, last=True)
                    for c in range(4) for g in range(2) for i in reversed(range(NT))]

        def fox_dsa_steps():
            return fox_steps() + [{**t, "c": t["c"] + 4} for t in dsa_steps()]

        STEPS = {"nsa": nsa_steps(), "fd": fox_dsa_steps()}
        N_SELECT = 2 + 2 * (TOPK // 8)
        SELECT_AT = [(12, 21), (22, 28), (28, 34)]
        at_qk, at_max, at_exp, at_rcp, at_nrm, at_tr, at_pt, at_pv, at_hi, at_done = (
            {ph: sem(f"{ph}_{w}") for ph in STEPS} for w in ("qk", "max", "exp", "rcp", "nrm", "tr", "pt", "pv", "hi", "done"))
        N_CH = {"nsa": 4, "fd": 8}
        OUT = {"nsa": [[O1["a"][k][:, c, :] for c in range(4)] for k in range(2)],
               "fd": [[O2["ab"[c // 4]][k][:, c % 4, :] for c in range(8)] for k in range(2)]}
        CHUNK_END = {ph: [max(s for s, t in enumerate(steps) if t["c"] == c) for c in range(N_CH[ph])]
                     for ph, steps in STEPS.items()}
        LAG = dict(max=1, exp=2, rcp=3, diag=4, turn=5, copy=6, values=7, out_hi=8, out_lo=9)
        ROUNDS = {ph: len(steps) + LAG["values"] for ph, steps in STEPS.items()}
        MOD_STEP = {11 * b + 14: b for b in range(9)}
        UNITS = [(i, (h,)) for i in (3, 2) for h in range(8)] + [(1, (h, h + 4)) for h in range(4)]
        UNIT_AT = {4 * (u // 3) + u % 3: u for u in range(len(UNITS))}
        SUMS = [0]
        for i, hs in UNITS:
            SUMS.append(SUMS[-1] + len(hs))
        ONES = col(C_AV + 1)

        def by_group(t, slot, c):
            return t[:, slot, :].rearrange("p (k g c d) -> p c k g d", k=4, g=2, c=2)[:, c]

        def by_head(t, slot, c):
            return t[:, slot, :].rearrange("p (k c g d) -> p c k g d", k=4, g=2, c=2)[:, c]

        block = ctx.enter_context(nc.Block())

        @block.sync
        def _(sp):
            def load(s, src, after=None):
                slot = s % SLOTS
                if after is not None:
                    sp.wait_ge(w_split, after)
                if len(src.shape) == 4:
                    for g in range(2):
                        dst = raw[:, slot, :].rearrange("p (k g n) -> p k g n", k=src.shape[1], g=2)[:, :, g, :]
                        sp.dma_start(dst, src[:, :, g, :]).then_inc(w_landed[slot], 16)
                    return
                for a in (0, 64):
                    dst = raw[a:a + 64, slot, :]
                    if len(src.shape) == 3:
                        dst = dst.rearrange("p (k n) -> p k n", k=src.shape[1])
                    sp.dma_start(dst, src[a:a + 64]).then_inc(w_landed[slot], 16)

            def load_next(s, src):
                load(s, src, s - SLOTS + 1 if s >= SLOTS else None)

            def cols(w, k0, c0, stride):
                v = w[k0 * P:(k0 + 4) * P, :].rearrange("(k p) n -> p k n", p=P)
                if stride == P:
                    return v[:, :, c0:c0 + 256]
                return v[:, :, c0:c0 + 2 * stride].rearrange("p k (g n) -> p k g n", n=stride)[:, :, :, 0:P]

            def load_projection(name, w, start=0, end=N_SLABS):
                s = AT[name]
                for b in BL[name]:
                    if b[0] in "AB":
                        for q in range(2):
                            if start <= s - AT[name] < end:
                                load_next(s, cols(w, 4 * q, b[1], b[2]))
                            s += 1
                    elif b[0] == "K":
                        load_next(s, w.rearrange("(k p) n -> p k n", p=P)[:, :, b[1]:b[1] + P])
                        s += 1

            def load_mix(name, w, ga, gb, wa, wb, heads_apart, start, end):
                s = AT[name]
                for n in range(4):
                    for gate, wp, apart in ((ga, wa, heads_apart), (gb, wb, False)):
                        for q in range(2):
                            if start <= s - AT[name] < end:
                                load_next(s, cols(w, 4 * q, gate + 256 * n, P))
                            s += 1
                        if start <= s - AT[name] < end and apart:
                            sp.wait_ge(w_split, s - SLOTS + 1)
                            for g in range(2):
                                sp.dma_start(
                                    raw[64 * g:64 * g + 64, s % SLOTS, :].rearrange("p (k n) -> p k n", k=4),
                                    wp[256 * g:256 * g + 256, 256 * n:256 * n + 256].rearrange("(c p) n -> p c n", p=64),
                                ).then_inc(w_landed[s % SLOTS], 16)
                        elif start <= s - AT[name] < end:
                            load_next(s, cols(wp, 0, 256 * n, P))
                        s += 1

            def load_rows(name, w, k0):
                s0 = AT[name]
                K = DOWN_K[name]
                v = w.rearrange("(k p) n -> k p n", p=P)
                n4 = K // 4
                with sp.Fori(0, n4) as i:
                    for j in range(4):
                        sp.wait_ge(w_split, i * 4 + (s0 + j - SLOTS + 1))
                        for a in (0, 64):
                            sp.dma_start(raw[a:a + 64, (s0 + j) % SLOTS, :],
                                         v[bass.ds(i * 4 + (k0 + j), 1), a:a + 64, :].rearrange("k p n -> (k p) n"))\
                              .then_inc(w_landed[(s0 + j) % SLOTS], 16)
                for k in range(4 * n4, K):
                    load_next(s0 + k, v[k0 + k])

            def load_up(name, c0, ws):
                s0 = AT[name]
                per = 2 * len(ws)
                n = {"up0": 4, "up1": 4}.get(name, (6 if name.endswith("0") else 5))
                body = [(w, q, b) for b in range(2 if len(ws) == 1 else 1) for w in ws for q in range(2)]
                step = 256 * (2 if len(ws) == 1 else 1)
                assert len(body) == 4
                with sp.Fori(0, n) as i:
                    for j, (w, q, b) in enumerate(body):
                        sp.wait_ge(w_split, i * 4 + (s0 + j - SLOTS + 1))
                        v = w[4 * q * P:4 * (q + 1) * P, :].rearrange("(k p) n -> p k n", p=P)
                        for a in (0, 64):
                            sp.dma_start(raw[a:a + 64, (s0 + j) % SLOTS, :].rearrange("p (k n) -> p k n", k=4),
                                         v[a:a + 64, :, bass.ds(i * step + (c0 + 256 * b), 256)])\
                              .then_inc(w_landed[(s0 + j) % SLOTS], 16)

            w_in, w_in_2 = T["w_in"][0], T["w_in_2"][0]
            load_projection("nsa", w_in)

            def load_cmp(name, w):
                v = w.rearrange("(s p) n -> p s n", p=P)
                for q in range(4):
                    load_next(AT[name] + q, v[:, 4 * q:4 * q + 4, :])

            load_projection("rq", w_in)
            load_cmp("cmpk", T["cmp_k_w1"][0])
            load_projection("rk", w_in)
            load_cmp("cmpv", T["cmp_v_w1"][0])
            load_projection("rvg", w_in)
            mix1 = ("mix1", w_in, W1["ga"], W1["gb"], T["w_proj_a"][0], T["w_proj_b"][0], True)
            load_mix(*mix1, 0, SLOTS)
            ada = T["ada_w_2"][0]
            sp.wait_ge(rt_pv, 16)
            sp.wait_ge(rt_sd, 16)
            for u in range(72):
                b, k = u // KD, u % KD
                if u >= ADA_SLOTS:
                    v = u - ADA_SLOTS
                    sp.wait_ge(*((mod_prod, v + 1) if v % KD == 0 else (mod_added, (KD - 1) * (v // KD) + v % KD)))
                sp.dma_start(ada_slot(u), ada[k * P:(k + 1) * P, b * D:(b + 1) * D])\
                  .then_inc(ada_landed[u % ADA_SLOTS], 16)
            load_mix(*mix1, SLOTS, 24)
            load_rows("out1", T["w_out"][0], 0)
            for h in range(2):
                load_up(f"up{h}", 2048 * h, [T["w_up"][0]])
                load_rows(f"down{h}", T["w_down"][0], 16 * h)

            def load_ffn(f, w1, w3, w2):
                for h in range(2):
                    load_up(f"{f}up{h}", 1536 * h, [w1, w3])
                    load_rows(f"{f}down{h}", w2, 12 * h)

            load_ffn("f1", T["ffn1_w1_2"][0], T["ffn1_w3_2"][0], T["ffn1_w2_2"][0])
            load_projection("fox", w_in_2)
            load_projection("dsa", w_in_2)
            load_mix("mix2", w_in_2, W2["ga"], W2["gb"], T["w_br_fox_2"][0], T["w_br_dsa_2"][0], False, 0, 24)
            load_rows("out2", T["w_out_2"][0], 0)
            load_ffn("f2", T["ffn2_w1_2"][0], T["ffn2_w3_2"][0], T["ffn2_w2_2"][0])
            for t in range(NT):
                sp.wait_ge(y_ready, 2 * t + 2)
                sp.dma_start(out[0, t * P:(t + 1) * P, :], xrow[:, t, :]).then_inc(y_stored, 16)
            sp.wait_ge(y_stored, 16 * NT)

        @block.gpsimd
        def _(pool):
            def low(s, i=None):
                slot = s % SLOTS
                pool.wait_ge(w_hi, s + 1 if i is None else i * SLOTS + (s + 1))
                parts = [(wlo[:, slot, :], raw[:, slot, :], whi[:, slot, :])]
                if i is None and s < 4:
                    parts = [(by_head(wlo, slot, c), by_group(raw, slot, c), by_head(whi, slot, c)) for c in range(2)]
                for lo, src, hi in parts:
                    last = pool.tensor_tensor(lo, src, hi.bitcast(F32), ALU.subtract)
                last.then_inc(w_split, 1)

            def lows(start, end):
                with pool.Fori(0, (end - start) // SLOTS) as i:
                    for j in range(SLOTS):
                        low(start + j, i)
                for s in range(end - (end - start) % SLOTS, end):
                    low(s)

            def retention():
                for h in range(4):
                    r, o = PT[:, h % 2, :], st[:, h % 2, :]
                    pool.wait_ge(rt_rcp, h + 1)
                    pool.tensor_tensor(o, o, r, ALU.mult).then_inc(rt_m, 1)
                    pool.wait_ge(rt_m, h + 1)
                    pool.wait_ge(pj_silu, h + 1)
                    pool.tensor_tensor(o, o, srg[:, h, :], ALU.mult).then_inc(rt_o, 1)
                    pool.wait_ge(rt_hi, h + 1)
                    pool.tensor_tensor(O1["b"][1][:, h, :], o, O1["b"][0][:, h, :].bitcast(F32), ALU.subtract)\
                      .then_inc(rt_done, 1)

            def modulation():
                for b in range(9):
                    for k in range(1, KD):
                        pool.wait_ge(mod_prod, KD * b + k + 1)
                        if k >= 2:
                            pool.wait_ge(mod_added, (KD - 1) * b + k - 1)
                        pool.tensor_tensor(modsum(b), modsum(b), ada_slot(KD * b + k), ALU.add).then_inc(mod_added, 1)

            for s in range(SLOTS):
                low(s)
            lows(SLOTS, AT["mix1"] + SLOTS)
            retention()
            modulation()
            lows(AT["mix1"] + SLOTS, N_SLABS)

        @block.tensor
        def _(pe):
            after_compress = {"rk": 1, "rvg": 2}

            def three(out_, lhi, llo, rhi, rlo, first, last):
                pe.matmul(out_, lhi, rhi, start=first, stop=False)
                pe.matmul(out_, lhi, rlo, start=False, stop=False)
                return pe.matmul(out_, llo, rhi, start=False, stop=last)

            def slab(s, k=4):
                return (whi[:, s % SLOTS, :].rearrange("p (k n) -> p k n", k=k),
                        wlo[:, s % SLOTS, :].rearrange("p (k n) -> p k n", k=k))

            def turn_vectors():
                pe.wait_ge(ld_rows, 16 * N_ROW_DMAS)
                pe.wait_ge(x_ready, 4)
                pe.transpose(ps[:, 2, 0:P], rows[:, 0:P], ident).then_inc(vec_turned, 1)
                pe.transpose(ps[:, 3, 0:V2_N], rows[0:V2_N, P:2 * P], cst[0:V2_N, C_ID:C_ID + V2_N]).then_inc(vec_turned, 1)

            def norm(n):
                for m in range(3):
                    if m < 2:
                        pe.wait_ge(n_sq, 8 * n + m + 1)
                    else:
                        if n == 0:
                            turn_vectors()
                        pe.wait_ge(n_add, 5 * n + 5)
                    src = SQUARES[m] if m < 2 else tmp[:, 0, :]
                    for t in range(NT):
                        mm = pe.matmul(ps[:, 0, t:t + 1], src[:, t * P:t * P + P], cst[:, C_MEAN:C_MEAN + 1],
                                       start=m == 0 and t == 0, stop=m == 2, skip_group_check=True)
                    mm.then_inc(n_sum, 1)
                for t in range(NT):
                    pe.wait_ge(n_diag, NT * n + t + 1)
                    mm = pe.matmul(ps[:, 7, t * P:t * P + P], cst[:, C_MEAN:C_MEAN + P], rdiag[:, t, :], start=True, stop=True)
                mm.then_inc(n_all, 1)

            def projection(name, hn):
                chunks, turns = PLAN[name]
                s, g = AT[name], G0[name]
                p, v = P0[name], 0
                out_of = []
                blocks = BL[name]

                def bank(x):
                    if x >= 4:
                        pe.wait_ge(pj_ev, x - 3)
                    if name in after_compress and x < G0[name] + 4 and x % 4 == 0:
                        pe.wait_ge(cm_hid, after_compress[name])
                    return x % 4

                for n in range(len(blocks) + 2):
                    if n < len(blocks):
                        b = blocks[n]
                        if b[0] == "B":
                            banks = [bank(g + c) for c in range(2)]
                            for q in range(2):
                                pe.wait_ge(w_split, s + 1)
                                hi, lo = slab(s)
                                for c in range(2):
                                    for k in range(4):
                                        kk = 4 * q + k
                                        if n == 0 and c == 0:
                                            pe.wait_ge(h_ready, 8 * hn + kk + 1)
                                        cc = slice(P * c, P * c + P)
                                        mm = three(ps[:, banks[c], :], hi[:, k, cc], lo[:, k, cc], hhi[:, kk, :], hlo[:, kk, :],
                                                   kk == 0, kk == 7)
                                    if q == 1 and c == 0:
                                        mm.then_inc(pj_mm, 1)
                                mm.then_inc(w_used, 1)
                                s += 1
                            for c in range(2):
                                if b[4][c][0] in ("rope", "norm", "normrope"):
                                    out_of.append(g + c)
                            g += 2
                        elif b[0] == "A":
                            banks = [bank(g + t) for t in range(NT)]
                            for q in range(2):
                                pe.wait_ge(w_split, s + 1)
                                hi, lo = slab(s)
                                for t in range(NT):
                                    tt = slice(t * P, t * P + P)
                                    for k in range(4):
                                        kk = 4 * q + k
                                        mm = three(ps[:, banks[t], 0:256], hhi[:, kk, tt], hlo[:, kk, tt], hi[:, k, :],
                                                   lo[:, k, :], kk == 0, kk == 7)
                                    if q == 1 and t < NT - 1:
                                        mm.then_inc(pj_mm, 1)
                                mm.then_inc(w_used, 1)
                                s += 1
                            g += NT
                        elif b[0] == "G":
                            pe.wait_ge(wsm_ready, b[3])
                            w, bk = b[1], bank(g)
                            for k in range(KD):
                                mm = three(ps[0:w, bk, :], wsmhi[:, k, 0:w], wsmlo[:, k, 0:w], hhi[:, k, :], hlo[:, k, :],
                                           k == 0, k == 7)
                            mm.then_inc(pj_mm, 1)
                            pe.wait_ge(pj_ev, g + 1)
                            bk = bank(g + 1)
                            for t in range(NT):
                                mm = pe.transpose(ps[:, bk, w * t:w * t + w], narrowT[0:w, t * P:t * P + P],
                                                  cst[0:w, C_ID:C_ID + w])
                            mm.then_inc(pj_mm, 1)
                            g += 2
                        else:
                            pe.wait_ge(w_split, s + 1)
                            hi, lo = slab(s, KD)
                            for t in range(NT):
                                tt = slice(t * P, t * P + P)
                                bk = bank(g)
                                for k in range(KD):
                                    mm = three(ps[:, bk, 0:P], hhi[:, k, tt], hlo[:, k, tt], hi[:, k, :], lo[:, k, :],
                                               k == 0, k == 7)
                                if t < NT - 1:
                                    mm.then_inc(pj_mm, 1)
                                g += 1
                            mm.then_inc(w_used, 1)
                            s += 1
                            pe.wait_ge(pj_ev, g)
                            for rowsrc in (dkrow, ikrow):
                                bk = bank(g)
                                for t in range(NT):
                                    mm = pe.transpose(ps[:, bk, t * P:t * P + P], rowsrc[:, t, :], ident)
                                mm.then_inc(pj_mm, 1)
                                out_of.append(g)
                                g += 1
                    for kind, v in turns[n]:
                        c = chunks[v]
                        if p >= 4:
                            pe.wait_ge(pj_dve, p - 3)
                        if kind == "ms":
                            pe.wait_ge(pj_ev, out_of[v] + 1)
                            m = n_ms[name, v]
                            pe.matmul(ps[:, 4 + p % 4, :], cst[:, C_HD64:C_HD64 + P], SQ[m % 4], start=True, stop=True)\
                              .then_inc(pj_post, 1)
                        else:
                            if c[0] == "rope":
                                pe.wait_ge(pj_ev, out_of[v] + 1)
                            else:
                                pe.wait_ge(pj_dve, post_event[name, "ms", v] + 1)
                            perm = c[4] if c[0] == "rope" else c[5]
                            pe.matmul(ps[:, 4 + p % 4, :], cst[:, perm:perm + P], st[:, v % 4, :], start=True, stop=True)\
                              .then_inc(pj_post, 1)
                        p += 1

            def retention():
                def pv(x):
                    h, j = x // NT, x % NT
                    pe.wait_ge(rt_sd, x + 1)
                    if j == 0 and h >= 2:
                        pe.wait_ge(rt_ev, h - 1)
                    pe.matmul(ps[:, 3 + h % 2, j * P:S], rv[:, j, h * P:h * P + P], tmp[:, x % 4, 0:S - j * P],
                              start=j == 0, stop=j == NT - 1).then_inc(rt_pv, 1)

                def head_sum(h):
                    pe.wait_ge(rt_ev, h + 1)
                    pe.matmul(ps[:, 5 + h % 2, :], cst[:, C_HD128:C_HD128 + P], PT[:, h % 2, :], start=True, stop=True)\
                      .then_inc(rt_sum, 1)

                pe.wait_ge(pj_dve, PEND["rvg"])
                pe.wait_ge(pj_ev, GEND["rvg"])
                for x in range(16 + 3):
                    if x < 16:
                        h, j = x // NT, x % NT
                        if x >= 3:
                            pe.wait_ge(rt_sd, x - 2)
                        pe.matmul(ps[:, x % 3, 0:S - j * P], rkT[:, h, j * P:j * P + P], rqT[:, h, j * P:S],
                                  start=True, stop=True).then_inc(rt_qk, 1)
                    if 2 <= x < 18:
                        pv(x - 2)
                    if x % NT == 2 and x >= 6:
                        head_sum(x // NT - 1)

            def compress_hidden(kv):
                name = ("cmpk", "cmpv")[kv]
                pe.wait_ge(cm_blk, kv + 1)
                pe.wait_ge(pj_ev, GEND[("rq", "rk")[kv]])
                for q in range(4):
                    s = AT[name] + q
                    pe.wait_ge(w_split, s + 1)
                    hi, lo = slab(s)
                    for k in range(4):
                        kk = 4 * q + k
                        mm = three(ps[0:62, 0, 0:256], blkhi[:, kk, :], blklo[:, kk, :], hi[:, k, :], lo[:, k, :],
                                   kk == 0, kk == CMP_S - 1)
                    mm.then_inc(w_used, 1)

            def compress_out():
                pe.wait_ge(cm_hid, 2)
                pe.wait_ge(ld_w2, 32)
                pe.wait_ge(pj_dve, PEND["rvg"])
                for kv in range(2):
                    for hc in range(2):
                        at = (2 * kv + hc) * 64
                        mm = pe.transpose(ps[:, 7, at:at + 62], hidrow[0:62, kv, P * hc:P * hc + P], cst[0:62, C_ID:C_ID + 62])
                mm.then_inc(cm_turn, 1)
                pe.wait_ge(cm_hidT, 1)
                for kv in range(2):
                    for g in range(2):
                        gs = slice(64 * g, 64 * g + 64)
                        for hc in range(2):
                            hid = hidc[:, kv, hc, N_CMP * g:N_CMP * (g + 1)]
                            if kv == 0:
                                mm = pe.matmul(ps[gs, 7, 0:N_CMP], cmpw2[:, 0, hc, :], hid, start=hc == 0, stop=hc == 1)
                            else:
                                mm = pe.matmul(ps[0:N_CMP, 7, 128 + 64 * g:192 + 64 * g], hid, cmpw2[:, 1, hc, :],
                                               start=hc == 0, stop=hc == 1)
                mm.then_inc(cm_out, 1)

            def modulation_sums(b):
                pe.wait_ge(mod_added, (KD - 1) * (b + 1))
                for m in range(KD):
                    mm = pe.matmul(ps[:, 7, KD * b + m:KD * b + m + 1], modsum(b)[:, m * P:(m + 1) * P], ONES,
                                   start=True, stop=True)
                mm.then_inc(mod_summed, 1)

            def index_unit(u):
                i, heads = UNITS[u]
                if u >= 1:
                    pe.wait_ge(ix_relu, u)
                pe.wait_ge(fk_ready, u // 3 + 1)
                for a, h in enumerate(heads):
                    rs, n = slice(32 * (h % 4), 32 * (h % 4) + 32), (i + 1) * P
                    mm = pe.matmul(ps[:, 7, a * n:a * n + n], iqT[rs, h // 4, i * P:(i + 1) * P], ikT[rs, 0, 0:n],
                                   start=True, stop=True)
                mm.then_inc(ix_mm, 1)

            def attention(ph):
                steps = STEPS[ph]

                def scores(s):
                    t = steps[s]
                    n, i = t["n"], t["i"]
                    if s >= 3:
                        pe.wait_ge(at_exp[ph], s - 2)
                    mask = {"causal": (i * P, C_CAUSAL, P), "fox": (i * P, C_CAUSAL, P), "cmp": (0, C_CMP + 32 * i, n),
                            "dsa": None}[t["mask"]]
                    mm = pe.matmul(ps[:, s % 3, 0:n], t["q"], t["k"], start=True, stop=mask is None)
                    if mask is not None:
                        at, c, w = mask
                        mm = pe.matmul(ps[:, s % 3, at:at + w], ident, cst[:, c:c + w], start=False, stop=True)
                    mm.then_inc(at_qk[ph], 1)

                def forget_keys(h):
                    if h >= 1:
                        pe.wait_ge(fk_ready, h)
                        pe.wait_ge(ix_relu, min(3 * h, len(UNITS)))
                    pe.matmul(ps[:, 7, :], cst[0:8, C_ID + h:C_ID + h + 1].broadcast_to([8, P]), FT[:, :],
                              start=True, stop=True).then_inc(fk_mm, 1)

                def turn(s):
                    t = steps[s]
                    pe.wait_ge(at_nrm[ph], s + 1)
                    if s >= 2:
                        pe.wait_ge(at_pt[ph], s - 1)
                    for j in range(len(t["v"])):
                        nk = min(P, t["n"] - j * P)
                        mm = pe.matmul(ps[0:nk, 3 + s % 2, j * P:j * P + P], PB4[s % 4][:, j * P:j * P + nk], diag[:, s % 2, :],
                                       start=True, stop=True)
                    mm.then_inc(at_tr[ph], 1)

                def values(s):
                    t = steps[s]
                    pe.wait_ge(at_pt[ph], s + 1)
                    if t["c"] >= 2 and s == CHUNK_END[ph][t["c"] - 1] + 1:
                        pe.wait_ge(at_done[ph], t["c"] - 1)
                    nv = len(t["v"])
                    for j in range(nv):
                        nk = min(P, t["n"] - j * P)
                        mm = pe.matmul(ps[64 * t["half"]:64 * t["half"] + 64, 5 + t["c"] % 2, t["i"] * P:(t["i"] + 1) * P],
                                       t["v"][j], PT4[s % 4][0:nk, j * P:j * P + P], start=t["first"] and j == 0,
                                       stop=t["last"] and j == nv - 1)
                    mm.then_inc(at_pv[ph], 1)

                n = len(steps)
                if ph == "fd":
                    forget_keys(0)
                for r in range(ROUNDS[ph]):
                    if r < n:
                        scores(r)
                    if 0 <= r - LAG["turn"] < n:
                        turn(r - LAG["turn"])
                    if 0 <= r - LAG["values"] < n:
                        values(r - LAG["values"])
                    if ph == "nsa" and r in MOD_STEP:
                        modulation_sums(MOD_STEP[r])
                    if ph == "fd" and r in UNIT_AT:
                        index_unit(UNIT_AT[r])
                    if ph == "fd" and r % NT == NT - 1 and r < 7 * NT:
                        forget_keys(r // NT + 1)

            def forget_back():
                pe.wait_ge(pj_ev, GEND["dsa"])
                pe.wait_ge(pj_dve, PEND["dsa"])
                pe.wait_ge(f_scan, 1)
                for t in range(NT):
                    mm = pe.transpose(ps[:, 6, 8 * t:8 * t + 8], FT[:, t * P:t * P + P], cst[0:8, C_ID:C_ID + 8])
                mm.then_inc(f_back, 1)
                pe.wait_ge(f_ready, 1)

            def mix(b, name, outs):
                s = AT[name]
                for n in range(4):
                    for br in range(2):
                        x0 = 16 * b + 4 * n + 2 * br
                        for c in range(2):
                            if n >= 1:
                                pe.wait_ge(mx_sig, x0 + c - 4 + 1)
                        for q in range(2):
                            pe.wait_ge(w_split, s + 1)
                            hi, lo = slab(s)
                            for c in range(2):
                                for k in range(4):
                                    kk = 4 * q + k
                                    mm = three(ps[:, 4 * br + c, :], hi[:, k, P * c:P * c + P], lo[:, k, P * c:P * c + P],
                                               hhi[:, kk, :], hlo[:, kk, :], kk == 0, kk == 7)
                                if q == 1 and c == 0:
                                    mm.then_inc(mx_g, 1)
                            mm.then_inc(w_used, 1)
                            s += 1
                        pe.wait_ge(w_split, s + 1)
                        hi, lo = slab(s)
                        ohi, olo = outs["ab"[br]]
                        for c in range(2):
                            if n >= 1:
                                pe.wait_ge(mx_m, x0 + c - 4 + 1)
                            for k in range(4):
                                mm = three(ps[:, 4 * br + 2 + c, :], hi[:, k, P * c:P * c + P], lo[:, k, P * c:P * c + P],
                                           ohi[:, k, :], olo[:, k, :], k == 0, k == 3)
                            if c == 0:
                                mm.then_inc(mx_p, 1)
                        mm.then_inc(w_used, 1)
                        s += 1

            def down(name, ahi, alo, ready, ready0, banks_free):
                K, s0 = DOWN_K[name], AT[name]

                def one(k, i=None, j=0):
                    if i is None:
                        s = s0 + k
                        pe.wait_ge(w_split, s + 1)
                        pe.wait_ge(ready, ready0 + k + 1)
                        rhi, rlo = ahi[:, k, :], alo[:, k, :]
                    else:
                        s = s0 + 1 + j
                        pe.wait_ge(w_split, i * 4 + (s + 1))
                        rhi = ahi[:, bass.ds(i * 4 + (1 + j), 1), :].rearrange("p k n -> p (k n)")
                        rlo = alo[:, bass.ds(i * 4 + (1 + j), 1), :].rearrange("p k n -> p (k n)")
                    hi, lo = slab(s, KD)
                    for m in range(KD):
                        if k == 0:
                            banks_free(m)
                        mm = three(ps[:, m, :], hi[:, m, :], lo[:, m, :], rhi, rlo, k == 0, k == K - 1)
                        if k == K - 1 and m < KD - 1:
                            mm.then_inc(dn_done, 1)
                    mm.then_inc(w_used, 1)

                if K > 8:
                    one(0)
                    pe.wait_ge(ready, ready0 + K)
                    loops = (K - 2) // 4
                    with pe.Fori(0, loops) as i:
                        for j in range(4):
                            one(1, i, j)
                    for k in range(1 + 4 * loops, K):
                        one(k)
                else:
                    for k in range(K):
                        one(k)

            def up(h):
                s0, u0 = AT[f"up{h}"], 16 * h

                def blocks(i):
                    for b in range(2):
                        for q in range(2):
                            j = 2 * b + q
                            pe.wait_ge(w_split, i * 4 + (s0 + j + 1))
                            hi, lo = slab(s0 + j)
                            for c in range(2):
                                ch = 2 * b + c
                                if q == 0:
                                    if isinstance(i, int):
                                        if h == 1:
                                            pe.wait_ge(x_ready, X_BEFORE_DOWN["down0"] + ch + 1)
                                    else:
                                        pe.wait_ge(up_relu, i * 4 + (u0 + ch - 3))
                                for k in range(4):
                                    kk = 4 * q + k
                                    if isinstance(i, int) and h == 0 and b == 0 and c == 0:
                                        pe.wait_ge(h_ready, 8 + kk + 1)
                                    mm = three(ps[:, ch, :], hi[:, k, P * c:P * c + P], lo[:, k, P * c:P * c + P],
                                               hhi[:, kk, :], hlo[:, kk, :], kk == 0, kk == 7)
                                if q == 1 and c == 0:
                                    mm.then_inc(up_mm, 1)
                            mm.then_inc(w_used, 1)

                blocks(0)
                with pe.Fori(1, 4) as i:
                    blocks(i)

            def ffn_up(f, h, hn):
                s0, u0 = AT[f"f{f + 1}up{h}"], 22 * f + 12 * h
                n = 6 - h
                before = X_BEFORE_DOWN[f"f{f + 1}down0"]

                def blocks(i):
                    for w, done, free in ((0, ff_g, ff_m1), (1, ff_u, ff_m2)):
                        for q in range(2):
                            j = 2 * w + q
                            pe.wait_ge(w_split, i * 4 + (s0 + j + 1))
                            hi, lo = slab(s0 + j)
                            for c in range(2):
                                if q == 0:
                                    if isinstance(i, int):
                                        if h == 1:
                                            pe.wait_ge(x_ready, before + 2 * w + c + 1)
                                    else:
                                        pe.wait_ge(free, i * 2 + (u0 + c - 1))
                                for k in range(4):
                                    kk = 4 * q + k
                                    if isinstance(i, int) and h == 0 and w == 0 and c == 0:
                                        pe.wait_ge(h_ready, 8 * hn + kk + 1)
                                    mm = three(ps[:, 2 * w + c, :], hi[:, k, P * c:P * c + P], lo[:, k, P * c:P * c + P],
                                               hhi[:, kk, :], hlo[:, kk, :], kk == 0, kk == 7)
                                if q == 1 and c == 0:
                                    mm.then_inc(done, 1)
                            mm.then_inc(w_used, 1)

                blocks(0)
                with pe.Fori(1, n) as i:
                    blocks(i)

            def ffn(f, hn):
                for h in range(2):
                    name = f"f{f + 1}down{h}"
                    ffn_up(f, h, hn)
                    u1 = 22 * f + 12 * h + (12 if h == 0 else 10)

                    def free(m):
                        if m < 4:
                            pe.wait_ge((ff_m1, ff_m2)[m // 2], u1)
                        elif h == 1:
                            pe.wait_ge(x_ready, X_BEFORE_DOWN[f"f{f + 1}down0"] + m + 1)
                    down(name, hidhi, hidlo, ff_ready, 22 * f + 12 * h, free)

            pe.wait_ge(ld_cst, 16)
            for m in range(KD):
                if m in (0, KD // 2):
                    pe.wait_ge(ld_x[2 * m // KD], 16)
                for t in range(NT):
                    mm = pe.transpose(ps[:, m, t * P:t * P + P], xrow[:, t, m * P:m * P + P], ident)
                mm.then_inc(x_turned, 1)
            norm(0)
            pe.wait_ge(vec_ready, 2)
            projection("nsa", 0)
            projection("rq", 0)
            compress_hidden(0)
            projection("rk", 0)
            compress_hidden(1)
            projection("rvg", 0)
            compress_out()
            retention()
            pe.wait_ge(cm_done, 2)
            pe.wait_ge(cond_ready, 1)
            pe.wait_ge(rt_sd, 16)
            pe.wait_ge(rt_root, 4)
            attention("nsa")
            pe.wait_ge(at_done["nsa"], 4)
            pe.wait_ge(mod_ready, 1)
            mix(0, "mix1", O1)
            down("out1", mixhi, mixlo, mx_ready, 0,
                 lambda m: pe.wait_ge((mx_sig, mx_m)[m // 2 % 2], 12 + 2 * (m // 4) + m % 2 + 1))
            norm(1)
            up(0)
            down("down0", hidhi, hidlo, up_ready, 0, lambda m: pe.wait_ge(up_relu, 12 + m + 1) if m < 4 else None)
            up(1)
            down("down1", hidhi, hidlo, up_ready, 16,
                 lambda m: pe.wait_ge(up_relu, 28 + m + 1) if m < 4 else pe.wait_ge(x_ready, 16 + m + 1))
            norm(2)
            norm(3)
            ffn(0, 2)
            norm(4)
            projection("fox", 3)
            projection("dsa", 3)
            forget_back()
            attention("fd")
            pe.wait_ge(at_done["fd"], 8)
            mix(1, "mix2", O2)
            down("out2", mixhi, mixlo, mx_ready, 8,
                 lambda m: pe.wait_ge((mx_sig, mx_m)[m // 2 % 2], 28 + 2 * (m // 4) + m % 2 + 1))
            norm(5)
            ffn(1, 4)
            for t in range(NT):
                for m in range(KD):
                    if t == 0:
                        pe.wait_ge(x_ready, 73 + m)
                    mm = pe.transpose(ps[:, 2 * t + m // 4, (m % 4) * P:(m % 4 + 1) * P], xT[:, m, t * P:t * P + P], ident)
                    if m % 4 == 3:
                        mm.then_inc(y_turned, 1)

        @block.scalar
        def _(sc):
            def high(s, i=None):
                if i is None and s >= N_SLABS:
                    return
                slot = s % SLOTS
                if i is None:
                    sc.wait_ge(w_landed[slot], 32 * (s // SLOTS + 1))
                    if s >= SLOTS:
                        sc.wait_ge(w_used, s - SLOTS + 1)
                else:
                    sc.wait_ge(w_landed[slot], i * 32 + 32 * (s // SLOTS + 1))
                    sc.wait_ge(w_used, i * SLOTS + (s - SLOTS + 1))
                if i is None and s < 4:
                    sc.activation(by_head(whi, slot, 0), by_group(raw, slot, 0), ACT.Copy)
                    sc.activation(by_head(whi, slot, 1), by_group(raw, slot, 1), ACT.Copy).then_inc(w_hi, 1)
                else:
                    sc.activation(whi[:, slot, :], raw[:, slot, :], ACT.Copy).then_inc(w_hi, 1)

            def highs_of_rows(name, late=0):
                K, s0 = DOWN_K[name], AT[name] + SLOTS
                n4 = (K - late) // 4
                with sc.Fori(0, n4) as i:
                    for j in range(4):
                        high(s0 + j, i)
                for k in range(4 * n4, K - late):
                    high(s0 + k)

            def norm(n, late=None):
                for m in range(KD):
                    sc.wait_ge(x_ready, X_BEFORE_NORM[n] + m + 1)
                    if m >= 6:
                        sc.wait_ge(n_sum, 3 * n + m - 5)
                    sc.activation(SQUARES[m], xT[:, m, :], ACT.Square).then_inc(n_sq, 1)
                    if n == 0 and m >= SLOTS:
                        high(m - SLOTS)
                if late is not None:
                    high(late)
                if n == 0:
                    sc.wait_ge(vec_turned, 1)
                    sc.activation(vec[:, :], ps[:, 2, 0:P], ACT.Copy).then_inc(vec_ready, 1)
                    sc.wait_ge(vec_turned, 2)
                    sc.activation(vec2[:, :], ps[:, 3, 0:V2_N], ACT.Copy).then_inc(vec_ready, 1)
                sc.activation(early[:, n:n + 1], col(C_EPS), ACT.Sqrt)
                sc.wait_ge(n_sum, 3 * n + 3)
                sc.activation(root[:, n, :], ps[:, 0, 0:NT], ACT.Sqrt, bias=col(C_EPS)).then_inc(n_root, 1)
                if n in H_NORM:
                    h8 = 8 * H_NORM[n]
                    for m in range(KD):
                        sc.wait_ge(n_t, h8 + m + 1)
                        if n in SHIFT:
                            sc.activation(hhi[:, m, :], st[:, 2 + m % 2, :], ACT.Identity,
                                          bias=SHIFT[n][:, m:m + 1]).then_inc(n_hi, 1)
                        else:
                            sc.activation(hhi[:, m, :], st[:, 2 + m % 2, :], ACT.Copy).then_inc(n_hi, 1)

            def projection(name, hooks={}):
                chunks, turns = PLAN[name]
                s = AT[name]
                g, v, x, root, silu, p = G0[name], 0, 0, R0[name], SL0[name], P0[name]
                msq = R0[name]
                for n in range(len(BL[name]) + 2):
                    if n in hooks:
                        hooks[n]()
                    if n < len(BL[name]):
                        b = BL[name][n]
                        if b[0] == "K":
                            sc.wait_ge(pj_ev, GEND["fox"])
                            sc.activation(ikrow.rearrange("p t (a d) -> p t a d", a=4),
                                          rowS[:, :, 8:40].unsqueeze(2).broadcast_to([P, NT, 4, 32]), ACT.Copy)
                            for t in range(NT):
                                sc.wait_ge(*OUT_DONE[g])
                                sc.activation(dvrow[:, t, :], ps[:, g % 4, 64:128], ACT.Copy)
                                sc.activation(dkrow[:, t, :].rearrange("p (a d) -> p a d", a=2),
                                              ps[:, g % 4, 0:64].unsqueeze(1).broadcast_to([P, 2, 64]), ACT.Copy)\
                                  .then_inc(pj_ev, 1)
                                g += 1
                        for c in (b[4] if b[0] in "BK" else ()):
                            sc.wait_ge(*OUT_DONE[g])
                            o = ps[:, g % 4, :]
                            if c[0] == "copy":
                                sc.activation(BUF[c[1]][:, c[2], :], o, ACT.Copy).then_inc(pj_ev, 1)
                            elif c[0] == "silu":
                                if silu - 2 >= SL0[name]:
                                    sc.wait_ge(pj_silu, silu - 1)
                                sc.activation(Pb[:, silu % 2, :], o, ACT.Copy)
                                sc.activation(PT[:, silu % 2, :], o, ACT.Sigmoid).then_inc(pj_ev, 1)
                                silu += 1
                            else:
                                if SLOT_FREE[name, v]:
                                    sc.wait_ge(pj_dve, SLOT_FREE[name, v])
                                scale = c[5] if c[0] == "rope" else 1.0
                                a = sc.activation(st[:, v % 4, :], o, ACT.Copy, scale=scale)
                                if c[0] != "rope":
                                    if msq >= 4:
                                        sc.wait_ge(pj_dve, MS_EVENT[msq - 4] + 1)
                                    a = sc.activation(SQ[msq % 4], o, ACT.Square)
                                    msq += 1
                                a.then_inc(pj_ev, 1)
                                v += 1
                            g += 1
                        if b[0] == "A":
                            for t in range(NT):
                                sc.wait_ge(*OUT_DONE[g])
                                sc.activation(BUF[b[3][0]][:, t, b[3][1]:b[3][1] + 256], ps[:, g % 4, 0:256], ACT.Copy)\
                                  .then_inc(pj_ev, 1)
                                g += 1
                        if b[0] == "G":
                            w = b[1]
                            sc.wait_ge(*OUT_DONE[g])
                            sc.activation(narrowT[0:w, :], ps[0:w, g % 4, :], ACT.Copy).then_inc(pj_ev, 1)
                            sc.wait_ge(*OUT_DONE[g + 1])
                            rows_of = ps[:, (g + 1) % 4, 0:NT * w].rearrange("p (t n) -> p t n", t=NT)
                            if b[2] == "gates":
                                sc.activation(gates[:, :, :], rows_of, ACT.Sigmoid).then_inc(pj_ev, 1)
                            else:
                                sc.activation(rowS[:, :, :], rows_of, ACT.Copy).then_inc(pj_ev, 1)
                            g += 2
                    for kind, _ in turns[n]:
                        if kind == "ms":
                            sc.wait_ge(pj_post, p + 1)
                            sc.activation(SQ[root % 4], ps[:, 4 + p % 4, :], ACT.Sqrt, bias=col(C_EPS)).then_inc(pj_root, 1)
                            root += 1
                        p += 1
                    if n < len(BL[name]):
                        for _ in range({"A": 2, "B": 2, "K": 1, "G": 0}[BL[name][n][0]]):
                            high(s + SLOTS)
                            s += 1

            def retention_high(h):
                sc.wait_ge(rt_o, h + 1)
                sc.activation(O1["b"][0][:, h, :], st[:, h % 2, :], ACT.Copy).then_inc(rt_hi, 1)

            def retention():
                for h in range(4):
                    sc.wait_ge(rt_pv, 4 * h + 4)
                    if h >= 2:
                        sc.wait_ge(rt_done, h - 1)
                    sc.activation(st[:, h % 2, :], ps[:, 3 + h % 2, :], ACT.Copy)
                    sc.activation(PT[:, h % 2, :], ps[:, 3 + h % 2, :], ACT.Square).then_inc(rt_ev, 1)
                    sc.wait_ge(rt_sum, h + 1)
                    sc.activation(PT[:, h % 2, :], ps[:, 5 + h % 2, :], ACT.Sqrt, bias=col(C_EPS)).then_inc(rt_root, 1)
                    if h >= 1:
                        retention_high(h - 1)

            def shift_dmas(kv):
                for g in range(2):
                    src = kvT[64 * g:64 * g + 64, kv, :]
                    sc.dma_start(kshift[0:64, g, :], src).then_inc(cm_shift, 16)
                    sc.dma_start(kshift[64:128, g, 0:S - 1], src[:, 1:S]).then_inc(cm_shift, 16)

            def attention(ph):
                steps = STEPS[ph]
                ohi = OUT[ph][0]

                def outputs(c):
                    sc.wait_ge(at_pv[ph], CHUNK_END[ph][c] + 1)
                    sc.activation(ohi[c], ps[:, 5 + c % 2, :], ACT.Copy).then_inc(at_hi[ph], 1)

                def forget_keys(h):
                    sc.wait_ge(fk_mm, h + 1)
                    if h >= 2:
                        sc.wait_ge(at_max[ph], NT * (h - 1))
                    sc.activation(fkb[:, h % 2, :], ps[:, 7, :], ACT.Copy).then_inc(fk_ready, 1)

                def diagonal(s):
                    sc.wait_ge(at_rcp[ph], s + 1)
                    if s >= 2:
                        sc.wait_ge(at_tr[ph], s - 1)
                    sc.activation(diag[:, s % 2, :], ident, ACT.Copy, scale=stat[:, s % 8, 2:3]).then_inc(at_nrm[ph], 1)

                def copy_turned(s):
                    sc.wait_ge(at_tr[ph], s + 1)
                    if s >= 4:
                        sc.wait_ge(at_pv[ph], s - 3)
                    t = steps[s]
                    nk, w = min(P, t["n"]), len(t["v"]) * P
                    sc.activation(PT4[s % 4][0:nk, 0:w], ps[0:nk, 3 + s % 2, 0:w], ACT.Copy).then_inc(at_pt[ph], 1)

                def exponentials(s):
                    t = steps[s]
                    sc.wait_ge(at_max[ph], s + 1)
                    if s >= 4:
                        sc.wait_ge(at_tr[ph], s - 3)
                    src = Sp[:, s % 2, 0:t["n"]] if t["mask"] in ("fox", "dsa") else ps[:, s % 3, 0:t["n"]]
                    sc.activation(PB4[s % 4][:, 0:t["n"]], src, ACT.Exp, bias=stat[:, s % 8, 0:1],
                                  accum_out=stat[:, s % 8, 1:2]).then_inc(at_exp[ph], 1)

                def index_relu(u):
                    i, heads = UNITS[u]
                    n = (i + 1) * P * len(heads)
                    sc.wait_ge(ix_mm, u + 1)
                    if u >= 2:
                        sc.wait_ge(ix_acc, SUMS[u - 1])
                    sc.activation(tmp[:, 2 + u % 2, 0:n], ps[:, 7, 0:n], ACT.Relu, scale=32 ** -0.5).then_inc(ix_relu, 1)

                for r in range(ROUNDS[ph] + 2):
                    if ph == "fd" and r % NT == 0 and r < 8 * NT:
                        forget_keys(r // NT)
                    if ph == "fd" and r - 1 in UNIT_AT:
                        index_relu(UNIT_AT[r - 1])
                    if 0 <= r - LAG["exp"] < len(steps):
                        exponentials(r - LAG["exp"])
                    if ph == "fd" and 0 <= r - LAG["diag"] < len(steps):
                        diagonal(r - LAG["diag"])
                    if ph == "nsa" and r == LAG["copy"]:
                        retention_high(3)
                        sc.wait_ge(rt_done, 4)
                    if 0 <= r - LAG["copy"] < len(steps):
                        copy_turned(r - LAG["copy"])
                    for c in range(N_CH[ph]):
                        if r == CHUNK_END[ph][c] + LAG["out_hi"]:
                            outputs(c)

            def forget():
                z, e = score[0:8, 0, :], score[0:8, 1, :]
                sc.wait_ge(pj_ev, GEND["fox"])
                sc.activation(z, narrowT[0:8, :], ACT.Identity, bias=foxb[:, 0:1]).then_inc(f_z, 1)
                sc.wait_ge(f_e, 1)
                sc.activation(e, e, ACT.Exp, scale=-1.0).then_inc(f_l, 1)
                sc.wait_ge(f_e, 2)
                sc.activation(e, e, ACT.Ln).then_inc(f_l, 1)

            def forget_back():
                sc.wait_ge(f_back, 1)
                sc.activation(Fq[:, :, :], ps[:, 6, 0:32].rearrange("p (t h) -> p t h", t=NT), ACT.Copy).then_inc(f_ready, 1)

            def mix(b):
                for n in range(4):
                    for br in range(2):
                        for c in range(2):
                            x = 16 * b + 4 * n + 2 * br + c
                            sc.wait_ge(*gate_done(b, n, br, c))
                            if n >= 1:
                                sc.wait_ge(mx_m, x - 3)
                            sc.activation(st[:, 2 * br + c, :], ps[:, 4 * br + c, :], ACT.Sigmoid).then_inc(mx_sig, 1)
                        for q in range(3):
                            high(AT[("mix1", "mix2")[b]] + 6 * n + 3 * br + q + SLOTS)
                    for c in range(2):
                        x = 8 * b + 2 * n + c
                        sc.wait_ge(mx_t, x + 1)
                        sc.activation(mixhi[:, 2 * n + c, :], tmp[:, c, :], ACT.Copy).then_inc(mx_hi, 1)

            def up(h):
                u0 = 16 * h

                def chunks(i):
                    for c in range(4):
                        at = lambda k: i * 4 + (u0 + c + k)
                        if c % 2 == 0:
                            sc.wait_ge(up_mm, i * 2 + (8 * h + c // 2 + 1))
                        else:
                            sc.wait_ge(w_used, i * 4 + (AT[f"up{h}"] + c + 1))
                        sc.activation(st[:, c, :], ps[:, c, :], ACT.Relu).then_inc(up_relu, 1)
                        sc.wait_ge(up_t, at(1))
                        o = hidhi[:, c, :] if isinstance(i, int) else hidhi[:, bass.ds(i * 4 + c, 1), :].rearrange(
                            "p k n -> p (k n)")
                        sc.activation(o, tmp[:, c, :], ACT.Copy).then_inc(up_hi, 1)
                        if c % 2:
                            for q in range(2):
                                high(AT[f"up{h}"] + SLOTS + c - 1 + q, None if isinstance(i, int) else i)
                chunks(0)
                with sc.Fori(1, 4) as i:
                    chunks(i)

            def ffn_up(f, h):
                u0 = 22 * f + 12 * h

                def chunks(i):
                    at = lambda c, k: i * 2 + (u0 + c + k)
                    for c in range(2):
                        if c == 0:
                            sc.wait_ge(ff_g, i + (11 * f + 6 * h + 1))
                        else:
                            sc.wait_ge(w_used, i * 4 + (AT[f"f{f + 1}up{h}"] + 2))
                        sc.activation(st[:, c, :], ps[:, c, :], ACT.Sigmoid).then_inc(ff_sig, 1)
                    for q in range(2):
                        high(AT[f"f{f + 1}up{h}"] + SLOTS + q, None if isinstance(i, int) else i)
                    for c in range(2):
                        sc.wait_ge(ff_m2, at(c, 1))
                        o = hidhi[:, c, :] if isinstance(i, int) else hidhi[:, bass.ds(i * 2 + c, 1), :].rearrange(
                            "p k n -> p (k n)")
                        sc.activation(o, tmp[:, 2 + c, :], ACT.Copy).then_inc(ff_hi, 1)
                    for q in range(2, 4):
                        high(AT[f"f{f + 1}up{h}"] + SLOTS + q, None if isinstance(i, int) else i)
                chunks(0)
                with sc.Fori(1, 6 - h) as i:
                    chunks(i)

            def small_weights(parts):
                for lo, src in parts:
                    sc.dma_start(wsm[:, :, lo:lo + src.shape[2]], src).then_inc(ld_wsm, 16)

            sc.dma_start(cst[:, :], T["consts"]).then_inc(ld_cst, 16)
            for half in range(2):
                cols = slice(half * D // 2, (half + 1) * D // 2)
                sc.dma_start(xrow[:, :, cols], T["x"][0].rearrange("(t p) d -> p t d", p=P)[:, :, cols])\
                  .then_inc(ld_x[half], 16)
            vectors = [(V_MIX, T["norm_mix"][0]), (V_MLP, T["norm_mlp"][0]), (V_FINAL, T["norm_final"]),
                       (V_G2, T["norm_g_2"][0].rearrange("s d -> (s d)")), (V_C, T["c_2"][0]), (V_ADAB, T["ada_b_2"][0])]
            for at, v in vectors:
                n = v.shape[0] // P
                sc.dma_start(rows[at:at + n, 0:P], v.rearrange("(r p) -> r p", p=P)).then_inc(ld_rows, 16)
            for at, v in ((V2_PEK, T["cmp_pos_k"][0]), (V2_PEV, T["cmp_pos_v"][0])):
                sc.dma_start(rows[at:at + CMP_S, P:2 * P], v.rearrange("(s l) d -> s (l d)", l=2)).then_inc(ld_rows, 16)
            for at, v in ((V2_FQ, T["fox_qk_g_2"][0]), (V2_DQ, T["dsa_qk_g_2"][0])):
                for half in range(2):
                    sc.dma_start(rows[at:at + 2, P + 64 * half:P + 64 * half + 64], v).then_inc(ld_rows, 16)
            sc.dma_start(foxb[:, :], T["fox_f_bias_2"][0].rearrange("(h a) -> h a", a=1)).then_inc(ld_rows, 16)
            sc.dma_start(posi[:, :], T["positions"].broadcast_to([P, S])).then_inc(ld_pos, 16)
            win = T["w_in"][0].rearrange("(k p) n -> p k n", p=P)
            with nc.allow_non_contiguous_dma(reason="24 gate columns"):
                small_weights([(0, win[:, :, W1["gates"]:W1["gates"] + 24])])
            for kv, n in enumerate(("cmp_k_w2", "cmp_v_w2")):
                sc.dma_start(cmpw2[:, kv, :, :], T[n][0].rearrange("(c p) n -> p c n", p=P)).then_inc(ld_w2, 16)
            norm(0)
            sc.wait_ge(vec_ready, 2)
            sc.activation(geff[:, 0:8], vec[:, V_C:V_C + 8], ACT.Sigmoid).then_inc(cond_sig, 1)

            def sines(table):
                for f in range(2):
                    sc.wait_ge(trig_arg, 4 * table[1] + 2 * table[0] + f + 1)
                    sc.activation(trig[:, table[0], f, :], trig[:, table[0], f, :], ACT.Sin).then_inc(trig_ready, 1)

            def compress_sigmoids(kv):
                name = ("cmpk", "cmpv")[kv]
                for q in range(4):
                    high(AT[name] + SLOTS + q)
                sc.wait_ge(w_used, AT[name] + 4)
                sc.activation(hidrow[0:62, kv, :], ps[0:62, 0, 0:256], ACT.Sigmoid).then_inc(cm_sig, 1)

            projection("nsa", {2: lambda: [sines((tb, 0)) for tb in range(2)]})
            sc.wait_ge(pj_dve, PEND["nsa"])
            sc.wait_ge(pj_ev, GEND["nsa"])
            shift_dmas(0)
            projection("rq")
            sc.wait_ge(cm_blk, 1)
            shift_dmas(1)
            compress_sigmoids(0)
            projection("rk")
            compress_sigmoids(1)
            sc.dma_start(dmat[:, :, :], T["decay"].rearrange("p (h n) -> p h n", h=4)).then_inc(ld_dmat, 16)
            projection("rvg")
            retention()
            attention("nsa")
            sc.dma_start(posi[:, :], T["positions_2"].broadcast_to([P, S])).then_inc(ld_pos, 16)
            sc.wait_ge(wsm_ready, 1)
            win2 = T["w_in_2"][0].rearrange("(k p) n -> p k n", p=P)
            sc.wait_ge(pj_ev, GEND["nsa"])
            with nc.allow_non_contiguous_dma(reason="48 narrow columns"):
                small_weights([(0, win2[:, :, W2["ff"]:W2["ff"] + 8]), (8, win2[:, :, W2["ik"]:W2["ik"] + 40])])
            mix(0)
            highs_of_rows("out1", 1)
            norm(1, AT["out1"] + DOWN_K["out1"] - 1 + SLOTS)
            up(0)
            highs_of_rows("down0")
            for tb in range(2):
                sines((tb, 1))
            up(1)
            highs_of_rows("down1", 1)
            norm(2, AT["down1"] + DOWN_K["down1"] - 1 + SLOTS)
            norm(3)
            for h in range(2):
                ffn_up(0, h)
                highs_of_rows(f"f1down{h}", h)
            norm(4, AT["f1down1"] + DOWN_K["f1down1"] - 1 + SLOTS)
            projection("fox")
            projection("dsa", {1: forget})
            forget_back()
            attention("fd")
            mix(1)
            highs_of_rows("out2", 1)
            norm(5, AT["out2"] + DOWN_K["out2"] - 1 + SLOTS)
            ffn_up(1, 0)
            highs_of_rows("f2down0")
            ffn_up(1, 1)
            for s in range(AT["f2down1"] + SLOTS, N_SLABS):
                high(s)
            for t in range(NT):
                for b in range(2):
                    sc.wait_ge(y_turned, 2 * t + b + 1)
                    sc.activation(xrow[:, t, 512 * b:512 * b + 512], ps[:, 2 * t + b, :], ACT.Copy).then_inc(y_ready, 1)

        @block.vector
        def _(ve):
            chain = [0]

            def link(ins):
                chain[0] += 1
                ins.then_inc(dve, 1)
                ve.wait_ge(dve, chain[0])

            def norm(n):
                a, b, q = tmp[:, 0, :], tmp[:, 1, :], SQUARES
                for x, (out_, in0, in1, square, add) in enumerate(((a, q[2], q[3], 4, 0), (b, q[4], q[5], 6, 0),
                                                                   (a, a, q[6], 7, 1), (b, b, q[7], 8, 2), (a, a, b, 8, 4))):
                    ve.wait_ge(n_sq, 8 * n + square)
                    if add:
                        ve.wait_ge(n_add, 5 * n + add)
                    ve.tensor_tensor(out_, in0, in1, ALU.add).then_inc(n_add, 1)
                ve.wait_ge(n_root, n + 1)
                link(ve.reciprocal(root[:, n, :], root[:, n, :]))
                for t in range(NT):
                    ve.tensor_scalar(rdiag[:, t, :], ident, root[:, n, t:t + 1], float(D), ALU.mult, ALU.mult)\
                      .then_inc(n_diag, 1)
                ve.wait_ge(n_all, n + 1)
                if n not in H_NORM:
                    for m in range(KD):
                        ve.scalar_tensor_tensor(out=xT[:, m, :], in0=xT[:, m, :], scalar=GAIN[n][:, m:m + 1],
                                                in1=ps[:, 7, :], op0=ALU.mult, op1=ALU.mult).then_inc(x_ready, 1)
                    return
                h8 = 8 * H_NORM[n]

                def low(m):
                    ve.wait_ge(n_hi, h8 + m + 1)
                    hi_ = hhi[:, m, :].bitcast(F32)
                    if n in SHIFT:
                        i_ = ve.scalar_tensor_tensor(out=hlo[:, m, :], in0=st[:, 2 + m % 2, :], scalar=SHIFT[n][:, m:m + 1],
                                                     in1=hi_, op0=ALU.add, op1=ALU.subtract)
                    else:
                        i_ = ve.tensor_tensor(hlo[:, m, :], st[:, 2 + m % 2, :], hi_, ALU.subtract)
                    i_.then_inc(h_ready, 1)

                for m in range(KD):
                    if m >= 2:
                        ve.wait_ge(h_ready, h8 + m - 1)
                    ve.scalar_tensor_tensor(out=st[:, 2 + m % 2, :], in0=xT[:, m, :], scalar=GAIN[n][:, m:m + 1],
                                            in1=ps[:, 7, :], op0=ALU.mult, op1=ALU.mult).then_inc(n_t, 1)
                    if m >= 1:
                        low(m - 1)
                low(KD - 1)

            def trig_tables(b):
                ve.wait_ge(ld_pos, 16 * (b + 1))
                if b == 1:
                    ve.wait_ge(up_ready, 16)
                link(ve.tensor_copy(posf, posi[:, :]))
                c1, c2 = 6.28125, 1.934051513671875e-03
                c3 = 2 * math.pi - c1 - c2
                ang, k = tmp[:, 0, :], tmp[:, 1, :]
                for tb in range(2):
                    link(ve.tensor_scalar(ang, posf, col(C_INV + 2 * b + tb), None, ALU.mult))
                    for f in range(2):
                        r = trig[:, tb, f, :]
                        link(ve.tensor_scalar(k, ang, 1 / (2 * math.pi), 0.25 if f == 0 else 0.0, ALU.mult, ALU.add))
                        link(ve.tensor_scalar(k, k, MAGIC, MAGIC, ALU.add, ALU.subtract))
                        link(ve.scalar_tensor_tensor(out=r, in0=k, scalar=-c1, in1=ang, op0=ALU.mult, op1=ALU.add))
                        link(ve.scalar_tensor_tensor(out=r, in0=k, scalar=-c2, in1=r, op0=ALU.mult, op1=ALU.add))
                        link(ve.scalar_tensor_tensor(out=r, in0=k, scalar=-c3, in1=r, op0=ALU.mult, op1=ALU.add))
                        link(ve.tensor_scalar(r, r, math.pi / 2 if f == 0 else 0.0, 3.1415925, ALU.add, ALU.min))
                        ve.tensor_scalar(r, r, -3.1415925, None, ALU.max).then_inc(trig_arg, 1)

            def projection(name, table_base, hooks={}):
                chunks, turns = PLAN[name]
                p, root, silu = P0[name], R0[name], SL0[name]
                g = G0[name]
                first_perm = [True]
                for n in range(len(BL[name]) + 2):
                    if n in hooks:
                        hooks[n]()
                    if n < len(BL[name]):
                        b = BL[name][n]
                        if b[0] == "B":
                            for c in range(2):
                                if b[4][c][0] == "silu":
                                    ve.wait_ge(pj_ev, g + c + 1)
                                    ve.tensor_tensor(srg[:, b[4][c][2], :], Pb[:, silu % 2, :], PT[:, silu % 2, :],
                                                     ALU.mult).then_inc(pj_silu, 1)
                                    silu += 1
                        g += n_out[b[0]]
                    for kind, v in turns[n]:
                        c = chunks[v]
                        if kind == "ms":
                            r = SQ[root % 4]
                            ve.wait_ge(pj_root, root + 1)
                            link(ve.reciprocal(r, r))
                            dst = BUF[c[1]][:, c[2], :] if c[0] == "norm" else st[:, v % 4, :]
                            gc = QKG[c[3]]
                            ve.scalar_tensor_tensor(out=dst, in0=st[:, v % 4, :], scalar=vec2[:, gc:gc + 1], in1=r,
                                                    op0=ALU.mult, op1=ALU.mult).then_inc(pj_dve, 1)
                            root += 1
                        else:
                            if first_perm[0]:
                                ve.wait_ge(trig_ready, table_base + 4)
                                first_perm[0] = False
                            tb = c[3] if c[0] == "rope" else c[4]
                            ve.wait_ge(pj_post, p + 1)
                            if p >= 1:
                                ve.wait_ge(pj_dve, p)
                            link(ve.tensor_tensor(tmp[:, 0, :], st[:, v % 4, :], trig[:, tb, 0, :], ALU.mult))
                            link(ve.tensor_tensor(tmp[:, 1, :], ps[:, 4 + p % 4, :], trig[:, tb, 1, :], ALU.mult))
                            ve.tensor_tensor(BUF[c[1]][:, c[2], :], tmp[:, 0, :], tmp[:, 1, :], ALU.add)\
                              .then_inc(pj_dve, 1)
                        p += 1

            def retention():
                def finish(h):
                    ve.wait_ge(rt_root, h + 1)
                    ve.reciprocal(PT[:, h % 2, :], PT[:, h % 2, :]).then_inc(rt_rcp, 1)

                ve.wait_ge(pj_silu, 4)
                ve.wait_ge(ld_dmat, 16)
                x = 0
                for h in range(4):
                    for j in range(NT):
                        n = S - j * P
                        ve.wait_ge(rt_qk, x + 1)
                        if x >= 4:
                            ve.wait_ge(rt_pv, x - 3)
                        ve.tensor_tensor(tmp[:, x % 4, 0:n], ps[:, x % 3, 0:n], dmat[:, h, 0:n], ALU.mult).then_inc(rt_sd, 1)
                        if j == 3 and h >= 1:
                            finish(h - 1)
                        x += 1
                finish(3)

            def compress_blocks(kv):
                ve.wait_ge(cm_shift, 64 * (kv + 1))
                if kv == 1:
                    ve.wait_ge(w_used, AT["cmpk"] + 4)
                pe_col = V2_PEK if kv == 0 else V2_PEV
                for g in range(2):
                    v = kshift[:, g, :].rearrange("p (c t) -> p t c", t=16)
                    for a in range(2):
                        last = ve.tensor_tensor(
                            blkf[:, 8 * a:8 * a + 8, N_CMP * g:N_CMP * (g + 1)], v[:, 0:16:2, a:a + N_CMP],
                            vec2[:, pe_col + 8 * a:pe_col + 8 * a + 8].unsqueeze(2).broadcast_to([P, 8, N_CMP]), ALU.add)
                link(last)
                link(ve.tensor_copy(blkhi[:, :, :], blkf))
                ve.tensor_tensor(blklo[:, :, :], blkf, blkhi[:, :, :].bitcast(F32), ALU.subtract).then_inc(cm_blk, 1)

            def compress_hidden(kv):
                ve.wait_ge(cm_sig, kv + 1)
                ve.tensor_tensor(hidrow[0:62, kv, :], ps[0:62, 0, 0:256], hidrow[0:62, kv, :], ALU.mult).then_inc(cm_hid, 1)

            def compress_out():
                ve.wait_ge(cm_turn, 1)
                ve.tensor_copy(hidc[:, :, :, :].rearrange("p v c n -> p (v c n)").rearrange("p (a n) -> p a n", a=4)[:, :, 0:62],
                               ps[:, 7, 0:256].rearrange("p (a n) -> p a n", a=4)[:, :, 0:62]).then_inc(cm_hidT, 1)
                ve.wait_ge(cm_out, 1)
                ve.tensor_copy(kcmpT[:, 0:N_CMP], ps[:, 7, 0:N_CMP]).then_inc(cm_done, 1)
                ve.tensor_copy(vcmp[0:N_CMP, :], ps[0:N_CMP, 7, P:2 * P]).then_inc(cm_done, 1)

            def attention(ph):
                steps = STEPS[ph]
                ohi, olo = OUT[ph]

                def maxima(s):
                    t = steps[s]
                    n, i = t["n"], t["i"]
                    sp_, o = Sp[:, s % 2, 0:n], ps[:, s % 3, 0:n]
                    ve.wait_ge(at_qk[ph], s + 1)
                    if ph == "fd" and s >= 2:
                        ve.wait_ge(at_exp[ph], s - 1)
                    if t["mask"] == "fox":
                        h = t["head"]
                        if i == 0:
                            ve.wait_ge(fk_ready, h + 1)
                        link(ve.scalar_tensor_tensor(out=sp_, in0=o, scalar=Fq[:, i, h:h + 1], in1=fkb[:, h % 2, 0:n],
                                                     op0=ALU.add, op1=ALU.subtract))
                    elif t["mask"] == "dsa":
                        if i >= 1:
                            ve.wait_ge(ix_done, 4 - i)
                        link(ve.tensor_tensor(sp_, o, sel[:, i, 0:n], ALU.add))
                    ve.tensor_reduce(stat[:, s % 8, 0:1], sp_ if ph == "fd" else o, AX, ALU.max,
                                     negate=True).then_inc(at_max[ph], 1)

                def reciprocals(s):
                    t = steps[s]
                    q = stat[:, s % 8, 2:3]
                    ve.wait_ge(at_exp[ph], s + 1)
                    ins = ve.reciprocal(q, stat[:, s % 8, 1:2])
                    if ph == "fd":
                        ins.then_inc(at_rcp[ph], 1)
                        return
                    link(ins)
                    if t["av"] is not None and t["i"] == 0:
                        link(ve.tensor_tensor(q, q, t["av"], ALU.mult))
                    if s >= 2:
                        ve.wait_ge(at_tr[ph], s - 1)
                    ve.tensor_scalar(diag[:, s % 2, :], ident, q, t["gate"], ALU.mult, ALU.mult).then_inc(at_nrm[ph], 1)

                def outputs(c):
                    if ph == "nsa" and c == 0:
                        ve.wait_ge(rt_done, 4)
                    ve.wait_ge(at_hi[ph], c + 1)
                    ve.tensor_tensor(olo[c], ps[:, 5 + c % 2, :], ohi[c].bitcast(F32), ALU.subtract)\
                      .then_inc(at_done[ph], 1)

                def modulation_product(u):
                    b, k = u // KD, u % KD
                    ve.wait_ge(ada_landed[u % ADA_SLOTS], 16 * (u // ADA_SLOTS) + 16)
                    if k == 0 and b >= 2:
                        ve.wait_ge(mod_summed, b - 1)
                    w = ada_slot(u)
                    ve.tensor_scalar(modsum(b) if k == 0 else w, w, vec[:, V_C + k:V_C + k + 1], None, ALU.mult)\
                      .then_inc(mod_prod, 1)

                unit = 0
                if ph == "nsa":
                    ve.wait_ge(cond_ready, 1)
                    ve.wait_ge(rt_pv, 16)
                selecting = select_ops() if ph == "fd" else []
                done = 0
                for r in range(ROUNDS[ph] + 3):
                    if 0 <= r - LAG["max"] < len(steps):
                        maxima(r - LAG["max"])
                    lag = LAG["diag"] if ph == "nsa" else LAG["rcp"]
                    if 0 <= r - lag < len(steps):
                        reciprocals(r - lag)
                    for c in range(N_CH[ph]):
                        if r == CHUNK_END[ph][c] + LAG["out_lo"]:
                            outputs(c)
                    if ph == "fd" and r - 2 in UNIT_AT:
                        index_sums(UNIT_AT[r - 2])
                    while ph == "nsa" and unit < 72 and 4 * unit <= 3 * r:
                        modulation_product(unit)
                        unit += 1
                    for tile, (start, end) in enumerate(SELECT_AT if ph == "fd" else []):
                        while start <= r and done < N_SELECT * (tile + min(1, (r - start + 1) / (end - start))):
                            if done >= N_SELECT * (tile + 1):
                                break
                            selecting[done]()
                            done += 1
                assert done == len(selecting)

            def forget():
                z, e, mn = score[0:8, 0, :], score[0:8, 1, :], sel[0:8, 3, :]
                ve.wait_ge(f_z, 1)
                ve.scalar_tensor_tensor(out=e, in0=z, scalar=-1.0, in1=z, op0=ALU.mult, op1=ALU.max).then_inc(f_e, 1)
                ve.tensor_scalar(mn, z, 0.0, None, ALU.min)
                ve.wait_ge(f_l, 1)
                ve.tensor_scalar(e, e, 1.0, None, ALU.add).then_inc(f_e, 1)
                ve.wait_ge(f_l, 2)
                ve.tensor_tensor_scan(FT[:, :], mn, e, 0.0, ALU.add, ALU.subtract).then_inc(f_scan, 1)

            def index_prepare():
                link(ve.tensor_copy(sel[:, 0, 0:P], cst[:, C_ADM:C_ADM + P]))
                link(ve.tensor_scalar(rowS[:, :, 40:48], rowS[:, :, 40:48], 8 ** -0.5, None, ALU.mult))

            def score_of(i):
                return sel[:, 0, P:3 * P] if i == 1 else score[:, i % 2, 0:(i + 1) * P]

            def index_sums(u):
                i, heads = UNITS[u]
                n = (i + 1) * P
                w = score_of(i)
                ve.wait_ge(ix_relu, u + 1)
                for a, h in enumerate(heads):
                    r, iw = tmp[:, 2 + u % 2, a * n:a * n + n], rowS[:, i, 40 + h:41 + h]
                    if h == 0:
                        ins = ve.tensor_scalar(w, r, iw, None, ALU.mult)
                    else:
                        ve.wait_ge(ix_acc, SUMS[u] + a)
                        ins = ve.scalar_tensor_tensor(out=w, in0=r, scalar=iw, in1=w, op0=ALU.mult, op1=ALU.add)
                    ins.then_inc(ix_acc, 1)

            def select_ops():
                ops = []
                for n_done, i in enumerate((3, 2, 1)):
                    w = score_of(i)
                    dg = w[:, i * P:(i + 1) * P]

                    def admissible(dg=dg, n_done=n_done):
                        ve.wait_ge(ix_acc, 8 * (n_done + 1))
                        link(ve.tensor_tensor(dg, dg, cst[:, C_ADM:C_ADM + P], ALU.add))

                    def largest(w=w):
                        link(ve.max(top8[:, :], w))

                    def take(w=w):
                        link(ve.match_replace(w, top8[:, :], w, TAKEN))

                    def mask(w=w, i=i):
                        ve.tensor_scalar(sel[:, i, 0:(i + 1) * P], w, (NEG + TAKEN) / 2, NEG, ALU.is_gt, ALU.mult)\
                          .then_inc(ix_done, 1)
                    ops += [admissible] + [largest, take] * (TOPK // 8) + [mask]
                return ops

            def mix(b):
                for n in range(4):
                    if n >= 1:
                        ve.wait_ge(mx_ready, 8 * b + 2 * n)
                    for br in range(2):
                        for c in range(2):
                            x = 16 * b + 4 * n + 2 * br + c
                            ve.wait_ge(mx_sig, x + 1)
                            ve.wait_ge(*branch_done(b, n, br, c))
                            ve.tensor_tensor(tmp[:, 2 * br + c, :], ps[:, 4 * br + 2 + c, :], st[:, 2 * br + c, :], ALU.mult)\
                              .then_inc(mx_m, 1)
                    for c in range(2):
                        ve.wait_ge(mx_m, 16 * b + 4 * n + 2 + c + 1)
                        ve.tensor_tensor(tmp[:, c, :], tmp[:, c, :], tmp[:, 2 + c, :], ALU.add).then_inc(mx_t, 1)
                    for c in range(2):
                        ve.wait_ge(mx_hi, 8 * b + 2 * n + c + 1)
                        ve.tensor_tensor(mixlo[:, 2 * n + c, :], tmp[:, c, :], mixhi[:, 2 * n + c, :].bitcast(F32),
                                         ALU.subtract).then_inc(mx_ready, 1)

            def down(name, scale=None):
                for m in range(KD):
                    ve.wait_ge(*DOWN_DONE[name, m])
                    if scale is None:
                        ve.tensor_tensor(xT[:, m, :], xT[:, m, :], ps[:, m, :], ALU.add).then_inc(x_ready, 1)
                    else:
                        ve.scalar_tensor_tensor(out=xT[:, m, :], in0=ps[:, m, :], scalar=scale[:, m:m + 1], in1=xT[:, m, :],
                                                op0=ALU.mult, op1=ALU.add).then_inc(x_ready, 1)

            def up(h):
                def chunks(i):
                    for c in range(4):
                        at = i * 4 + (16 * h + c + 1)
                        ve.wait_ge(up_relu, at)
                        if not isinstance(i, int):
                            ve.wait_ge(up_ready, i * 4 + (16 * h + c - 3))
                        ve.tensor_tensor(tmp[:, c, :], st[:, c, :], st[:, c, :], ALU.mult).then_inc(up_t, 1)
                        ve.wait_ge(up_hi, at)
                        pick = lambda t: t[:, c, :] if isinstance(i, int) else t[:, bass.ds(i * 4 + c, 1), :].rearrange(
                            "p k n -> p (k n)")
                        ve.tensor_tensor(pick(hidlo), tmp[:, c, :], pick(hidhi).bitcast(F32), ALU.subtract)\
                          .then_inc(up_ready, 1)
                chunks(0)
                with ve.Fori(1, 4) as i:
                    chunks(i)

            def ffn_up(f, h):
                u0 = 22 * f + 12 * h

                def chunks(i):
                    at = lambda c: i * 2 + (u0 + c + 1)
                    for c in range(2):
                        ve.wait_ge(ff_sig, at(c))
                        ve.tensor_tensor(tmp[:, c, :], ps[:, c, :], st[:, c, :], ALU.mult).then_inc(ff_m1, 1)
                    for c in range(2):
                        if c == 0:
                            ve.wait_ge(ff_u, i + (11 * f + 6 * h + 1))
                        else:
                            ve.wait_ge(w_used, i * 4 + (AT[f"f{f + 1}up{h}"] + 4))
                        ve.wait_ge(ff_m1, at(c))
                        if not isinstance(i, int):
                            ve.wait_ge(ff_ready, i * 2 + (u0 + c - 1))
                        ve.tensor_tensor(tmp[:, 2 + c, :], ps[:, 2 + c, :], tmp[:, c, :], ALU.mult).then_inc(ff_m2, 1)
                    for c in range(2):
                        ve.wait_ge(ff_hi, at(c))
                        pick = lambda t: t[:, c, :] if isinstance(i, int) else t[:, bass.ds(i * 2 + c, 1), :].rearrange(
                            "p k n -> p (k n)")
                        ve.tensor_tensor(pick(hidlo), tmp[:, 2 + c, :], pick(hidhi).bitcast(F32), ALU.subtract)\
                          .then_inc(ff_ready, 1)
                chunks(0)
                with ve.Fori(1, 6 - h) as i:
                    chunks(i)

            def ffn(f, scale):
                for h in range(2):
                    ffn_up(f, h)
                    down(f"f{f + 1}down{h}", scale)

            def split_small(b):
                ve.wait_ge(ld_wsm, 16 if b == 0 else 48)
                n = 24 if b == 0 else 48
                ve.tensor_copy(wsmhi[:, :, 0:n], wsm[:, :, 0:n]).then_inc(wsm_hi, 1)
                ve.wait_ge(wsm_hi, b + 1)
                ve.tensor_tensor(wsmlo[:, :, 0:n], wsm[:, :, 0:n], wsmhi[:, :, 0:n].bitcast(F32), ALU.subtract)\
                  .then_inc(wsm_ready, 1)

            for m in range(KD):
                ve.wait_ge(x_turned, m + 1)
                ve.tensor_copy(xT[:, m, :], ps[:, m, :]).then_inc(x_ready, 1)
            ve.wait_ge(vec_ready, 2)
            for c in (V2_FQ, V2_DQ):
                link(ve.tensor_scalar(vec2[:, c:c + 1], vec2[:, c:c + 1], 0.125, None, ALU.mult))
            norm(0)
            ve.wait_ge(cond_sig, 1)
            ve.tensor_tensor(vec[:, V_C:V_C + 8], vec[:, V_C:V_C + 8], geff[:, 0:8], ALU.mult).then_inc(cond_ready, 1)
            trig_tables(0)
            split_small(0)
            projection("nsa", 0)
            compress_blocks(0)
            projection("rq", 0)
            compress_hidden(0)
            compress_blocks(1)
            projection("rk", 0)
            compress_hidden(1)
            projection("rvg", 0)
            compress_out()
            retention()
            attention("nsa")
            ve.wait_ge(mod_summed, 9)
            link(ve.tensor_tensor(mod[:, :], ps[:, 7, 0:72], vec[:, V_ADAB:V_ADAB + 72], ALU.add))
            for j in range(3):
                link(ve.scalar_tensor_tensor(out=geff[:, 8 * j:8 * j + 8], in0=mod[:, 24 * j + 8:24 * j + 16], scalar=1.0,
                                             in1=vec[:, V_G2 + 8 * j:V_G2 + 8 * j + 8], op0=ALU.add, op1=ALU.mult))
                if j != 1:
                    link(ve.tensor_scalar(mod[:, 24 * j + 16:24 * j + 24], mod[:, 24 * j + 16:24 * j + 24], 0.5, None,
                                          ALU.mult))
            ve.tensor_copy(stat[:, 0, 3:4], mod[:, 0:1]).then_inc(mod_ready, 1)
            mix(0)
            down("out1")
            norm(1)
            up(0)
            trig_tables(1)
            split_small(1)
            down("down0")
            up(1)
            down("down1")
            norm(2)
            norm(3)
            ffn(0, mod[:, 16:24])
            norm(4)
            projection("fox", 4)
            projection("dsa", 4, {1: forget})
            index_prepare()
            attention("fd")
            mix(1)
            down("out2", mod[:, 40:48])
            norm(5)
            ffn(1, mod[:, 64:72])



def constants():
    c = np.zeros((P, C_END), np.float32)
    r = np.arange(P)
    c[:, C_ID:C_ID + P] = np.eye(P)
    c[:, C_MEAN:C_MEAN + P] = 1.0 / D
    c[:, C_HD128:C_HD128 + P] = 1.0 / 128
    c[:, C_HD64:C_HD64 + P] = (r[:, None] // 64 == r[None, :] // 64) / 64.0
    for at, width, rot in ((C_PN, 64, 16), (C_PR, 128, 128), (C_PI, 32, 8)):
        half = rot // 2
        for m in range(P):
            d = m % width
            if d < half:
                c[m + half, at + m] = -1.0
            elif d < rot:
                c[m - half, at + m] = 1.0
    c[:, C_CAUSAL:C_CAUSAL + P] = np.where(r[None, :] <= r[:, None], 0.0, NEG)
    c[:, C_ADM:C_ADM + P] = np.where(r[None, :] // 64 <= r[:, None] // 64, 0.0, NEG)
    for i in range(NT):
        t = i * P + r
        end = 16 * np.arange(N_CMP) + 31
        c[:, C_CMP + 32 * i:C_CMP + 32 * i + N_CMP] = np.where(end[None, :] <= t[:, None], 0.0, NEG)
        c[:, C_AV + i] = t >= 31
    f32 = np.float32

    def inverse(base, rot):
        return np.exp(f32(-math.log(base)) * np.arange(rot // 2, dtype=f32) * f32(2.0) / f32(rot))

    def inverse2(rot):
        return (500000.0 ** (-np.arange(0, rot, 2, dtype=f32) / f32(rot)).astype(np.float64)).astype(f32)

    for n, (inv, width) in enumerate(((inverse(500000.0, 16), 64), (inverse(10000.0, 128), 128), (inverse2(16), 64),
                                      (inverse2(8), 32))):
        half = len(inv)
        for m in range(P):
            d = m % width
            c[m, C_INV + n] = inv[d % half] if d < 2 * half else 0.0
    c[:, C_EPS] = EPS
    return c


def decay_table():
    g = 1.0 - 2.0 ** (-5.0 - np.arange(4))
    rel = np.arange(S)[None, :] - np.arange(P)[:, None]
    t = np.where(rel[:, None, :] >= 0, g[None, :, None] ** np.maximum(rel, 0)[:, None, :], 0.0)
    return np.ascontiguousarray(t.reshape(P, 4 * S).astype(np.float32))


_NAMES = ["x", "positions", "norm_mix", "w_in", "cmp_pos_k", "cmp_pos_v", "cmp_k_w1", "cmp_k_w2", "cmp_v_w1", "cmp_v_w2",
          "w_proj_a", "w_proj_b", "w_out", "norm_mlp", "w_up", "w_down", "norm_final", "c_2", "positions_2", "ada_w_2",
          "ada_b_2", "norm_g_2", "ffn1_w1_2", "ffn1_w3_2", "ffn1_w2_2", "w_in_2", "fox_f_bias_2", "fox_qk_g_2",
          "dsa_qk_g_2", "w_br_fox_2", "w_br_dsa_2", "w_out_2", "ffn2_w1_2", "ffn2_w3_2", "ffn2_w2_2"]


def kernel(**inputs):
    import concourse.bacc as bacc
    from concourse.bass_utils import run_bass_kernel_spmd

    nc = bacc.Bacc("TRN2", target_bir_lowering=False, num_devices=1)
    arrays = {name: np.ascontiguousarray(inputs[name]) for name in _NAMES}
    arrays["consts"] = constants()
    arrays["decay"] = decay_table()
    tensors = {name: nc.dram_tensor(f"in_{name}", a.shape, mybir.dt.from_np(a.dtype), kind="ExternalInput").ap()
               for name, a in arrays.items()}
    out = nc.dram_tensor("out_y", (1, S, D), F32, kind="ExternalOutput").ap()
    mix_kernel(nc, tensors, out)
    r = run_bass_kernel_spmd(nc, [{f"in_{name}": a for name, a in arrays.items()}], core_ids=[0])
    return r.results[0]["out_y"]
```
